# Optimizing a Trainium2 kernel written in Bass

```python
import math
import jax
import jax.numpy as jnp
from jax import lax
import numpy as np

D_MODEL = 2048
BATCH = 1
SEQ = 256
DEPTH = 2
DEC_BATCH = 8
DEC_SEQ = 4
PAST_LEN = 2048
PAGE_SIZE = 128

N_MIXERS = 2
N_S5_LAYERS = (DEPTH + N_MIXERS - 1) // N_MIXERS
N_LRU_LAYERS = DEPTH // N_MIXERS
S5_GROUP = 16
S5_GROUPS = D_MODEL // S5_GROUP
S5_STATE = 64
S5_DT_MIN = 1e-3
S5_DT_MAX = 1e-1
D_RNN = D_MODEL
LRU_HEADS = 8
LRU_BLOCK = D_RNN // LRU_HEADS
CONV_WIDTH = 4
LRU_C = 8.0
LRU_MIN_RAD = 0.9
LRU_MAX_RAD = 0.999
PEER_HEADS = 8
N_KEYS = 128
N_EXPERTS = N_KEYS * N_KEYS
D_KEY = 256
D_HALF = D_KEY // 2
TOPK = 16
PEER_TOKEN_BLOCK = 128
RMS_EPS = 1e-6

kernel_name = "s5_rglru_peer_hybrid_step"

def rmsnorm(x, g):
    xf = x.astype(jnp.float32)
    y = xf * lax.rsqrt(jnp.mean(xf * xf, axis=-1, keepdims=True) + RMS_EPS)
    return (y * g.astype(jnp.float32)).astype(x.dtype)

def cmul(ar, ai, br, bi):
    return ar * br - ai * bi, ar * bi + ai * br

def s5_discretize(lam_re, lam_im, log_dt, b_re, b_im):
    dt = jnp.exp(log_dt.astype(jnp.float32))[:, None]
    lr = lam_re.astype(jnp.float32)
    li = lam_im.astype(jnp.float32)
    mag = jnp.exp(lr * dt)
    ab_re = mag * jnp.cos(li * dt)
    ab_im = mag * jnp.sin(li * dt)
    nr, ni = ab_re - 1.0, ab_im
    den = lr * lr + li * li
    f_re = (nr * lr + ni * li) / den
    f_im = (ni * lr - nr * li) / den
    br = b_re.astype(jnp.float32)
    bi = b_im.astype(jnp.float32)
    bb_re = f_re[..., None] * br - f_im[..., None] * bi
    bb_im = f_re[..., None] * bi + f_im[..., None] * br
    return ab_re, ab_im, bb_re, bb_im

def _s5_combine(left, right):
    a1r, a1i, b1r, b1i = left
    a2r, a2i, b2r, b2i = right
    ar, ai = cmul(a2r, a2i, a1r, a1i)
    br, bi = cmul(a2r, a2i, b1r, b1i)
    return ar, ai, br + b2r, bi + b2i

def s5_mixer(h, h0_re, h0_im, lam_re, lam_im, log_dt, b_re, b_im, c_re, c_im, d_skip, w_glu, b_glu):
    bsz, t = h.shape[0], h.shape[1]
    hf = h.astype(jnp.float32)
    u = hf.reshape(bsz, t, S5_GROUPS, S5_GROUP)
    ab_re, ab_im, bb_re, bb_im = s5_discretize(lam_re, lam_im, log_dt, b_re, b_im)
    bu_re = jnp.einsum("btgc,gpc->btgp", u, bb_re)
    bu_im = jnp.einsum("btgc,gpc->btgp", u, bb_im)
    if h0_re is not None:
        c0_re, c0_im = cmul(ab_re, ab_im, h0_re.astype(jnp.float32), h0_im.astype(jnp.float32))
        bu_re = bu_re.at[:, 0].add(c0_re)
        bu_im = bu_im.at[:, 0].add(c0_im)
    a_re = jnp.broadcast_to(ab_re, (1, t) + ab_re.shape)
    a_im = jnp.broadcast_to(ab_im, (1, t) + ab_im.shape)
    _, _, s_re, s_im = lax.associative_scan(_s5_combine, (a_re, a_im, bu_re, bu_im), axis=1)
    y = (jnp.einsum("btgp,gcp->btgc", s_re, c_re.astype(jnp.float32))
         - jnp.einsum("btgp,gcp->btgc", s_im, c_im.astype(jnp.float32)))
    y = y.reshape(bsz, t, D_MODEL) + d_skip.astype(jnp.float32) * hf
    y = jax.nn.gelu(y, approximate=False)
    out = y * jax.nn.sigmoid(y @ w_glu.astype(jnp.float32) + b_glu.astype(jnp.float32))
    return out.astype(h.dtype), s_re[:, -1], s_im[:, -1]

def causal_conv(xb, buf, w, b):
    bsz, t, c = xb.shape
    if buf is None:
        buf = jnp.zeros((bsz, CONV_WIDTH - 1, c), xb.dtype)
    xp = jnp.concatenate([buf.astype(jnp.float32), xb.astype(jnp.float32)], axis=1)
    wf = w.astype(jnp.float32)
    y = b.astype(jnp.float32) + sum(xp[:, k:k + t] * wf[k] for k in range(CONV_WIDTH))
    return y, xp[:, -(CONV_WIDTH - 1):]

def _lin_combine(left, right):
    a1, b1 = left
    a2, b2 = right
    return a1 * a2, a2 * b1 + b2

def rglru(x, h0, w_a, b_a, w_i, b_i, lam):
    bsz, t, _ = x.shape
    xh = x.reshape(bsz, t, LRU_HEADS, LRU_BLOCK)
    r = jax.nn.sigmoid(jnp.einsum("bthi,hij->bthj", xh, w_a.astype(jnp.float32)) + b_a.astype(jnp.float32))
    ig = jax.nn.sigmoid(jnp.einsum("bthi,hij->bthj", xh, w_i.astype(jnp.float32)) + b_i.astype(jnp.float32))
    r = r.reshape(bsz, t, D_RNN)
    ig = ig.reshape(bsz, t, D_RNN)
    log_a = -LRU_C * r * jax.nn.softplus(-lam.astype(jnp.float32))
    a = jnp.exp(log_a)
    bx = jnp.sqrt(-jnp.expm1(2.0 * log_a)) * (ig * x)
    if h0 is not None:
        bx = bx.at[:, 0].add(a[:, 0] * h0.astype(jnp.float32))
    _, hs = lax.associative_scan(_lin_combine, (a, bx), axis=1)
    return hs, hs[:, -1]

def lru_mixer(h, conv_buf, h0, w_in, conv_w, conv_b, w_a, b_a, w_i, b_i, lam, w_out):
    z = h @ w_in
    gate, xb = z[..., :D_RNN], z[..., D_RNN:]
    xc, new_buf = causal_conv(xb, conv_buf, conv_w, conv_b)
    hs, h_last = rglru(xc, h0, w_a, b_a, w_i, b_i, lam)
    y = (hs * jax.nn.gelu(gate.astype(jnp.float32), approximate=False)) @ w_out.astype(jnp.float32)
    return y.astype(h.dtype), h_last, new_buf

def peer_retrieve(hf, w_q, sub_keys):
    n = hf.shape[0]
    q = (hf @ w_q).astype(jnp.float32).reshape(n, PEER_HEADS, 2, D_HALF)
    s = jnp.einsum("nhsk,hsmk->nhsm", q, sub_keys.astype(jnp.float32))
    top_s, top_i = lax.top_k(s, TOPK)
    cand_s = (top_s[:, :, 0, :, None] + top_s[:, :, 1, None, :]).reshape(n, PEER_HEADS, TOPK * TOPK)
    cand_i = (top_i[:, :, 0, :, None] * N_KEYS + top_i[:, :, 1, None, :]).reshape(n, PEER_HEADS, TOPK * TOPK)
    best_s, pos = lax.top_k(cand_s, TOPK)
    idx = jnp.take_along_axis(cand_i, pos, axis=-1)
    g = jax.nn.softmax(best_s, axis=-1)
    return idx, g

def peer_ffn(h, w_q, sub_keys, u_emb, v_emb):
    bsz, t, d = h.shape
    n = bsz * t
    hf = h.reshape(n, d)
    idx, g = peer_retrieve(hf, w_q, sub_keys)
    blk = min(PEER_TOKEN_BLOCK, n)
    n_pad = -(-n // blk) * blk
    pad = n_pad - n
    hp = jnp.pad(hf, ((0, pad), (0, 0))).reshape(-1, blk, d)
    ip = jnp.pad(idx, ((0, pad), (0, 0), (0, 0))).reshape(-1, blk, PEER_HEADS, TOPK)
    gp = jnp.pad(g, ((0, pad), (0, 0), (0, 0))).reshape(-1, blk, PEER_HEADS, TOPK)

    def block(args):
        xb, ib, gb = args
        u = u_emb[ib].astype(jnp.float32)
        act = jnp.einsum("nd,nhkd->nhk", xb.astype(jnp.float32), u)
        wgt = jax.nn.gelu(act, approximate=False) * gb
        v = v_emb[ib].astype(jnp.float32)
        return jnp.einsum("nhk,nhkd->nd", wgt, v)

    out = lax.map(block, (hp, ip, gp))
    return out.reshape(n_pad, d)[:n].reshape(bsz, t, d).astype(h.dtype)

def setup_inputs(seed: int = 0) -> dict:
    key = jax.random.key(seed)
    ks = iter(jax.random.split(key, 48))
    f32 = jnp.float32

    def nrm(shape, scale):
        return scale * jax.random.normal(next(ks), shape, f32)

    n_idx = jnp.arange(S5_STATE, dtype=f32)
    s5_shape = (N_S5_LAYERS, S5_GROUPS, S5_STATE)
    u_r = jax.random.uniform(next(ks), (N_LRU_LAYERS, D_RNN), f32, LRU_MIN_RAD ** 2, LRU_MAX_RAD ** 2)
    return {
        "x_prompt": nrm((BATCH, SEQ, D_MODEL), 1.0),
        "x_sample": nrm((DEC_BATCH, DEC_SEQ, D_MODEL), 1.0),
        "state_s5_re": nrm((N_S5_LAYERS, DEC_BATCH, S5_GROUPS, S5_STATE), 0.1),
        "state_s5_im": nrm((N_S5_LAYERS, DEC_BATCH, S5_GROUPS, S5_STATE), 0.1),
        "state_lru_h": nrm((N_LRU_LAYERS, DEC_BATCH, D_RNN), 0.5),
        "state_lru_conv": nrm((N_LRU_LAYERS, DEC_BATCH, CONV_WIDTH - 1, D_RNN), 1.0),
        "norm_mix": 1.0 + nrm((DEPTH, D_MODEL), 0.02),
        "norm_ffn": 1.0 + nrm((DEPTH, D_MODEL), 0.02),
        "norm_final": 1.0 + nrm((D_MODEL,), 0.02),
        "s5_lam_re": -0.5 + nrm(s5_shape, 0.01),
        "s5_lam_im": jnp.pi * n_idx + nrm(s5_shape, 0.01),
        "s5_log_dt": jax.random.uniform(next(ks), (N_S5_LAYERS, S5_GROUPS), f32,
                                        math.log(S5_DT_MIN), math.log(S5_DT_MAX)),
        "s5_b_re": nrm((N_S5_LAYERS, S5_GROUPS, S5_STATE, S5_GROUP), (2 * S5_GROUP) ** -0.5),
        "s5_b_im": nrm((N_S5_LAYERS, S5_GROUPS, S5_STATE, S5_GROUP), (2 * S5_GROUP) ** -0.5),
        "s5_c_re": nrm((N_S5_LAYERS, S5_GROUPS, S5_GROUP, S5_STATE), S5_STATE ** -0.5),
        "s5_c_im": nrm((N_S5_LAYERS, S5_GROUPS, S5_GROUP, S5_STATE), S5_STATE ** -0.5),
        "s5_d": 1.0 + nrm((N_S5_LAYERS, D_MODEL), 0.1),
        "s5_w_glu": nrm((N_S5_LAYERS, D_MODEL, D_MODEL), D_MODEL ** -0.5),
        "s5_b_glu": nrm((N_S5_LAYERS, D_MODEL), 0.01),
        "lru_w_in": nrm((N_LRU_LAYERS, D_MODEL, 2 * D_RNN), D_MODEL ** -0.5),
        "lru_conv_w": nrm((N_LRU_LAYERS, CONV_WIDTH, D_RNN), CONV_WIDTH ** -0.5),
        "lru_conv_b": nrm((N_LRU_LAYERS, D_RNN), 0.01),
        "lru_w_a": nrm((N_LRU_LAYERS, LRU_HEADS, LRU_BLOCK, LRU_BLOCK), LRU_BLOCK ** -0.5),
        "lru_b_a": nrm((N_LRU_LAYERS, LRU_HEADS, LRU_BLOCK), 0.01),
        "lru_w_i": nrm((N_LRU_LAYERS, LRU_HEADS, LRU_BLOCK, LRU_BLOCK), LRU_BLOCK ** -0.5),
        "lru_b_i": nrm((N_LRU_LAYERS, LRU_HEADS, LRU_BLOCK), 0.01),
        "lru_lam": -jnp.log(u_r ** -0.5 - 1.0),
        "lru_w_out": nrm((N_LRU_LAYERS, D_RNN, D_MODEL), D_RNN ** -0.5),
        "peer_w_q": nrm((DEPTH, D_MODEL, PEER_HEADS * D_KEY), D_MODEL ** -0.5),
        "peer_sub_keys": nrm((DEPTH, PEER_HEADS, 2, N_KEYS, D_HALF), D_HALF ** -0.5),
        "peer_u": nrm((DEPTH, N_EXPERTS, D_MODEL), D_MODEL ** -0.5),
        "peer_v": nrm((DEPTH, N_EXPERTS, D_MODEL), PEER_HEADS ** -0.5),
    }

def reference(x_prompt, x_sample, state_s5_re, state_s5_im, state_lru_h, state_lru_conv,
              norm_mix, norm_ffn, norm_final,
              s5_lam_re, s5_lam_im, s5_log_dt, s5_b_re, s5_b_im, s5_c_re, s5_c_im, s5_d, s5_w_glu, s5_b_glu,
              lru_w_in, lru_conv_w, lru_conv_b, lru_w_a, lru_b_a, lru_w_i, lru_b_i, lru_lam, lru_w_out,
              peer_w_q, peer_sub_keys, peer_u, peer_v):
    yp, ys = x_prompt, x_sample
    s5_rp, s5_ip, s5_rs, s5_is = [], [], [], []
    lru_hp, lru_cp, lru_hs, lru_cs = [], [], [], []
    for i in range(DEPTH):
        j = i // N_MIXERS
        hp = rmsnorm(yp, norm_mix[i])
        hs = rmsnorm(ys, norm_mix[i])
        if i % N_MIXERS == 0:
            prm = (s5_lam_re[j], s5_lam_im[j], s5_log_dt[j], s5_b_re[j], s5_b_im[j],
                   s5_c_re[j], s5_c_im[j], s5_d[j], s5_w_glu[j], s5_b_glu[j])
            op, rp, ip_ = s5_mixer(hp, None, None, *prm)
            os_, rs, is_ = s5_mixer(hs, state_s5_re[j], state_s5_im[j], *prm)
            s5_rp.append(rp)
            s5_ip.append(ip_)
            s5_rs.append(rs)
            s5_is.append(is_)
        else:
            prm = (lru_w_in[j], lru_conv_w[j], lru_conv_b[j], lru_w_a[j], lru_b_a[j],
                   lru_w_i[j], lru_b_i[j], lru_lam[j], lru_w_out[j])
            op, hlp, cbp = lru_mixer(hp, None, None, *prm)
            os_, hls, cbs = lru_mixer(hs, state_lru_conv[j], state_lru_h[j], *prm)
            lru_hp.append(hlp)
            lru_cp.append(cbp)
            lru_hs.append(hls)
            lru_cs.append(cbs)
        yp = yp + op
        ys = ys + os_
        yp = yp + peer_ffn(rmsnorm(yp, norm_ffn[i]), peer_w_q[i], peer_sub_keys[i], peer_u[i], peer_v[i])
        ys = ys + peer_ffn(rmsnorm(ys, norm_ffn[i]), peer_w_q[i], peer_sub_keys[i], peer_u[i], peer_v[i])
    y_prompt = rmsnorm(yp, norm_final)
    y_sample = rmsnorm(ys, norm_final)
    return (y_prompt, y_sample,
            jnp.stack(s5_rp), jnp.stack(s5_ip), jnp.stack(s5_rs), jnp.stack(s5_is),
            jnp.stack(lru_hp), jnp.stack(lru_cp), jnp.stack(lru_hs), jnp.stack(lru_cs))


_drawn_inputs = setup_inputs


def setup_inputs(seed=0):
    import zlib

    import numpy as np

    out = dict(_drawn_inputs(seed))
    spreads = {}
    factors = {'norm_final': 7.717,
     's5_lam_re': 16.862,
     's5_b_glu': 5.424,
     'lru_b_a': 26.35,
     'lru_b_i': 8.0}
    for name, (base, spread) in spreads.items():
        noise = np.random.default_rng([zlib.crc32(name.encode()), seed]).standard_normal(out[name].shape)
        drawn = base * np.exp(spread * noise) if base else spread * noise
        out[name] = jnp.asarray(drawn.astype(out[name].dtype))
    for name, factor in factors.items():
        out[name] = (out[name] * factor).astype(out[name].dtype)
    return out
```

```python
from contextlib import ExitStack

import concourse.bass as bass
from concourse import mybir

F32 = mybir.dt.float32
I32 = mybir.dt.int32
U32 = mybir.dt.uint32
ALU = mybir.AluOpType
ACT = mybir.ActivationFunctionType
AX_X = mybir.AxisListType.X

P = 128
D = 2048
KT = D // P
SEQ = 256
SB, ST = 8, 4
NS = SB * ST
NT = SEQ + NS
TILES = 3
COPIES = P // NS
BANK = 512
GROUP = 4
PI = 3.14159265358979
TWO_PI_LOW = 6.283185
ROUND = 12582912.0
EPS = 1e-6
LOWEST = -3.0e38

S5_Q = 64
QK = 4
QC = 32

SLAB_GLU, SLAB_Q0, SLAB_KEY0, SLAB_IN = 0, 16, 32, 33
SLAB_GATE, SLAB_OUT, SLAB_Q1, SLAB_KEY1, SLABS = 65, 69, 85, 101, 102
WRING = 4

HEADS, TOPK, NKEYS = 8, 16, 128
LISTS = 2 * HEADS
PICKS = HEADS * TOPK
RING = 8
COLS = 2 * PICKS + PICKS // COPIES
ROUNDS_OF = [PICKS // RING, PICKS // RING, PICKS // COPIES // RING]
ROUND_AT = [0, PICKS // RING, 2 * PICKS // RING]
ROUNDS = COLS // RING

V_D, V_BGLU, V_CW, V_CB, V_BA, V_BI, V_LAM, V_N = 0, 1, 2, 6, 7, 8, 9, 10


def token_cols(t):
    return slice(t * P, (t + 1) * P) if t < 2 else slice(SEQ, NT)


class Steps:

    def __init__(self):
        self.base, self.i, self.per, self.n = 0, 0, 0, 0

    def enter(self, i, per):
        self.base, self.i, self.per, self.n = self.base + self.n, i, per, 0

    def leave(self, rounds):
        assert self.n == self.per, (self.n, self.per)
        self.base, self.i, self.per, self.n = self.base + rounds * self.per, 0, 0, 0

    def next(self):
        self.n += 1
        return self.i * self.per + (self.base + self.n)


def hybrid_step(nc, x, norms, slabs, chan, s5_vec, s5_bc, s5_h0, lru_in, u0, v0, u1, v1,
                y_out, ys_out, s5p_out, s5s_out, lru_out):
    experts_u, experts_v = [u0, u1], [v0, v1]
    with ExitStack() as ctx:
        def sb(name, shape, dt=F32):
            return ctx.enter_context(nc.sbuf_tensor(name, shape, dt))

        def sem(name):
            return ctx.enter_context(nc.semaphore(name))

        X = sb("X", [P, TILES, D])
        HN = sb("HN", [P, TILES, D])
        HT = sb("HT", [P, KT, NT])
        W = sb("W", [P, WRING, D])
        GB = sb("GB", [P, 2, D])
        CH = sb("CH", [P, V_N, KT])
        arena = sb("arena", [P, 22528])
        ident = sb("ident", [P, P])
        repsum = sb("repsum", [P, P])
        iota = sb("iota", [P, SEQ])
        cst = sb("cst", [P, 2])
        ixs = sb("ixs", [P, RING], I32)
        nrm = sb("nrm", [P, 12])
        ps = ctx.enter_context(nc.psum_tensor("ps", [P, 8, BANK], F32))
        hn_flat = HN[:].rearrange("p a b -> p (a b)")

        def view(at, n, base=None):
            return (arena if base is None else base)[:, at:at + n]

        YT = view(0, KT * NT).rearrange("p (k n) -> p k n", k=KT)
        SSO = view(4608, 1024).rearrange("p (c q b) -> p c q b", c=2, q=S5_Q)
        S0 = view(5632, 1024).rearrange("p (c q b) -> p c q b", c=2, q=S5_Q)
        par = [view(6656 + 68 * n, 68) for n in range(24)]
        BC = view(8320, 1024).rearrange("p (h c n) -> p h c n", h=2, c=4)
        BX = view(9344, 256).rearrange("p (c n) -> p c n", c=2)
        BT = view(9600, 256).rearrange("p (c n) -> p c n", c=2)
        CN = view(9856, 256).rearrange("p (h n) -> p h n", h=2)
        DD = view(10112, 256).rearrange("p (h n) -> p h n", h=2)
        BS = view(10368, 512).rearrange("p (h c q b t) -> p h c q b t", h=2, c=2, q=QK, b=SB)
        BSF = view(10368, 512).rearrange("p (h c n) -> p h c n", h=2, c=2)
        SF = view(10880, 128).rearrange("p (c q) -> p c q", c=2)
        PT = view(11008, 512).rearrange("p (n m) -> p n m", n=4)
        UX = view(11520, QK * NT).rearrange("p (q n) -> p q n", q=QK)
        PRD = view(12672, 1024).rearrange("p (q t) -> p q t", q=QK)
        COS = view(13696, 2048).rearrange("p (h q t) -> p h q t", h=2, q=QK)
        SIN = view(15744, 2048).rearrange("p (h q t) -> p h q t", h=2, q=QK)
        M = [view(17792 + 1024 * n, 1024).rearrange("p (q t) -> p q t", q=QK) for n in range(4)]
        PR = [hn_flat[:, 1024 * n:1024 * (n + 1)].rearrange("p (q t) -> p q t", q=QK) for n in range(4)]
        vecs = view(21888, 192)
        SIG = view(17792, 4 * NT).rearrange("p (n m) -> p n m", n=4)
        OT0 = hn_flat[:, 0:KT * NT].rearrange("p (k n) -> p k n", k=KT)
        REP0 = view(12672, D)
        GT = view(0, KT * NT).rearrange("p (k n) -> p k n", k=KT)
        XC = view(4608, KT * NT).rearrange("p (k n) -> p k n", k=KT)
        XBP = view(9216, KT * (SEQ + 3)).rearrange("p (k n) -> p k n", k=KT)
        XBS = view(9216 + KT * (SEQ + 3), KT * SB * 7).rearrange("p (k b n) -> p k b n", k=KT, b=SB)
        TH = view(9216, KT * NT).rearrange("p (k n) -> p k n", k=KT)
        RA = view(14256, KT * NT).rearrange("p (k n) -> p k n", k=KT)
        IG = hn_flat[:, 0:KT * NT].rearrange("p (k n) -> p k n", k=KT)
        LIN = view(18864, 512)
        LCONV = view(18864, 384).rearrange("p (k b n) -> p k b n", k=KT, b=SB)
        LH0 = view(18864 + 384, 128).rearrange("p (k b) -> p k b", k=KT)
        LOUT = view(19376, 576)
        LT = view(19952, 128).rearrange("p (k b) -> p k b", k=KT)
        LS = [view(20080 + 16 * n, 16) for n in range(8)]
        OT1 = XC
        REP1 = view(14256, D)
        QT = view(0, KT * NT).rearrange("p (k n) -> p k n", k=KT)
        REPQ = view(4608, D)
        SC = view(6656, D)
        SCW = view(8704, D)
        OH = view(10752, D)
        TV = view(12800, 256)
        TI = view(13056, 256).bitcast(U32)
        TF = view(13312, 256)
        BV = view(13568, 128)
        BP = view(13696, 128).bitcast(U32)
        AB = view(13824, 256).bitcast(U32)
        ABF = view(14080, 256)
        II = view(14336, 256)
        GE = view(14592, 128)
        GE2 = view(14720, 128)
        GS = view(14848, 16)
        ring = view(0, RING * D).rearrange("p (r d) -> p r d", r=RING)
        ACC = view(18432, D)
        GI = view(20480, 384).bitcast(I32)
        GG = view(20864, 384)
        AV = view(21248, 384)
        WG = view(21632, 384)
        A8 = view(22016, RING)

        x_in = sem("x_in")
        small_in = sem("small_in")
        s5_in = sem("s5_in")
        lru_in_sem = sem("lru_in_sem")
        gain_in = sem("gain_in")
        consts = sem("consts")
        slab_in = [sem(f"slab_in{r}") for r in range(WRING)]
        slab_done = sem("slab_done")
        bank_read = sem("bank_read")
        norm_sq, norm_v, norm_rt, norm_h = sem("norm_sq"), sem("norm_v"), sem("norm_rt"), sem("norm_h")
        norm_tp, norm_ht = sem("norm_tp"), sem("norm_ht")
        glu_out = sem("glu_out")
        mix_rep, mix_tp, mix_x = sem("mix_rep"), sem("mix_tp"), sem("mix_x")
        vstep, pstep, astep = sem("vstep"), sem("pstep"), sem("astep")
        s5_pa, s5_pv = sem("s5_pa"), sem("s5_pv")
        s5_bc_in = [sem("s5_bc_in0"), sem("s5_bc_in1")]
        s5_bx, s5_bt, s5_btc, s5_ux = sem("s5_bx"), sem("s5_bt"), sem("s5_btc"), sem("s5_ux")
        s5_cn, s5_dd, s5_bu, s5_bur = sem("s5_cn"), sem("s5_dd"), sem("s5_bu"), sem("s5_bur")
        s5_bsc, s5_bsd, s5_prod, s5_f = sem("s5_bsc"), sem("s5_bsd"), sem("s5_prod"), sem("s5_f")
        s5_tab, s5_p, s5_y, s5_yg = sem("s5_tab"), sem("s5_p"), sem("s5_y"), sem("s5_yg")
        s5_sf, s5_zero, stores = sem("s5_sf"), sem("s5_zero"), sem("stores")
        y_stored, top_go, pool_go = sem("y_stored"), sem("top_go"), sem("pool_go")
        lru_pad, lru_xb, lru_xc, lru_st = sem("lru_pad"), sem("lru_xb"), sem("lru_xc"), sem("lru_st")
        gate_mm, gate_ev, lru_sp, lru_a = sem("gate_mm"), sem("gate_ev"), sem("lru_sp"), sem("lru_a")
        lru_th, lru_v, lru_rt, lru_y = sem("lru_th"), sem("lru_v"), sem("lru_rt"), sem("lru_y")
        lru_hs = sem("lru_hs")
        key_rep, key_mm, key_sc, tile_top = sem("key_rep"), sem("key_mm"), sem("key_sc"), sem("tile_top")
        soft_in, soft_exp, picks_ready = sem("soft_in"), sem("soft_exp"), sem("picks_ready")
        row_in = [sem(f"row_in{r}") for r in range(RING)]
        row_used, index_set, gather_go = sem("row_used"), sem("index_set"), sem("gather_go")
        dots, act_g, peer_acc, peer_sum, peer_x = sem("dots"), sem("act_g"), sem("peer_acc"), sem("peer_sum"), sem("peer_x")

        block = ctx.enter_context(nc.Block())

        @block.sync
        def _(sp):
            for t in range(TILES):
                sp.dma_start(X[:, t, :], x[t]).then_inc(x_in, 16)
            for r in range(WRING):
                sp.dma_start(W[:, r, :], slabs[r]).then_inc(slab_in[r], 16)
            with sp.Fori(1, SLABS // WRING) as g:
                for r in range(WRING):
                    sp.wait_ge(slab_done, g * WRING + (r - WRING + 1))
                    sp.dma_start(W[:, r, :], slabs[bass.ds(g * WRING + r, 1)].rearrange("a p n -> p (a n)")).then_inc(slab_in[r], 16)
            for n in range(SLABS // WRING * WRING, SLABS):
                sp.wait_ge(slab_done, n - WRING + 1)
                sp.dma_start(W[:, n % WRING, :], slabs[n]).then_inc(slab_in[n % WRING], 16)
            for t in range(2):
                sp.wait_ge(norm_h, 12 + t + 1)
                sp.dma_start(y_out[t], HN[:, t, :]).then_inc(y_stored, 16)
            sp.wait_ge(norm_h, 15)
            sp.dma_start(ys_out, HN[0:NS, 2, :]).then_inc(y_stored, 16)
            sp.wait_ge(y_stored, 16 * 3)

        @block.gpsimd
        def _(pool):
            st = Steps()
            for n in range(2):
                pool.dma_start(GB[:, n, :], norms[n:n + 1, :].partition_broadcast(P)).then_inc(gain_in, 16)
            nc.gpsimd.memset(ident[:], 0.0).then_inc(pstep, 1)
            nc.gpsimd.memset(repsum[:], 0.0).then_inc(pstep, 1)
            nc.gpsimd.memset(cst[:], PI / 2).then_inc(pstep, 1)
            nc.gpsimd.iota(iota[:], [[1, SEQ]], base=0, channel_multiplier=0,
                           allow_small_or_imprecise_dtypes=True).then_inc(pstep, 1)
            for _ in range(3):
                st.next()
            pool.wait_ge(pstep, st.next())
            nc.gpsimd.affine_select(out=ident[:], in_=ident[:], compare_op=ALU.not_equal, fill=1.0, base=0,
                                    pattern=[[-1, P]], channel_multiplier=1).then_inc(consts, 1)
            for c in range(-COPIES + 1, COPIES):
                nc.gpsimd.affine_select(out=repsum[:], in_=repsum[:], compare_op=ALU.not_equal, fill=1.0,
                                        base=-NS * c, pattern=[[-1, P]], channel_multiplier=1).then_inc(pstep, 1)
                pool.wait_ge(pstep, st.next())
            pool.sem_inc(consts, 1)

            abr, abi, fr, fi = par[0], par[1], par[2], par[3]

            def s5_tile(i, h, first):
                k = 2 * i + h
                if not first:
                    pool.wait_ge(s5_y, k - 1)
                pool.dma_start(BC[:, h, :, :].rearrange("p c n -> p (c n)"),
                               s5_bc[bass.ds(k, 1)].rearrange("a p n -> p (a n)")).then_inc(s5_bc_in[h], 16)
                nc.gpsimd.tensor_tensor(DD[:, h, :], ident[:], CH[:, V_D, bass.ds(k, 1)].to_broadcast([P, P]),
                                        ALU.mult).then_inc(s5_dd, 1)
                pool.wait_ge(s5_bc_in[h], (i + 1) * 16)
                pool.sem_inc(pool_go, 1)
                b = [BC[:, h, c, :].rearrange("p (q n) -> p q n", q=QK) for c in range(2)]
                f = [w[:, bass.ds(k * QK, QK)].unsqueeze(2).to_broadcast([P, QK, QC]) for w in (fr, fi)]
                t = [PT[:, n, :].rearrange("p (q n) -> p q n", q=QK) for n in range(4)]
                for n, (c, e) in enumerate([(0, 0), (1, 1), (0, 1), (1, 0)]):
                    ins = nc.gpsimd.tensor_tensor(t[n], b[c], f[e], ALU.mult)
                ins.then_inc(pstep, 1)
                pool.wait_ge(pstep, st.next())
                pool.wait_ge(s5_bt, k)
                nc.gpsimd.tensor_tensor(BX[:, 0, :], PT[:, 0, :], PT[:, 1, :], ALU.subtract)
                nc.gpsimd.tensor_tensor(BX[:, 1, :], PT[:, 2, :], PT[:, 3, :], ALU.add).then_inc(s5_bx, 1)
                pool.wait_ge(s5_bx, k + 1)
                pool.wait_ge(s5_bsc, k + 1)
                pool.sem_inc(pool_go, 1)
                a = [w[:, bass.ds(k * QK, QK)].unsqueeze(2).to_broadcast([P, QK, SB]) for w in (abr, abi)]
                s = [S0[:, c, bass.ds(k * QK, QK), :] for c in range(2)]
                t = [PT[:, n, 0:QK * SB].rearrange("p (q b) -> p q b", q=QK) for n in range(4)]
                for step in range(ST):
                    for n, (c, e) in enumerate([(0, 0), (1, 1), (0, 1), (1, 0)]):
                        ins = nc.gpsimd.tensor_tensor(t[n], a[c], s[e], ALU.mult)
                    ins.then_inc(pstep, 1)
                    pool.wait_ge(pstep, st.next())
                    nc.gpsimd.tensor_tensor(t[0], t[0], t[1], ALU.subtract)
                    nc.gpsimd.tensor_tensor(t[2], t[2], t[3], ALU.add).then_inc(pstep, 1)
                    pool.wait_ge(pstep, st.next())
                    s = [BS[:, h, c, :, :, step] for c in range(2)]
                    nc.gpsimd.tensor_tensor(s[0], s[0], t[0], ALU.add)
                    ins = nc.gpsimd.tensor_tensor(s[1], s[1], t[2], ALU.add)
                    if step < ST - 1:
                        ins.then_inc(pstep, 1)
                        pool.wait_ge(pstep, st.next())
                        pool.sem_inc(pool_go, 1)
                ins.then_inc(s5_bsd, 1)
                pool.wait_ge(s5_bsd, k + 1)
                pool.sem_inc(pool_go, 1)
                for c in range(2):
                    ins = nc.gpsimd.tensor_copy(SSO[:, c, bass.ds(k * QK, QK), :], s[c])
                ins.then_inc(pstep, 1)
                pool.wait_ge(pstep, st.next())

            pool.wait_ge(small_in, 16)
            pool.wait_ge(s5_pv, 3)
            per_tile = 1 + 3 * ST
            for h in range(2):
                s5_tile(0, h, True)
            with pool.Fori(1, KT // 2) as i:
                st.enter(i - 1, 2 * per_tile + 0)
                for h in range(2):
                    s5_tile(i, h, False)
            st.leave(KT // 2 - 1)
            pool.dma_start(s5s_out, SSO[:].rearrange("p c q b -> p (c q b)")).then_inc(stores, 16)
            pool.wait_ge(s5_sf, 1)
            pool.dma_start(s5p_out, SF[:].rearrange("p c q -> p (c q)")).then_inc(stores, 16)
            pool.wait_ge(stores, 32)
            pool.sem_inc(s5_zero, 1)

            def gathers(layer):
                for n in ((2, 3) if layer == 0 else (4,)):
                    pool.wait_ge(norm_h, 3 * (n - 1))
                    pool.dma_start(GB[:, n % 2, :], norms[n:n + 1, :].partition_broadcast(P)).then_inc(gain_in, 16)
                pool.wait_ge(picks_ready, layer + 1)
                for table, base in ((experts_u[layer], 2 * layer * ROUNDS), (experts_v[layer], (2 * layer + 1) * ROUNDS)):
                    with pool.Fori(0, ROUNDS) as i:
                        for r in range(RING):
                            pool.wait_ge(row_used, i * RING + (base * RING + r + 1))
                            nc.gpsimd.tensor_copy(ixs[:, r:r + 1], GI[:, bass.ds(i * RING + r, 1)]).then_inc(index_set, 1)
                            pool.wait_ge(index_set, i * RING + (base * RING + r + 1))
                            pool.sem_inc(gather_go, 1)
                            pool.indirect_dma_start(ring[:, r, :], None, table,
                                                    bass.IndirectOffsetOnAxis(ap=ixs[:, r:r + 1], axis=0)).then_inc(row_in[r], 16)

            gathers(0)
            pool.wait_ge(peer_x, 1)
            pool.dma_start(LIN, lru_in).then_inc(lru_in_sem, 16)
            nc.gpsimd.memset(XBP[:, :, 0:3], 0.0).then_inc(lru_pad, 1)
            pool.wait_ge(lru_in_sem, 16)
            nc.gpsimd.tensor_copy(XBS[:, :, :, 0:3], LCONV).then_inc(lru_pad, 1)
            pool.wait_ge(lru_hs, 1)
            pool.dma_start(lru_out, LOUT).then_inc(stores, 16)
            pool.wait_ge(stores, 48)
            pool.sem_inc(s5_zero, 1)
            gathers(1)

        @block.tensor
        def _(pe):
            def norm_transposes(j):
                for t in range(TILES):
                    pe.wait_ge(norm_h, 3 * j + t + 1)
                    rows = P if t < 2 else NS
                    for g in range(GROUP):
                        n = 12 * j + 4 * t + g
                        if n >= 2:
                            pe.wait_ge(norm_ht, n - 1)
                        for e in range(4):
                            k = 4 * g + e
                            mm = nc.tensor.transpose(ps[:, 2 + n % 2, rows * e:rows * (e + 1)],
                                                     HN[0:rows, t, P * k:P * (k + 1)], ident[0:rows, 0:rows])
                        mm.then_inc(norm_tp, 1)

            def product(slab, n0, groups, rhs):
                with pe.Fori(0, groups) as g:
                    for r in range(GROUP):
                        slot = (slab + r) % WRING
                        pe.wait_ge(slab_in[slot], g * 16 + 16 * ((slab + r) // WRING + 1))
                        pe.wait_ge(bank_read, g * GROUP + (n0 + r + 1))
                        for k in range(KT):
                            mm = nc.tensor.matmul(ps[:, r % 2, 0:NT], W[:, slot, P * k:P * (k + 1)], rhs[:, k, :],
                                                  start=(k == 0), stop=(k == KT - 1))
                        mm.then_inc(slab_done, 1)

            def mixer_out(o, src, rep):
                for t in range(TILES):
                    if t == 2:
                        pe.wait_ge(mix_rep, o + 1)
                    for g in range(GROUP):
                        n = 12 * o + 4 * t + g
                        if n >= 2:
                            pe.wait_ge(mix_x, n - 1)
                        for e in range(4):
                            k = 4 * g + e
                            part = src[:, k, t * P:(t + 1) * P] if t < 2 else rep[:, P * k:P * (k + 1)]
                            mm = nc.tensor.transpose(ps[:, 2 + n % 2, P * e:P * (e + 1)], part, ident[:])
                        mm.then_inc(mix_tp, 1)

            def scores(layer):
                slab = (SLAB_KEY0, SLAB_KEY1)[layer]
                slot = slab % WRING
                pe.wait_ge(slab_in[slot], 16 * (slab // WRING + 1))
                pe.wait_ge(bank_read, (16 if layer == 0 else 80) + 16 + 2)
                for t in range(TILES):
                    if t == 2:
                        pe.wait_ge(key_rep, layer + 1)
                    if t > 0:
                        pe.wait_ge(key_sc, 3 * layer + t)
                    for j in range(LISTS):
                        q = QT[:, j, t * P:(t + 1) * P] if t < 2 else REPQ[:, P * j:P * (j + 1)]
                        mm = nc.tensor.matmul(ps[:, 4 + j // 4, P * (j % 4):P * (j % 4 + 1)], q,
                                              W[:, slot, P * j:P * (j + 1)], start=True, stop=True)
                    mm.then_inc(key_mm, 1)
                pe.wait_ge(key_sc, 3 * layer + 3)
                pe.sem_inc(slab_done, 1)

            def sample_sum(layer):
                pe.wait_ge(peer_acc, layer + 1)
                for c in range(4):
                    mm = nc.tensor.matmul(ps[:, 4 + c, :], repsum[:], ACC[:, BANK * c:BANK * (c + 1)], start=True, stop=True)
                mm.then_inc(peer_sum, 1)

            pe.wait_ge(consts, 2)
            norm_transposes(0)

            def s5_in_part(i, h, first):
                k = 2 * i + h
                pe.wait_ge(s5_bx, k + 1)
                pe.wait_ge(s5_btc, k)
                for c in range(2):
                    mm = nc.tensor.transpose(ps[:, 4, P * c:P * (c + 1)], BX[:, c, :], ident[:])
                mm.then_inc(s5_bt, 1)
                pe.wait_ge(s5_btc, k + 1)
                pe.wait_ge(s5_ux, k + 1)
                pe.wait_ge(s5_bur, k)
                pe.wait_ge(s5_bsc, k)
                for c in range(2):
                    for e in range(2):
                        nc.tensor.matmul(ps[:, 2 * c + e, :], BT[:, c, :], UX[:, 2 * e:2 * e + 2, 0:SEQ],
                                         start=True, stop=True)
                    mm = nc.tensor.matmul(ps[:, 6, P * c:P * (c + 1)], BT[:, c, :], UX[:, :, SEQ:NT],
                                          start=True, stop=True)
                mm.then_inc(s5_bu, 1)

            def s5_out_part(k, h):
                pe.wait_ge(s5_dd, k + 1)
                pe.wait_ge(s5_cn, k + 1)
                pe.wait_ge(s5_p, k + 1)
                pe.wait_ge(s5_bsd, k + 1)
                pe.wait_ge(s5_yg, k)
                nc.tensor.matmul(ps[:, 5, 0:SEQ], DD[:, h, :], HT[:, bass.ds(k, 1), 0:SEQ].rearrange("p a n -> p (a n)"),
                                 start=True, stop=False, skip_group_check=True)
                nc.tensor.matmul(ps[:, 7, 0:NS], DD[:, h, :], HT[:, bass.ds(k, 1), SEQ:NT].rearrange("p a n -> p (a n)"),
                                 start=True, stop=False, skip_group_check=True)
                for q in range(QK):
                    rows = slice(QC * q, QC * (q + 1))
                    cr, ci = BC[:, h, 2, rows], CN[:, h, rows]
                    for n, c in enumerate((cr, cr, ci, ci)):
                        nc.tensor.matmul(ps[rows, 5, 0:SEQ], c, PR[n][:, q, :], start=False, stop=(n == 3), skip_group_check=True)
                    for n, c in enumerate((cr, ci)):
                        mm = nc.tensor.matmul(ps[rows, 7, 0:NS], c, BSF[:, h, n, NS * q:NS * (q + 1)], start=False,
                                              stop=(n == 1), skip_group_check=True)
                mm.then_inc(s5_y, 1)

            s5_in_part(0, 0, True)
            s5_in_part(0, 1, True)
            s5_out_part(0, 0)
            with pe.Fori(1, KT // 2) as i:
                for h in range(2):
                    s5_in_part(i, h, False)
                    s5_out_part(2 * i + (h - 1), 1 - h)
            s5_out_part(KT - 1, 1)

            pe.wait_ge(s5_yg, KT)
            product(SLAB_GLU, 0, 4, YT)
            pe.wait_ge(glu_out, GROUP + 16)
            mixer_out(0, OT0, REP0)
            norm_transposes(1)
            pe.wait_ge(norm_ht, 24)
            product(SLAB_Q0, 16, 4, HT)
            scores(0)
            sample_sum(0)

            norm_transposes(2)
            pe.wait_ge(norm_ht, 36)
            product(SLAB_IN, 32, 8, HT)
            pe.wait_ge(lru_xc, 1)
            pe.wait_ge(bank_read, 64 + 2)
            for s in range(4):
                slot = (SLAB_GATE + s) % WRING
                pe.wait_ge(slab_in[slot], 16 * ((SLAB_GATE + s) // WRING + 1))
                for b in range(8):
                    n = 8 * s + b
                    head = 2 * s + b // 4
                    if n >= 2:
                        pe.wait_ge(gate_ev, n - 1)
                    for e in range(2):
                        at = P * (2 * b + e)
                        mm = nc.tensor.matmul(ps[:, n % 2, 0:NT], W[:, slot, at:at + P], XC[:, 2 * head + e, :],
                                              start=(e == 0), stop=(e == 1))
                    mm.then_inc(gate_mm, 1)
                pe.drain().then_inc(slab_done, 1)
            pe.wait_ge(gate_ev, 32)
            pe.wait_ge(lru_y, 1)
            product(SLAB_OUT, 64, 4, GT)
            pe.wait_ge(bank_read, 80 + 2)
            mixer_out(1, OT1, REP1)
            norm_transposes(3)
            pe.wait_ge(norm_ht, 48)
            product(SLAB_Q1, 80, 4, HT)
            scores(1)
            sample_sum(1)

        @block.scalar
        def _(act):
            act.dma_start(CH[:].rearrange("p v k -> p (v k)"), chan).then_inc(small_in, 16)
            act.dma_start(vecs, s5_vec).then_inc(s5_in, 16)
            act.dma_start(S0[:].rearrange("p c q b -> p (c q b)"), s5_h0).then_inc(s5_in, 16)
            act.sem_inc(bank_read, 2)
            A = nc.scalar.activation
            ast = Steps()

            def norm(j):
                if j == 0:
                    act.wait_ge(x_in, 16 * TILES)
                elif j % 2:
                    act.wait_ge(mix_x, 12 * (j // 2 + 1))
                else:
                    act.wait_ge(peer_x, j // 2)
                for t in range(TILES):
                    A(HN[:, t, :], X[:, t, :], ACT.Square, accum_out=nrm[:, t:t + 1]).then_inc(norm_sq, 1)
                act.wait_ge(norm_v, 2 * j + 1)
                A(nrm[:, 6:9], nrm[:, 3:6], ACT.Sqrt).then_inc(norm_rt, 1)

            def norm_rows(j):
                for t in range(TILES):
                    w = P if t < 2 else NS
                    for g in range(GROUP):
                        n = 12 * j + 4 * t + g
                        act.wait_ge(norm_tp, n + 1)
                        A(HT[:, 4 * g:4 * g + 4, token_cols(t)],
                          ps[:, 2 + n % 2, 0:4 * w].rearrange("p (k n) -> p k n", k=4), ACT.Copy).then_inc(norm_ht, 1)

            def replicate(rep, src):
                return A(rep.rearrange("p (k r n) -> p k r n", k=KT, r=COPIES),
                         src[:, :, SEQ:NT].unsqueeze(2).to_broadcast([P, KT, COPIES, NS]), ACT.Copy)

            def out_rows(o, src, rep):
                replicate(rep, src).then_inc(mix_rep, 1)

            norm(0)
            lr, li, dt = vecs[:, 0:64], vecs[:, 64:128], vecs[:, 128:192]
            dte, tnh, s1, c1, sh, tmp = (par[n][:, 0:64] for n in (4, 5, 6, 7, 8, 9))
            phi, half = par[10], par[11][:, 0:64]
            lrdt = par[12][:, 0:64]
            act.wait_ge(s5_in, 32)
            A(dte, dt, ACT.Exp).then_inc(s5_pa, 1)
            act.wait_ge(s5_pv, 1)
            A(tnh, lrdt, ACT.Tanh, scale=0.5).then_inc(s5_pa, 1)
            act.wait_ge(consts, 2)
            act.wait_ge(s5_pv, 2)
            A(s1, phi[:, 0:64], ACT.Sin, scale=TWO_PI_LOW).then_inc(s5_pa, 1)
            A(sh, phi[:, 0:64], ACT.Sin, scale=TWO_PI_LOW / 2).then_inc(s5_pa, 1)
            A(tmp, phi[:, 0:64], ACT.Abs).then_inc(s5_pa, 1)
            act.wait_ge(s5_pa, 5)
            A(c1, tmp, ACT.Sin, scale=-TWO_PI_LOW, bias=cst[:, 0:1]).then_inc(s5_pa, 1)
            norm_rows(0)
            act.wait_ge(norm_ht, 12)

            def turns(k1):
                for q in range(QK):
                    ins = A(PRD[:, q, :], iota[:], ACT.Copy, scale=phi[:, bass.ds(k1 * QK + q, 1)])
                ins.then_inc(s5_prod, 1)

            def tables(k1, slot):
                act.wait_ge(s5_f, k1 + 1)
                A(SIN[:, slot], PRD, ACT.Sin, scale=TWO_PI_LOW).then_inc(astep, 1)
                act.wait_ge(astep, ast.next())
                A(PRD, PRD, ACT.Abs).then_inc(astep, 1)
                act.wait_ge(astep, ast.next())
                A(COS[:, slot], PRD, ACT.Sin, scale=-TWO_PI_LOW, bias=cst[:, 0:1]).then_inc(s5_tab, 1)

            def gelu_y(k):
                act.wait_ge(s5_y, k + 1)
                A(YT[:, bass.ds(k, 1), 0:SEQ].rearrange("p a n -> p (a n)"), ps[:, 5, 0:SEQ], ACT.Gelu)
                A(YT[:, bass.ds(k, 1), SEQ:NT].rearrange("p a n -> p (a n)"), ps[:, 7, 0:NS], ACT.Gelu).then_inc(s5_yg, 1)

            def s5_tile(i, h, first):
                k = 2 * i + h
                act.wait_ge(s5_bu, k)
                for q in range(QK):
                    rows = slice(QC * q, QC * (q + 1))
                    ins = A(UX[rows, q, :], HT[rows, bass.ds(k, 1), :].rearrange("p a n -> p (a n)"), ACT.Copy)
                ins.then_inc(s5_ux, 1)
                act.wait_ge(s5_bc_in[h], (i + 1) * 16)
                if not first:
                    act.wait_ge(s5_y, k - 1)
                A(CN[:, h, :], BC[:, h, 3, :], ACT.Copy, scale=-1.0).then_inc(s5_cn, 1)
                act.wait_ge(s5_bt, k + 1)
                A(BT[:].rearrange("p c n -> p (c n)"), ps[:, 4, 0:2 * P], ACT.Copy).then_inc(s5_btc, 1)
                act.wait_ge(s5_tab, k + 1)
                turns(k + 1)
                if not (first and h == 0):
                    act.wait_ge(s5_p, k)
                tables(k + 1, 1 - h)
                act.wait_ge(s5_bu, k + 1)
                A(BSF[:, h, :, :], ps[:, 6, 0:2 * P].rearrange("p (c n) -> p c n", c=2), ACT.Copy).then_inc(s5_bsc, 1)
                if not (first and h == 0):
                    gelu_y(k - 1)

            act.wait_ge(s5_pv, 3)
            turns(0)
            tables(0, 0)
            s5_tile(0, 0, True)
            s5_tile(0, 1, True)
            with act.Fori(1, KT // 2) as i:
                ast.enter(i - 1, 4)
                s5_tile(i, 0, False)
                s5_tile(i, 1, False)
            ast.leave(KT // 2 - 1)
            gelu_y(KT - 1)

            with act.Fori(0, 4) as g:
                for r in range(GROUP):
                    act.wait_ge(slab_done, g * GROUP + (SLAB_GLU + r + 1))
                    act.wait_ge(glu_out, g * GROUP + (r + 1))
                    A(SIG[:, r, :], ps[:, r % 2, 0:NT], ACT.Sigmoid,
                      bias=CH[:, V_BGLU, bass.ds(g * GROUP + r, 1)]).then_inc(bank_read, 1)
            act.wait_ge(glu_out, GROUP + 16)
            out_rows(0, OT0, REP0)
            norm(1)
            norm_rows(1)

            def evacuate(slab, groups, dst):
                with act.Fori(0, groups) as g:
                    for r in range(GROUP):
                        act.wait_ge(slab_done, g * GROUP + (slab + r + 1))
                        A(dst[:, bass.ds(g * GROUP + r, 1), :].rearrange("p a n -> p (a n)"), ps[:, r % 2, 0:NT],
                          ACT.Copy).then_inc(bank_read, 1)

            def peer(layer):
                act.wait_ge(s5_zero, layer + 1)
                evacuate((SLAB_Q0, SLAB_Q1)[layer], 4, QT)
                act.wait_ge(bank_read, (34, 98)[layer])
                replicate(REPQ, QT).then_inc(key_rep, 1)
                for t in range(TILES):
                    act.wait_ge(key_mm, 3 * layer + t + 1)
                    if t > 0:
                        act.wait_ge(tile_top, 3 * layer + t)
                    A(SC, ps[:, 4:8, :].rearrange("p b n -> p (b n)"), ACT.Copy).then_inc(key_sc, 1)
                    act.wait_ge(soft_in, 3 * layer + t + 1)
                    A(GE2, GE, ACT.Exp).then_inc(soft_exp, 1)
                act.wait_ge(dots, layer + 1)
                A(WG[:, 0:COLS], AV[:, 0:COLS], ACT.Gelu).then_inc(act_g, 1)

            peer(0)
            norm(2)
            norm_rows(2)
            with act.Fori(0, 4) as g:
                for r in range(GROUP):
                    act.wait_ge(slab_done, g * GROUP + (SLAB_IN + r + 1))
                    A(GT[:, bass.ds(g * GROUP + r, 1), :].rearrange("p a n -> p (a n)"), ps[:, r % 2, 0:NT],
                      ACT.Gelu).then_inc(bank_read, 1)
            act.wait_ge(lru_pad, 2)
            with act.Fori(0, 4) as g:
                for r in range(GROUP):
                    act.wait_ge(slab_done, g * GROUP + (SLAB_IN + 16 + r + 1))
                    A(XBP[:, bass.ds(g * GROUP + r, 1), 3:].rearrange("p a n -> p (a n)"), ps[:, r % 2, 0:SEQ], ACT.Copy)
                    A(XBS[:, bass.ds(g * GROUP + r, 1), :, 3:].rearrange("p a b n -> p (a b) n"),
                      ps[:, r % 2, SEQ:NT].rearrange("p (b n) -> p b n", b=SB), ACT.Copy).then_inc(bank_read, 1)
            lam = CH[:, V_LAM, :]
            A(LS[0], lam, ACT.Abs).then_inc(lru_sp, 1)
            act.wait_ge(lru_sp, 1)
            A(LS[1], LS[0], ACT.Exp, scale=-1.0).then_inc(lru_sp, 1)
            act.wait_ge(lru_sp, 3)
            A(LS[3], LS[2], ACT.Ln).then_inc(lru_sp, 1)
            for s in range(4):
                for b in range(8):
                    n = 8 * s + b
                    head, gate, jt = 2 * s + b // 4, b // 2 % 2, b % 2
                    ch = 2 * head + jt
                    act.wait_ge(gate_mm, n + 1)
                    A((RA, IG)[gate][:, ch, :], ps[:, n % 2, 0:NT], ACT.Sigmoid,
                      bias=CH[:, (V_BA, V_BI)[gate], ch:ch + 1]).then_inc(gate_ev, 1)
            act.wait_ge(lru_sp, 5)
            act.wait_ge(gate_ev, 32)
            act.wait_ge(lru_st, 1)
            for k in range(KT):
                ins = A(TH[:, k, :], RA[:, k, :], ACT.Tanh, scale=LS[5][:, k:k + 1])
            ins.then_inc(lru_th, 1)
            for k in range(KT):
                ins = A(RA[:, k, :], RA[:, k, :], ACT.Exp, scale=LS[6][:, k:k + 1])
            ins.then_inc(lru_a, 1)
            act.wait_ge(lru_v, 1)
            A(TH, TH, ACT.Sqrt).then_inc(lru_rt, 1)
            evacuate(SLAB_OUT, 4, OT1)
            act.wait_ge(bank_read, 82)
            out_rows(1, OT1, REP1)
            norm(3)
            norm_rows(3)
            peer(1)
            norm(4)

        @block.vector
        def _(dve):
            V = nc.vector
            st = Steps()
            dve.sem_inc(row_used, RING)
            dve.sem_inc(glu_out, GROUP)

            def settle(ins):
                ins.then_inc(vstep, 1)
                dve.wait_ge(vstep, st.next())

            def settle_all(ins):
                settle(ins)
                dve.sem_inc(top_go, 1)

            def norm(j):
                dve.wait_ge(norm_sq, 3 * (j + 1))
                V.tensor_scalar(nrm[:, 3:6], nrm[:, 0:3], 1.0 / D, EPS, ALU.mult, ALU.add).then_inc(norm_v, 1)
                dve.wait_ge(norm_rt, j + 1)
                V.reciprocal(nrm[:, 9:12], nrm[:, 6:9]).then_inc(norm_v, 1)
                dve.wait_ge(norm_v, 2 * j + 2)
                dve.wait_ge(gain_in, (32, 32, 64, 64, 80)[j])
                for t in range(TILES):
                    V.scalar_tensor_tensor(HN[:, t, :], X[:, t, :], nrm[:, 9 + t:10 + t], GB[:, j % 2, :],
                                           ALU.mult, ALU.mult).then_inc(norm_h, 1)

            def add_mixer(o):
                for t in range(TILES):
                    for g in range(GROUP):
                        n = 12 * o + 4 * t + g
                        dve.wait_ge(mix_tp, n + 1)
                        cols = slice(BANK * g, BANK * (g + 1))
                        V.tensor_tensor(X[:, t, cols], ps[:, 2 + n % 2, :], X[:, t, cols], ALU.add).then_inc(mix_x, 1)

            norm(0)
            lr, li = vecs[:, 0:64], vecs[:, 64:128]
            abr, abi, fr, fi = (par[n][:, 0:64] for n in range(4))
            dte, tnh, s1, c1, sh = (par[n][:, 0:64] for n in (4, 5, 6, 7, 8))
            phi, lrdt = par[10], par[12][:, 0:64]
            e1, den, nr, t1, t2, dec, trn, t3 = (par[n][:, 0:64] for n in range(13, 21))
            V.memset(UX, 0.0)
            V.memset(phi, 0.0).then_inc(vstep, 1)
            st.next()
            dve.wait_ge(s5_pa, 1)
            V.tensor_tensor(lrdt, lr, dte, ALU.mult).then_inc(s5_pv, 1)
            settle(V.tensor_tensor(trn, li, dte, ALU.mult))
            settle(V.tensor_scalar(trn, trn, 1.0 / (2 * PI), None, ALU.mult))
            settle(V.tensor_scalar(t1, trn, ROUND, ROUND, ALU.add, ALU.subtract))
            V.tensor_tensor(phi[:, 0:64], trn, t1, ALU.subtract).then_inc(s5_pv, 1)
            V.tensor_tensor(t3, lr, lr, ALU.mult)
            settle(V.tensor_tensor(t2, li, li, ALU.mult))
            settle(V.tensor_tensor(den, t3, t2, ALU.add))
            V.reciprocal(den, den)
            dve.wait_ge(s5_pa, 2)
            settle(V.tensor_scalar(t1, tnh, -1.0, 1.0, ALU.mult, ALU.add))
            settle(V.reciprocal(t1, t1))
            settle(V.scalar_tensor_tensor(e1, tnh, 2.0, t1, ALU.mult, ALU.mult))
            settle(V.tensor_scalar(dec, e1, 1.0, None, ALU.add))
            dve.wait_ge(s5_pa, 6)
            V.tensor_tensor(abr, dec, c1, ALU.mult)
            V.tensor_tensor(abi, dec, s1, ALU.mult)
            V.scalar_tensor_tensor(t1, sh, -2.0, sh, ALU.mult, ALU.mult)
            settle(V.tensor_tensor(nr, e1, c1, ALU.mult))
            settle(V.tensor_tensor(nr, nr, t1, ALU.add))
            V.tensor_tensor(fr, nr, lr, ALU.mult)
            V.tensor_tensor(t1, abi, li, ALU.mult)
            V.tensor_tensor(fi, abi, lr, ALU.mult)
            settle(V.tensor_tensor(t2, nr, li, ALU.mult))
            V.tensor_tensor(fr, fr, t1, ALU.add)
            settle(V.tensor_tensor(fi, fi, t2, ALU.subtract))
            V.tensor_tensor(fr, fr, den, ALU.mult)
            V.tensor_tensor(fi, fi, den, ALU.mult).then_inc(s5_pv, 1)

            def fractions(k1):
                dve.wait_ge(s5_prod, k1 + 1)
                settle(V.tensor_scalar(M[0], PRD, ROUND, ROUND, ALU.add, ALU.subtract))
                V.tensor_tensor(PRD, PRD, M[0], ALU.subtract).then_inc(s5_f, 1)

            def s5_tile(i, h, first):
                k = 2 * i + h
                fractions(k + 1)
                dve.wait_ge(s5_f, k + 2)
                dve.wait_ge(s5_bu, k + 1)
                dve.wait_ge(s5_tab, k + 1)
                re = ps[:, 0:2, :].rearrange("p b (q t) -> p (b q) t", q=2)
                im = ps[:, 2:4, :].rearrange("p b (q t) -> p (b q) t", q=2)
                cos, sin = COS[:, h], SIN[:, h]
                V.tensor_tensor(M[0], re, cos, ALU.mult)
                V.tensor_tensor(M[1], im, sin, ALU.mult)
                V.tensor_tensor(M[2], im, cos, ALU.mult)
                V.tensor_tensor(M[3], re, sin, ALU.mult).then_inc(s5_bur, 1)
                dve.wait_ge(s5_bur, k + 1)
                V.tensor_tensor(M[0], M[0], M[1], ALU.add)
                settle(V.tensor_tensor(M[2], M[2], M[3], ALU.subtract))
                for src, dst in ((M[0], M[1]), (M[2], M[3])):
                    for q in range(QK):
                        ins = V.tensor_tensor_scan(dst[:, q, :], dec[:, bass.ds(k * QK + q, 1)].to_broadcast([P, SEQ]),
                                                   src[:, q, :], 0.0, ALU.mult, ALU.add)
                settle(ins)
                if not (first and h == 0):
                    dve.wait_ge(s5_y, k)
                V.tensor_tensor(PR[0], cos, M[1], ALU.mult)
                V.scalar_tensor_tensor(PR[1], sin, -1.0, M[3], ALU.mult, ALU.mult)
                V.tensor_tensor(PR[2], sin, M[1], ALU.mult)
                V.tensor_tensor(PR[3], cos, M[3], ALU.mult).then_inc(s5_p, 1)
                dve.wait_ge(s5_p, k + 1)
                last = [w[:, :, SEQ - 1:SEQ].rearrange("p q a -> p (q a)") for w in PR]
                V.tensor_tensor(SF[:, 0, bass.ds(k * QK, QK)], last[0], last[1], ALU.add)
                V.tensor_tensor(SF[:, 1, bass.ds(k * QK, QK)], last[2], last[3], ALU.add)

            dve.wait_ge(norm_tp, 12)
            fractions(0)
            dve.wait_ge(s5_f, 1)
            s5_tile(0, 0, True)
            s5_tile(0, 1, True)
            with dve.Fori(1, KT // 2) as i:
                st.enter(i - 1, 6)
                s5_tile(i, 0, False)
                s5_tile(i, 1, False)
            st.leave(KT // 2 - 1)
            dve.drain().then_inc(s5_sf, 1)

            dve.wait_ge(s5_y, KT)
            with dve.Fori(0, 4) as g:
                for r in range(GROUP):
                    dve.wait_ge(bank_read, g * GROUP + (r + 3))
                    n = g * GROUP + r
                    V.tensor_tensor(OT0[:, bass.ds(n, 1), :].rearrange("p a n -> p (a n)"), SIG[:, r, :],
                                    YT[:, bass.ds(n, 1), :].rearrange("p a n -> p (a n)"), ALU.mult).then_inc(glu_out, 1)
            add_mixer(0)
            dve.wait_ge(mix_x, 12)
            norm(1)

            def lists(ap, n, w):
                return [ap[:, w * j:w * (j + 1)] for j in range(n)]

            def top16(values, work, best, index, n, w):
                vs, ws, bs, ix = lists(values, n, w), lists(work, n, w), lists(best, n, TOPK), lists(index, n, TOPK)
                for j in range(n):
                    ins = V.max(bs[j][:, 0:8], vs[j])
                settle_all(ins)
                for j in range(n):
                    V.max_index(ix[j][:, 0:8], bs[j][:, 0:8], vs[j])
                    ins = V.match_replace(ws[j], bs[j][:, 0:8], vs[j], LOWEST)
                settle_all(ins)
                for j in range(n):
                    ins = V.max(bs[j][:, 8:16], ws[j])
                settle_all(ins)
                for j in range(n):
                    ins = V.max_index(ix[j][:, 8:16], bs[j][:, 8:16], ws[j])
                settle_all(ins)

            tv4 = TV.rearrange("p (h s k) -> p h s k", h=HEADS, s=2)
            tf4 = TF.rearrange("p (h s k) -> p h s k", h=HEADS, s=2)
            cube = [P, HEADS, TOPK, TOPK]

            def as_cube(ap):
                return ap.rearrange("p (h a b) -> p h a b", h=HEADS, a=TOPK)

            def choose(layer, t):
                dve.wait_ge(key_sc, t + (3 * layer + 1))
                dve.sem_inc(top_go, 1)
                top16(SC, SCW, TV, TI, LISTS, NKEYS)
                V.tensor_copy(TF, TI)
                settle_all(V.tensor_tensor(as_cube(SC), tv4[:, :, 0, :].unsqueeze(3).to_broadcast(cube),
                                       tv4[:, :, 1, :].unsqueeze(2).to_broadcast(cube), ALU.add))
                top16(SC, SCW, BV, BP, HEADS, TOPK * TOPK)
                bv = BV.rearrange("p (h k) -> p h k", h=HEADS)
                V.tensor_scalar(AB[:, 0:PICKS], BP, 4, None, ALU.logical_shift_right)
                V.tensor_scalar(AB[:, PICKS:], BP, 15, None, ALU.bitwise_and)
                V.tensor_tensor(GE.rearrange("p (h k) -> p h k", h=HEADS), bv,
                                bv[:, :, 0:1].to_broadcast([P, HEADS, TOPK]), ALU.subtract).then_inc(soft_in, 1)
                dve.wait_ge(soft_in, t + (3 * layer + 1))
                settle(V.tensor_copy(ABF, AB))
                for s in range(2):
                    part = ABF[:, PICKS * s:PICKS * (s + 1)].rearrange("p (h k) -> p h k", h=HEADS)
                    settle(V.tensor_tensor(as_cube(OH), part.unsqueeze(3).to_broadcast(cube),
                                           iota[:, 0:TOPK].unsqueeze(1).unsqueeze(1).to_broadcast(cube), ALU.is_equal))
                    settle(V.tensor_tensor(as_cube(OH), as_cube(OH),
                                           tf4[:, :, s, :].unsqueeze(2).to_broadcast(cube), ALU.mult))
                    settle(V.tensor_reduce(II[:, PICKS * s:PICKS * (s + 1)], as_cube(OH).rearrange("p h a b -> p (h a) b"),
                                           AX_X, ALU.add))
                V.scalar_tensor_tensor(GI[:, bass.ds(t * PICKS, PICKS)], II[:, 0:PICKS], float(NKEYS), II[:, PICKS:],
                                       ALU.mult, ALU.add)
                dve.wait_ge(soft_exp, t + (3 * layer + 1))
                ge = GE2.rearrange("p (h k) -> p h k", h=HEADS)
                settle(V.tensor_reduce(GS[:, 0:HEADS], ge, AX_X, ALU.add))
                settle(V.reciprocal(GS[:, HEADS:], GS[:, 0:HEADS]))
                V.tensor_tensor(GG[:, bass.ds(t * PICKS, PICKS)].rearrange("p (h k) -> p h k", h=HEADS), ge,
                                GS[:, HEADS:].unsqueeze(2).to_broadcast([P, HEADS, TOPK]), ALU.mult).then_inc(tile_top, 1)

            def peer(layer):
                with dve.Fori(0, TILES) as t:
                    st.enter(t, 18)
                    choose(layer, t)
                st.leave(TILES)
                dve.wait_ge(tile_top, 3 * layer + 3)
                for c in range(1, COPIES):
                    rows, src = slice(NS * c, NS * (c + 1)), slice(2 * PICKS + NS * c, 2 * PICKS + NS * (c + 1))
                    V.tensor_copy(GG[rows, 2 * PICKS:COLS], GG[rows, src])
                    ins = V.tensor_copy(GI[rows, 2 * PICKS:COLS], GI[rows, src])
                ins.then_inc(picks_ready, 1)
                dve.wait_ge(picks_ready, layer + 1)
                settle(V.memset(ACC, 0.0))
                base = 2 * layer * ROUNDS
                for t in range(TILES):
                    with dve.Fori(0, ROUNDS_OF[t]) as i:
                        first = base + ROUND_AT[t]
                        for r in range(RING):
                            dve.wait_ge(row_in[r], i * 16 + 16 * (first + 1))
                            V.tensor_tensor_reduce(ring[:, r, :], ring[:, r, :], HN[:, t, :], 1.0, 0.0, ALU.mult, ALU.add,
                                                   A8[:, r:r + 1]).then_inc(row_used, 1)
                        dve.wait_ge(row_used, i * RING + (RING * (first + 1) + RING))
                        st.enter(i, 1)
                        settle(V.tensor_copy(AV[:, bass.ds(i * RING + ROUND_AT[t] * RING, RING)], A8))
                    st.leave(ROUNDS_OF[t])
                dve.sem_inc(dots, 1)
                dve.wait_ge(act_g, layer + 1)
                settle(V.tensor_tensor(WG[:, 0:COLS], WG[:, 0:COLS], GG[:, 0:COLS], ALU.mult))
                base += ROUNDS
                for t in range(TILES):
                    to = X[:, t, :] if t < 2 else ACC
                    with dve.Fori(0, ROUNDS_OF[t]) as i:
                        first = base + ROUND_AT[t]
                        for r in range(RING):
                            dve.wait_ge(row_in[r], i * 16 + 16 * (first + 1))
                            dve.wait_ge(row_used, i * RING + (RING * first + RING + r))
                            V.scalar_tensor_tensor(to, ring[:, r, :], WG[:, bass.ds(i * RING + (ROUND_AT[t] * RING + r), 1)],
                                                   to, ALU.mult, ALU.add).then_inc(row_used, 1)
                dve.wait_ge(row_used, RING * (base + ROUNDS) + RING)
                dve.sem_inc(peer_acc, 1)
                dve.wait_ge(peer_sum, layer + 1)
                V.tensor_tensor(X[:, 2, :], ps[:, 4:8, :].rearrange("p b n -> p (b n)"), X[:, 2, :], ALU.add).then_inc(peer_x, 1)
                dve.wait_ge(peer_x, layer + 1)

            peer(0)
            norm(2)
            lam = CH[:, V_LAM, :]
            dve.wait_ge(lru_sp, 2)
            V.tensor_scalar(LS[2], LS[1], 1.0, None, ALU.add).then_inc(lru_sp, 1)
            dve.wait_ge(lru_sp, 4)
            settle(V.tensor_scalar(LS[4], LS[2], -1.0, None, ALU.add))
            settle(V.tensor_scalar(LS[7], LS[4], 0.0, None, ALU.is_equal))
            settle(V.tensor_tensor(LS[4], LS[4], LS[7], ALU.add))
            settle(V.reciprocal(LS[4], LS[4]))
            settle(V.tensor_tensor(LS[3], LS[3], LS[7], ALU.add))
            settle(V.tensor_tensor(LS[3], LS[3], LS[4], ALU.mult))
            settle(V.tensor_tensor(LS[3], LS[3], LS[1], ALU.mult))
            settle(V.tensor_scalar(LS[4], lam, -1.0, 0.0, ALU.mult, ALU.max))
            settle(V.tensor_tensor(LS[3], LS[3], LS[4], ALU.add))
            V.tensor_scalar(LS[5], LS[3], 8.0, None, ALU.mult)
            V.tensor_scalar(LS[6], LS[3], -8.0, None, ALU.mult).then_inc(lru_sp, 1)
            cw = [CH[:, V_CW + n, :] for n in range(4)]
            with dve.Fori(0, KT) as k:
                dve.wait_ge(bank_read, k + (48 + 3))
                st.enter(k, 4)
                xp = XBP[:, bass.ds(k, 1), :].rearrange("p a n -> p (a n)")
                xs = XBS[:, bass.ds(k, 1), :, :].rearrange("p a b n -> p (a b) n")
                op = XC[:, bass.ds(k, 1), 0:SEQ].rearrange("p a n -> p (a n)")
                os_ = XC[:, bass.ds(k, 1), SEQ:NT].rearrange("p a (b n) -> p (a b) n", b=SB)
                one = bass.ds(k, 1)
                V.tensor_scalar(op, xp[:, 0:SEQ], cw[0][:, one], CH[:, V_CB, one], ALU.mult, ALU.add)
                settle(V.tensor_scalar(os_, xs[:, :, 0:ST], cw[0][:, one], CH[:, V_CB, one], ALU.mult, ALU.add))
                for n in range(1, 4):
                    V.scalar_tensor_tensor(op, xp[:, n:n + SEQ], cw[n][:, one], op, ALU.mult, ALU.add)
                    settle(V.scalar_tensor_tensor(os_, xs[:, :, n:n + ST], cw[n][:, one], os_, ALU.mult, ALU.add))
            st.leave(KT)
            V.tensor_copy(LOUT[:, 16:64].rearrange("p (k n) -> p k n", k=KT), XBP[:, :, SEQ:SEQ + 3])
            V.tensor_copy(LOUT[:, 192:576].rearrange("p (k b n) -> p k b n", k=KT, b=SB), XBS[:, :, :, 4:7]).then_inc(lru_st, 1)
            dve.sem_inc(lru_xc, 1)
            dve.wait_ge(gate_ev, 32)
            V.tensor_tensor(IG, IG, XC, ALU.mult)
            dve.wait_ge(lru_th, 1)
            settle(V.tensor_scalar(HT[:], TH, 1.0, None, ALU.add))
            settle(V.reciprocal(HT[:], HT[:]))
            V.scalar_tensor_tensor(TH, TH, 2.0, HT[:], ALU.mult, ALU.mult).then_inc(lru_v, 1)
            dve.wait_ge(lru_rt, 1)
            settle(V.tensor_tensor(IG, IG, TH, ALU.mult))
            dve.wait_ge(lru_a, 1)
            with dve.Fori(0, KT) as k:
                one = bass.ds(k, 1)
                V.tensor_tensor_scan(XC[:, one, 0:SEQ].rearrange("p a n -> p (a n)"),
                                     RA[:, one, 0:SEQ].rearrange("p a n -> p (a n)"),
                                     IG[:, one, 0:SEQ].rearrange("p a n -> p (a n)"), 0.0, ALU.mult, ALU.add)
            ra_s = RA[:, :, SEQ:NT].rearrange("p k (b t) -> p k b t", b=SB)
            bx_s = IG[:, :, SEQ:NT].rearrange("p k (b t) -> p k b t", b=SB)
            hs_s = XC[:, :, SEQ:NT].rearrange("p k (b t) -> p k b t", b=SB)
            prev = LH0
            for n in range(ST):
                settle(V.tensor_tensor(LT, ra_s[:, :, :, n], prev, ALU.mult))
                settle(V.tensor_tensor(hs_s[:, :, :, n], bx_s[:, :, :, n], LT, ALU.add))
                prev = hs_s[:, :, :, n]
            V.tensor_copy(LOUT[:, 0:16], XC[:, :, SEQ - 1])
            V.tensor_copy(LOUT[:, 64:192].rearrange("p (k b) -> p k b", k=KT), prev).then_inc(lru_hs, 1)
            V.tensor_tensor(GT, GT, XC, ALU.mult).then_inc(lru_y, 1)
            dve.wait_ge(bank_read, 82)
            add_mixer(1)
            dve.wait_ge(mix_x, 24)
            norm(3)
            peer(1)
            norm(4)


def kernel(**inputs):
    import numpy as np
    import concourse.bacc as _bacc
    from concourse import mybir as _mybir
    from concourse.bass_utils import run_bass_kernel_spmd as _run

    a = {k: np.asarray(v) for k, v in inputs.items()}

    def column_slabs(w):
        n = w.shape[1] // P
        return w.reshape(KT, P, n, P).transpose(2, 1, 0, 3).reshape(n, P, D)

    gates = np.stack([a["lru_w_a"][0], a["lru_w_i"][0]]).reshape(2, 4, 2, 2, P, 2, P)
    keys = a["peer_sub_keys"].reshape(2, LISTS, NKEYS, P).transpose(0, 3, 1, 2).reshape(2, P, D)
    slabs = np.concatenate([
        column_slabs(a["s5_w_glu"][0]), column_slabs(a["peer_w_q"][0]), keys[0:1], column_slabs(a["lru_w_in"][0]),
        gates.transpose(1, 4, 2, 0, 5, 3, 6).reshape(4, P, D), column_slabs(a["lru_w_out"][0]),
        column_slabs(a["peer_w_q"][1]), keys[1:2]])

    def channels(v):
        return v.reshape(KT, P).T

    chan = np.concatenate([channels(v) for v in (
        a["s5_d"][0], a["s5_b_glu"][0], *a["lru_conv_w"][0], a["lru_conv_b"][0],
        a["lru_b_a"][0].reshape(-1), a["lru_b_i"][0].reshape(-1), a["lru_lam"][0])], axis=1)

    def states(v):
        return v.reshape(S5_Q, 2, 64, *v.shape[2:]).transpose(1, 2, 0, *range(3, v.ndim + 1)).reshape(P, S5_Q, *v.shape[2:])

    log_dt = np.repeat(a["s5_log_dt"][0][:, None], 64, axis=1)
    s5_vec = np.concatenate([states(a["s5_lam_re"][0]), states(a["s5_lam_im"][0]), states(log_dt)], axis=1)

    def by_group(v):
        out = np.zeros((2, 64, S5_Q, 2, 16), v.dtype)
        w = v.reshape(2, 64, S5_Q, 16)
        out[0, :, :, 0], out[1, :, :, 1] = w[0], w[1]
        return out.reshape(P, KT, P)

    bc = [by_group(states(v)) for v in (a["s5_b_re"][0], a["s5_b_im"][0], a["s5_c_re"][0].transpose(0, 2, 1),
                                        a["s5_c_im"][0].transpose(0, 2, 1))]
    s5_bc = np.stack(bc, axis=2).transpose(1, 0, 2, 3).reshape(KT, P, 4 * P)
    s5_h0 = np.concatenate([states(v[0].transpose(1, 2, 0)).reshape(P, -1) for v in (a["state_s5_re"], a["state_s5_im"])], axis=1)
    conv = a["state_lru_conv"][0].reshape(SB, 3, KT, P).transpose(3, 2, 0, 1).reshape(P, -1)
    h0 = a["state_lru_h"][0].reshape(SB, KT, P).transpose(2, 1, 0).reshape(P, -1)
    sample = a["x_sample"].reshape(NS, D)
    arrays = {
        "x": np.concatenate([a["x_prompt"].reshape(2, P, D), np.tile(sample, (COPIES, 1))[None]]),
        "norms": np.stack([a["norm_mix"][0], a["norm_ffn"][0], a["norm_mix"][1], a["norm_ffn"][1], a["norm_final"]]),
        "slabs": slabs, "chan": chan, "s5_vec": s5_vec, "s5_bc": s5_bc, "s5_h0": s5_h0,
        "lru_in": np.concatenate([conv, h0], axis=1),
        "u0": a["peer_u"][0], "v0": a["peer_v"][0], "u1": a["peer_u"][1], "v1": a["peer_v"][1],
    }
    outs = {"y": (2, P, D), "ys": (NS, D), "s5p": (P, 2 * S5_Q), "s5s": (P, 2 * S5_Q * SB), "lru": (P, 576)}

    nc = _bacc.Bacc("TRN2", target_bir_lowering=False, num_devices=1)
    args, in_map = [], {}
    for name, v in arrays.items():
        v = np.ascontiguousarray(v)
        in_map[f"in_{name}_dram"] = v
        args.append(nc.dram_tensor(f"in_{name}_dram", v.shape, _mybir.dt.from_np(v.dtype), kind="ExternalInput").ap())
    for name, shape in outs.items():
        args.append(nc.dram_tensor(f"out_{name}_dram", shape, F32, kind="ExternalOutput").ap())
    hybrid_step(nc, *args)
    r = _run(nc, [in_map], core_ids=[0]).results[0]
    y, ys, s5p, s5s, lru = (np.asarray(r[f"out_{name}_dram"]) for name in outs)

    def groups(v):
        return v.reshape(2, 64, S5_Q, -1).transpose(3, 2, 0, 1).reshape(-1, 2 * S5_Q, 64)

    s5p = s5p.reshape(P, 2, S5_Q)
    s5s = s5s.reshape(P, 2, S5_Q, SB)
    hp, cp, hs, cs = lru[:, 0:16], lru[:, 16:64], lru[:, 64:192], lru[:, 192:576]
    return (y.reshape(1, SEQ, D), ys.reshape(SB, ST, D),
            groups(s5p[:, 0])[None], groups(s5p[:, 1])[None], groups(s5s[:, 0])[None], groups(s5s[:, 1])[None],
            hp.T.reshape(1, 1, D), cp.reshape(P, KT, 3).transpose(2, 1, 0).reshape(1, 1, 3, D),
            hs.reshape(P, KT, SB).transpose(2, 1, 0).reshape(1, SB, D),
            cs.reshape(P, KT, SB, 3).transpose(2, 3, 1, 0).reshape(1, SB, 3, D))
```

```python
from contextlib import ExitStack

import concourse.bass as bass
from concourse import mybir

F32 = mybir.dt.float32
I32 = mybir.dt.int32
U32 = mybir.dt.uint32
ALU = mybir.AluOpType
ACT = mybir.ActivationFunctionType
AX_X = mybir.AxisListType.X

P = 128
D = 2048
KT = D // P
SEQ = 256
SB, ST = 8, 4
NS = SB * ST
NT = SEQ + NS
TILES = 3
COPIES = P // NS
BANK = 512
GROUP = 4
PI = 3.14159265358979
TWO_PI_LOW = 6.283185
ROUND = 12582912.0
EPS = 1e-6
LOWEST = -3.0e38

S5_Q = 64
QK = 4
QC = 32

SLAB_GLU, SLAB_Q0, SLAB_XB, SLAB_GATE, SLAB_IN, SLAB_OUT, SLAB_Q1, SLABS = 0, 16, 32, 48, 52, 68, 84, 100
WRING = 4

HEADS, TOPK, NKEYS = 8, 16, 128
CANDS = TOPK * TOPK
PICKS = HEADS * TOPK
RING = 8
EARLY = 6
COLS = 2 * PICKS + PICKS // COPIES
ROUNDS_OF = [PICKS // RING, PICKS // RING, PICKS // COPIES // RING]
ROUND_AT = [0, PICKS // RING, 2 * PICKS // RING]
ROUNDS = COLS // RING

V_D, V_BGLU, V_CW, V_CB, V_BA, V_BI, V_LAM, V_N = 0, 1, 2, 6, 7, 8, 9, 10


def token_cols(t):
    return slice(t * P, (t + 1) * P) if t < 2 else slice(SEQ, NT)


class Steps:

    def __init__(self):
        self.base, self.i, self.per, self.n = 0, 0, 0, 0

    def enter(self, i, per):
        self.base, self.i, self.per, self.n = self.base + self.n, i, per, 0

    def leave(self, rounds):
        assert self.n == self.per, (self.n, self.per)
        self.base, self.i, self.per, self.n = self.base + rounds * self.per, 0, 0, 0

    def next(self):
        self.n += 1
        return self.i * self.per + (self.base + self.n)


def hybrid_step(nc, x, norms, slabs, keys, chan, s5_vec, s5_bc, s5_h0, lru_in, u0, v0, u1, v1,
                y_out, ys_out, s5p_out, s5s_out, lru_out):
    experts_u, experts_v = [u0, u1], [v0, v1]
    with ExitStack() as ctx:
        def sb(name, shape, dt=F32):
            return ctx.enter_context(nc.sbuf_tensor(name, shape, dt))

        def sem(name):
            return ctx.enter_context(nc.semaphore(name))

        X = sb("X", [P, TILES, D])
        HN = sb("HN", [P, TILES, D])
        HT = sb("HT", [P, KT, NT])
        W = sb("W", [P, WRING, D])
        GB = sb("GB", [P, 2, D])
        CH = sb("CH", [P, V_N, KT])
        arena = sb("arena", [P, 22528])
        ident = sb("ident", [P, P])
        repsum = sb("repsum", [P, P])
        iota = sb("iota", [P, SEQ])
        cst = sb("cst", [P, 2])
        ixs = sb("ixs", [P, RING], I32)
        nrm = sb("nrm", [P, 12])
        ps = ctx.enter_context(nc.psum_tensor("ps", [P, 8, BANK], F32))
        hn_flat = HN[:].rearrange("p a b -> p (a b)")

        def view(at, n, base=None):
            return (arena if base is None else base)[:, at:at + n]

        YT = view(0, KT * NT).rearrange("p (k n) -> p k n", k=KT)
        SSO = view(4608, 1024).rearrange("p (c q b) -> p c q b", c=2, q=S5_Q)
        S0 = view(5632, 1024).rearrange("p (c q b) -> p c q b", c=2, q=S5_Q)
        par = [view(6656 + 68 * n, 68) for n in range(24)]
        BC = view(8320, 1024).rearrange("p (h c n) -> p h c n", h=2, c=4)
        BX = view(9344, 256).rearrange("p (c n) -> p c n", c=2)
        BT = view(9600, 256).rearrange("p (c n) -> p c n", c=2)
        CN = view(9856, 256).rearrange("p (h n) -> p h n", h=2)
        DD = view(10112, 256).rearrange("p (h n) -> p h n", h=2)
        BS = view(10368, 512).rearrange("p (h c q b t) -> p h c q b t", h=2, c=2, q=QK, b=SB)
        BSF = view(10368, 512).rearrange("p (h c n) -> p h c n", h=2, c=2)
        SF = view(10880, 128).rearrange("p (c q) -> p c q", c=2)
        PT = view(11008, 512).rearrange("p (n m) -> p n m", n=4)
        UX = view(11520, QK * NT).rearrange("p (q n) -> p q n", q=QK)
        PRD = view(12672, 1024).rearrange("p (q t) -> p q t", q=QK)
        COS = view(13696, 2048).rearrange("p (h q t) -> p h q t", h=2, q=QK)
        SIN = view(15744, 2048).rearrange("p (h q t) -> p h q t", h=2, q=QK)
        M = [view(17792 + 1024 * n, 1024).rearrange("p (q t) -> p q t", q=QK) for n in range(4)]
        PR = [hn_flat[:, 1024 * n:1024 * (n + 1)].rearrange("p (q t) -> p q t", q=QK) for n in range(4)]
        PRY = hn_flat[:, 4096:5120].rearrange("p (q t) -> p q t", q=QK)
        vecs = view(21888, 192)
        SIG = view(17792, 4 * NT).rearrange("p (n m) -> p n m", n=4)
        OT0 = view(13056, KT * NT).rearrange("p (k n) -> p k n", k=KT)
        REP0 = view(18944, D)
        GT = view(0, KT * NT).rearrange("p (k n) -> p k n", k=KT)
        XC = view(4608, KT * NT).rearrange("p (k n) -> p k n", k=KT)
        XBP = view(9216, KT * (SEQ + 3)).rearrange("p (k n) -> p k n", k=KT)
        XBS = view(9216 + KT * (SEQ + 3), KT * SB * 7).rearrange("p (k b n) -> p k b n", k=KT, b=SB)
        TH = view(9216, KT * NT).rearrange("p (k n) -> p k n", k=KT)
        RA = view(14256, KT * NT).rearrange("p (k n) -> p k n", k=KT)
        IG = hn_flat[:, 0:KT * NT].rearrange("p (k n) -> p k n", k=KT)
        LIN = view(18864, 512)
        LCONV = view(18864, 384).rearrange("p (k b n) -> p k b n", k=KT, b=SB)
        LH0 = view(18864 + 384, 128).rearrange("p (k b) -> p k b", k=KT)
        LOUT = view(19376, 576)
        LT = view(19952, 128).rearrange("p (k b) -> p k b", k=KT)
        LS = [view(20080 + 16 * n, 16) for n in range(8)]
        LV = view(20208, KT // 2 * NT).rearrange("p (k n) -> p k n", k=KT // 2)
        OT1 = XC
        REP1 = view(14256, D)
        KEYS = view(EARLY * D, D)
        QT = view((EARLY + 1) * D, 4 * NT).rearrange("p (h s n) -> p h s n", h=2, s=2)
        REPQ = view((EARLY + 1) * D + 4 * NT, 4 * P).rearrange("p (h s n) -> p h s n", h=2, s=2)
        at = RING * D
        small = {}
        for name, n in (("TV", 6 * TOPK), ("TI", 6 * TOPK), ("TF", 12 * TOPK), ("C", TILES * CANDS),
                        ("LEFT", TILES * CANDS), ("BV", 3 * TOPK), ("BP", 3 * TOPK), ("AB", 6 * TOPK),
                        ("ABF", 12 * TOPK), ("OH", 2 * TILES * CANDS), ("II", 6 * TOPK), ("GS", 6 * HEADS)):
            small[name] = view(at, n)
            at += n
        assert at <= RING * D + 2 * D
        LEFT_OF = [view(21248 + CANDS * t, CANDS) for t in range(TILES)]
        GE = view(22032, TILES * PICKS)
        TV, TI, TF, C, LEFT = (small[n] for n in ("TV", "TI", "TF", "C", "LEFT"))
        BV, BP, AB, ABF, OH, II, GS = (small[n] for n in ("BV", "BP", "AB", "ABF", "OH", "II", "GS"))
        TI, BP, AB = (w.bitcast(U32) for w in (TI, BP, AB))
        TF, ABF = ([w[:, 6 * TOPK * n:6 * TOPK * (n + 1)] for n in range(2)] for w in (TF, ABF))
        cube = [P, TILES, TOPK, TOPK]
        ring = view(0, RING * D).rearrange("p (r d) -> p r d", r=RING)
        ACC = view(18432, D)
        GI = view(20480, 384).bitcast(I32)
        GG = view(20864, 384)
        AV = view(21248, 384)
        WG = view(21632, 384)
        A8 = view(22016, RING)

        x_in = [sem(f"x_in{t}") for t in range(TILES)]
        small_in = sem("small_in")
        s5_in = sem("s5_in")
        lru_in_sem = sem("lru_in_sem")
        gain_in = sem("gain_in")
        consts = sem("consts")
        slab_in = [sem(f"slab_in{r}") for r in range(WRING)]
        slab_done = sem("slab_done")
        bank_read = sem("bank_read")
        norm_sq, norm_v, norm_rt, norm_h = sem("norm_sq"), sem("norm_v"), sem("norm_rt"), sem("norm_h")
        norm_tp, norm_ht = sem("norm_tp"), sem("norm_ht")
        glu_out = sem("glu_out")
        mix_rep, mix_tp, mix_x = sem("mix_rep"), sem("mix_tp"), sem("mix_x")
        vstep, pstep, astep = sem("vstep"), sem("pstep"), sem("astep")
        s5_pa, s5_pv = sem("s5_pa"), sem("s5_pv")
        s5_b_in, s5_c_in = [sem("s5_b_in0"), sem("s5_b_in1")], [sem("s5_c_in0"), sem("s5_c_in1")]
        s5_bx, s5_bt, s5_btc, s5_ux = sem("s5_bx"), sem("s5_bt"), sem("s5_btc"), sem("s5_ux")
        s5_cn, s5_dd, s5_bu, s5_bur = sem("s5_cn"), sem("s5_dd"), sem("s5_bu"), sem("s5_bur")
        s5_bsc, s5_bsd, s5_prod, s5_f = sem("s5_bsc"), sem("s5_bsd"), sem("s5_prod"), sem("s5_f")
        s5_tab, s5_p, s5_y, s5_yg = sem("s5_tab"), sem("s5_p"), sem("s5_y"), sem("s5_yg")
        s5_sf, s5_zero, stores = sem("s5_sf"), sem("s5_zero"), sem("stores")
        y_stored, top_go, pool_go = sem("y_stored"), sem("top_go"), sem("pool_go")
        lru_pad, lru_xb, lru_xc, lru_st = sem("lru_pad"), sem("lru_xb"), sem("lru_xc"), sem("lru_st")
        gate_mm, gate_ev, lru_sp, lru_a = sem("gate_mm"), sem("gate_ev"), sem("lru_sp"), sem("lru_a")
        lru_th, lru_v, lru_rt, lru_y = sem("lru_th"), sem("lru_v"), sem("lru_rt"), sem("lru_y")
        lru_hs = sem("lru_hs")
        pos_set, pos_off, one_hot = sem("pos_set"), sem("pos_off"), sem("one_hot")
        picked, pick_read, experts_set = sem("picked"), sem("pick_read"), sem("experts_set")
        keys_in, key_mm, key_used = sem("keys_in"), sem("key_mm"), sem("key_used")
        soft_in, soft_exp, picks_ready = sem("soft_in"), sem("soft_exp"), sem("picks_ready")
        row_in = [sem(f"row_in{r}") for r in range(RING)]
        row_used, index_set, gather_go = sem("row_used"), sem("index_set"), sem("gather_go")
        dots_done, act_g, peer_acc, peer_sum, peer_x = sem("dots_done"), sem("act_g"), sem("peer_acc"), sem("peer_sum"), sem("peer_x")

        block = ctx.enter_context(nc.Block())

        @block.sync
        def _(sp):
            for t in range(TILES):
                sp.dma_start(X[:, t, :], x[t]).then_inc(x_in[t], 16)
            def s5_bc_tile(i, h, first):
                k = 2 * i + h
                for part, slot_in, used in ((0, s5_b_in, s5_bx), (1, s5_c_in, s5_y)):
                    if not first:
                        sp.wait_ge(used, k - 1)
                    sp.dma_start(BC[:, h, 2 * part:2 * part + 2, :].rearrange("p c n -> p (c n)"),
                                 s5_bc[bass.ds(k, 1), :, 2 * P * part:2 * P * (part + 1)].rearrange("a p n -> p (a n)")
                                 ).then_inc(slot_in[h], 16)

            for h in range(2):
                s5_bc_tile(0, h, True)
            for r in range(WRING):
                sp.dma_start(W[:, r, :], slabs[r]).then_inc(slab_in[r], 16)
            with sp.Fori(1, KT // 2) as i:
                for h in range(2):
                    s5_bc_tile(i, h, False)
            with sp.Fori(1, SLABS // WRING) as g:
                for r in range(WRING):
                    sp.wait_ge(slab_done, g * WRING + (r - WRING + 1))
                    sp.dma_start(W[:, r, :], slabs[bass.ds(g * WRING + r, 1)].rearrange("a p n -> p (a n)")).then_inc(slab_in[r], 16)
            for n in range(SLABS // WRING * WRING, SLABS):
                sp.wait_ge(slab_done, n - WRING + 1)
                sp.dma_start(W[:, n % WRING, :], slabs[n]).then_inc(slab_in[n % WRING], 16)
            for t in range(2):
                sp.wait_ge(norm_h, 12 + t + 1)
                sp.dma_start(y_out[t], HN[:, t, :]).then_inc(y_stored, 16)
            sp.wait_ge(norm_h, 15)
            sp.dma_start(ys_out, HN[0:NS, 2, :]).then_inc(y_stored, 16)
            sp.wait_ge(y_stored, 16 * 3)

        @block.gpsimd
        def _(pool):
            st = Steps()
            for n in range(2):
                pool.dma_start(GB[:, n, :], norms[n:n + 1, :].partition_broadcast(P)).then_inc(gain_in, 16)
            nc.gpsimd.memset(ident[:], 0.0).then_inc(pstep, 1)
            nc.gpsimd.memset(repsum[:], 0.0).then_inc(pstep, 1)
            nc.gpsimd.memset(cst[:, 0:1], PI / 2).then_inc(pstep, 1)
            nc.gpsimd.memset(cst[:, 1:2], ROUND).then_inc(pstep, 1)
            nc.gpsimd.iota(iota[:], [[1, SEQ]], base=0, channel_multiplier=0,
                           allow_small_or_imprecise_dtypes=True).then_inc(pstep, 1)
            for _ in range(4):
                st.next()
            pool.wait_ge(pstep, st.next())
            nc.gpsimd.affine_select(out=ident[:], in_=ident[:], compare_op=ALU.not_equal, fill=1.0, base=0,
                                    pattern=[[-1, P]], channel_multiplier=1).then_inc(consts, 1)
            for c in range(-COPIES + 1, COPIES):
                nc.gpsimd.affine_select(out=repsum[:], in_=repsum[:], compare_op=ALU.not_equal, fill=1.0,
                                        base=-NS * c, pattern=[[-1, P]], channel_multiplier=1).then_inc(pstep, 1)
                pool.wait_ge(pstep, st.next())
            pool.sem_inc(consts, 1)

            abr, abi, fr, fi = par[0], par[1], par[2], par[3]

            def diagonal(i, h):
                nc.gpsimd.tensor_tensor(DD[:, h, :], ident[:], CH[:, V_D, bass.ds(2 * i + h, 1)].to_broadcast([P, P]),
                                        ALU.mult).then_inc(s5_dd, 1)

            def discrete_b(i, h, first):
                k = 2 * i + h
                pool.wait_ge(s5_b_in[h], (i + 1) * 16)
                pool.sem_inc(pool_go, 1)
                b = [BC[:, h, c, :].rearrange("p (q n) -> p q n", q=QK) for c in range(2)]
                f = [w[:, bass.ds(k * QK, QK)].unsqueeze(2).to_broadcast([P, QK, QC]) for w in (fr, fi)]
                t = [PT[:, n, :].rearrange("p (q n) -> p q n", q=QK) for n in range(4)]
                for n, (c, e) in enumerate([(0, 0), (1, 1), (0, 1), (1, 0)]):
                    ins = nc.gpsimd.tensor_tensor(t[n], b[c], f[e], ALU.mult)
                ins.then_inc(pstep, 1)
                pool.wait_ge(pstep, st.next())
                if not first:
                    pool.wait_ge(s5_bt, k)
                nc.gpsimd.tensor_tensor(BX[:, 0, :], PT[:, 0, :], PT[:, 1, :], ALU.subtract)
                nc.gpsimd.tensor_tensor(BX[:, 1, :], PT[:, 2, :], PT[:, 3, :], ALU.add).then_inc(s5_bx, 1)
                pool.wait_ge(s5_bx, k + 1)

            def sample_states(i, h):
                k = 2 * i + h
                pool.wait_ge(s5_bsc, k + 1)
                pool.sem_inc(pool_go, 1)
                a = [w[:, bass.ds(k * QK, QK)].unsqueeze(2).to_broadcast([P, QK, SB]) for w in (abr, abi)]
                s = [S0[:, c, bass.ds(k * QK, QK), :] for c in range(2)]
                t = [PT[:, n, 0:QK * SB].rearrange("p (q b) -> p q b", q=QK) for n in range(4)]
                for step in range(ST):
                    for n, (c, e) in enumerate([(0, 0), (1, 1), (0, 1), (1, 0)]):
                        ins = nc.gpsimd.tensor_tensor(t[n], a[c], s[e], ALU.mult)
                    ins.then_inc(pstep, 1)
                    pool.wait_ge(pstep, st.next())
                    nc.gpsimd.tensor_tensor(t[0], t[0], t[1], ALU.subtract)
                    nc.gpsimd.tensor_tensor(t[2], t[2], t[3], ALU.add).then_inc(pstep, 1)
                    pool.wait_ge(pstep, st.next())
                    s = [BS[:, h, c, :, :, step] for c in range(2)]
                    nc.gpsimd.tensor_tensor(s[0], s[0], t[0], ALU.add)
                    ins = nc.gpsimd.tensor_tensor(s[1], s[1], t[2], ALU.add)
                    if step < ST - 1:
                        ins.then_inc(pstep, 1)
                        pool.wait_ge(pstep, st.next())
                        pool.sem_inc(pool_go, 1)
                ins.then_inc(s5_bsd, 1)
                pool.wait_ge(s5_bsd, k + 1)
                pool.sem_inc(pool_go, 1)
                for c in range(2):
                    ins = nc.gpsimd.tensor_copy(SSO[:, c, bass.ds(k * QK, QK), :], s[c])
                ins.then_inc(pstep, 1)
                pool.wait_ge(pstep, st.next())

            def s5_tile(i, h, first=False, last=False):
                nxt = (i, 1) if h == 0 else (i + 1, 0)
                if not last:
                    discrete_b(*nxt, False)
                sample_states(i, h)
                if not last:
                    if not first:
                        pool.wait_ge(s5_y, 2 * i + h)
                        pool.sem_inc(pool_go, 1)
                    diagonal(*nxt)

            pool.wait_ge(small_in, 16)
            pool.wait_ge(s5_pv, 3)
            diagonal(0, 0)
            discrete_b(0, 0, True)
            per_tile = 1 + 3 * ST
            s5_tile(0, 0, True)
            s5_tile(0, 1)
            with pool.Fori(1, KT // 2 - 1) as i:
                st.enter(i - 1, 2 * per_tile)
                s5_tile(i, 0)
                s5_tile(i, 1)
            st.leave(KT // 2 - 2)
            s5_tile(KT // 2 - 1, 0)
            s5_tile(KT // 2 - 1, 1, last=True)
            pool.dma_start(s5s_out, SSO[:].rearrange("p c q b -> p (c q b)")).then_inc(stores, 16)
            pool.wait_ge(s5_sf, 1)
            pool.dma_start(s5p_out, SF[:].rearrange("p c q -> p (c q)")).then_inc(stores, 16)
            pool.wait_ge(stores, 32)
            pool.sem_inc(s5_zero, 1)
            pool.wait_ge(mix_x, 12)
            pool.dma_start(KEYS, keys[0]).then_inc(keys_in, 16)

            def gather(table, base, i, r):
                pool.wait_ge(row_used, i * RING + (base * RING + r + 1))
                nc.gpsimd.tensor_copy(ixs[:, r:r + 1], GI[:, bass.ds(i * RING + r, 1)]).then_inc(index_set, 1)
                pool.wait_ge(index_set, i * RING + (base * RING + r + 1))
                pool.sem_inc(gather_go, 1)
                pool.indirect_dma_start(ring[:, r, :], None, table,
                                        bass.IndirectOffsetOnAxis(ap=ixs[:, r:r + 1], axis=0)).then_inc(row_in[r], 16)

            def index_parts(layer):
                oh = [OH[:, TILES * CANDS * s:TILES * CANDS * (s + 1)] for s in range(2)]

                def one_head(h, par):
                    pool.wait_ge(pos_set, h + (HEADS * layer + 1))
                    pool.wait_ge(pick_read, h + (HEADS * layer + 1))
                    for s in range(2):
                        part = ABF[par][:, 3 * TOPK * s:3 * TOPK * (s + 1)]
                        ins = nc.gpsimd.tensor_tensor(oh[s].rearrange("p (a b) -> p a b", b=TOPK),
                                                      part.unsqueeze(2).to_broadcast([P, 3 * TOPK, TOPK]),
                                                      iota[:, 0:TOPK].unsqueeze(1).to_broadcast([P, 3 * TOPK, TOPK]),
                                                      ALU.subtract)
                    ins.then_inc(pos_off, 1)
                    pool.wait_ge(one_hot, h + (HEADS * layer + 1))
                    tf4 = TF[par].rearrange("p (t s k) -> p t s k", t=TILES, s=2)
                    for s in range(2):
                        cells = oh[s].rearrange("p (t a b) -> p t a b", t=TILES, a=TOPK)
                        ins = nc.gpsimd.tensor_tensor(cells, cells, tf4[:, :, s, :].unsqueeze(2).to_broadcast(cube), ALU.mult)
                    ins.then_inc(picked, 1)

                one_head(0, 0)
                one_head(1, 1)
                pool.wait_ge(experts_set, HEADS * layer + 1)
                for r in range(EARLY):
                    gather(experts_u[layer], 2 * layer * ROUNDS, 0, r)
                with pool.Fori(1, HEADS // 2 - 1) as i:
                    one_head(i * 2, 0)
                    one_head(i * 2 + 1, 1)
                pool.wait_ge(key_mm, HEADS * (layer + 1))
                for r in range(EARLY, RING):
                    gather(experts_u[layer], 2 * layer * ROUNDS, 0, r)
                one_head(HEADS - 2, 0)
                one_head(HEADS - 1, 1)

            def gathers(layer):
                for n in ((2, 3) if layer == 0 else (4,)):
                    pool.wait_ge(norm_h, 3 * (n - 1))
                    pool.dma_start(GB[:, n % 2, :], norms[n:n + 1, :].partition_broadcast(P)).then_inc(gain_in, 16)
                index_parts(layer)
                base = 2 * layer * ROUNDS
                last = (HEADS - 1) * TOPK // RING
                pool.wait_ge(experts_set, HEADS * layer + HEADS - 1)
                with pool.Fori(1, last) as i:
                    for r in range(RING):
                        gather(experts_u[layer], base, i, r)
                pool.wait_ge(picks_ready, layer + 1)
                with pool.Fori(last, ROUNDS) as i:
                    for r in range(RING):
                        gather(experts_u[layer], base, i, r)
                with pool.Fori(0, ROUNDS) as i:
                    for r in range(RING):
                        gather(experts_v[layer], base + ROUNDS, i, r)

            gathers(0)
            pool.wait_ge(peer_x, 1)
            pool.dma_start(LIN, lru_in).then_inc(lru_in_sem, 16)
            nc.gpsimd.memset(XBP[:, :, 0:3], 0.0).then_inc(lru_pad, 1)
            pool.wait_ge(lru_in_sem, 16)
            nc.gpsimd.tensor_copy(XBS[:, :, :, 0:3], LCONV).then_inc(lru_pad, 1)
            pool.wait_ge(lru_hs, 1)
            pool.dma_start(lru_out, LOUT).then_inc(stores, 16)
            pool.wait_ge(stores, 48)
            pool.sem_inc(s5_zero, 1)
            pool.wait_ge(mix_x, 24)
            pool.dma_start(KEYS, keys[1]).then_inc(keys_in, 16)
            gathers(1)

        @block.tensor
        def _(pe):
            def norm_transposes(j):
                for t in range(TILES):
                    pe.wait_ge(norm_h, 3 * j + t + 1)
                    rows = P if t < 2 else NS
                    for g in range(GROUP):
                        n = 12 * j + 4 * t + g
                        if n >= 2:
                            pe.wait_ge(norm_ht, n - 1)
                        for e in range(4):
                            k = 4 * g + e
                            mm = nc.tensor.transpose(ps[:, 2 + n % 2, rows * e:rows * (e + 1)],
                                                     HN[0:rows, t, P * k:P * (k + 1)], ident[0:rows, 0:rows])
                        mm.then_inc(norm_tp, 1)

            def product(slab, n0, groups, rhs):
                with pe.Fori(0, groups) as g:
                    for r in range(GROUP):
                        slot = (slab + r) % WRING
                        pe.wait_ge(slab_in[slot], g * 16 + 16 * ((slab + r) // WRING + 1))
                        pe.wait_ge(bank_read, g * GROUP + (n0 + r + 1))
                        for k in range(KT):
                            mm = nc.tensor.matmul(ps[:, r % 2, 0:NT], W[:, slot, P * k:P * (k + 1)], rhs[:, k, :],
                                                  start=(k == 0), stop=(k == KT - 1))
                        mm.then_inc(slab_done, 1)

            def mixer_out(o, src, rep):
                for t in range(TILES):
                    if t == 2:
                        pe.wait_ge(mix_rep, o + 1)
                    for g in range(GROUP):
                        n = 12 * o + 4 * t + g
                        if n >= 2:
                            pe.wait_ge(mix_x, n - 1)
                        for e in range(4):
                            k = 4 * g + e
                            part = src[:, k, t * P:(t + 1) * P] if t < 2 else rep[:, P * k:P * (k + 1)]
                            mm = nc.tensor.transpose(ps[:, 4 + n % 2, P * e:P * (e + 1)], part, ident[:])
                        mm.then_inc(mix_tp, 1)

            def queries(slab, n0, layer):
                def scores(h, par):
                    pe.wait_ge(bank_read, h * 2 + (n0 + 4))
                    pe.wait_ge(key_used, h + (8 * layer + 1))
                    for t in range(TILES):
                        for e in range(2):
                            q = QT[:, par, e, t * P:(t + 1) * P] if t < 2 else REPQ[:, par, e, :]
                            at = 256 * (t % 2) + P * e
                            mm = nc.tensor.matmul(ps[:, 4 + 2 * par + t // 2, at:at + P], q,
                                                  KEYS[:, bass.ds(h * 256 + P * e, P)], start=True, stop=True)
                    mm.then_inc(key_mm, 1)

                def slab_product(g, r):
                    slot = (slab + r) % WRING
                    pe.wait_ge(slab_in[slot], g * 16 + 16 * ((slab + r) // WRING + 1))
                    pe.wait_ge(bank_read, g * GROUP + (n0 + r + 1))
                    for k in range(KT):
                        mm = nc.tensor.matmul(ps[:, r % 2, 0:NT], W[:, slot, P * k:P * (k + 1)], HT[:, k, :],
                                              start=(k == 0), stop=(k == KT - 1))
                    mm.then_inc(slab_done, 1)

                pe.wait_ge(keys_in, 16 * (layer + 1))
                for r in range(GROUP):
                    slab_product(0, r)
                    if r == 2:
                        scores(0, 0)
                with pe.Fori(1, 4) as g:
                    slab_product(g, 0)
                    scores(g * 2 - 1, 1)
                    slab_product(g, 1)
                    slab_product(g, 2)
                    scores(g * 2, 0)
                    slab_product(g, 3)
                scores(HEADS - 1, 1)

            def sample_sum(layer):
                pe.wait_ge(peer_acc, layer + 1)
                for c in range(4):
                    mm = nc.tensor.matmul(ps[:, 4 + c, :], repsum[:], ACC[:, BANK * c:BANK * (c + 1)], start=True, stop=True)
                mm.then_inc(peer_sum, 1)

            pe.wait_ge(consts, 2)
            norm_transposes(0)

            def s5_in_part(i, h, first):
                k = 2 * i + h
                pe.wait_ge(s5_bx, k + 1)
                pe.wait_ge(s5_btc, k)
                for c in range(2):
                    mm = nc.tensor.transpose(ps[:, 4, P * c:P * (c + 1)], BX[:, c, :], ident[:])
                mm.then_inc(s5_bt, 1)
                pe.wait_ge(s5_btc, k + 1)
                pe.wait_ge(s5_ux, k + 1)
                pe.wait_ge(s5_bur, k)
                pe.wait_ge(s5_bsc, k)
                for c in range(2):
                    for e in range(2):
                        nc.tensor.matmul(ps[:, 2 * c + e, :], BT[:, c, :], UX[:, 2 * e:2 * e + 2, 0:SEQ],
                                         start=True, stop=True)
                    mm = nc.tensor.matmul(ps[:, 6, P * c:P * (c + 1)], BT[:, c, :], UX[:, :, SEQ:NT],
                                          start=True, stop=True)
                mm.then_inc(s5_bu, 1)

            def s5_out_part(k, h):
                pe.wait_ge(s5_dd, k + 1)
                pe.wait_ge(s5_cn, k + 1)
                pe.wait_ge(s5_p, k + 1)
                pe.wait_ge(s5_bsd, k + 1)
                pe.wait_ge(s5_yg, k)
                nc.tensor.matmul(ps[:, 5, 0:SEQ], DD[:, h, :], HT[:, bass.ds(k, 1), 0:SEQ].rearrange("p a n -> p (a n)"),
                                 start=True, stop=False, skip_group_check=True)
                nc.tensor.matmul(ps[:, 7, 0:NS], DD[:, h, :], HT[:, bass.ds(k, 1), SEQ:NT].rearrange("p a n -> p (a n)"),
                                 start=True, stop=False, skip_group_check=True)
                for q in range(QK):
                    rows = slice(QC * q, QC * (q + 1))
                    cr, ci = BC[:, h, 2, rows], CN[:, h, rows]
                    for n, c in enumerate((cr, cr, ci, ci)):
                        nc.tensor.matmul(ps[rows, 5, 0:SEQ], c, PR[n][:, q, :], start=False, stop=(n == 3), skip_group_check=True)
                    for n, c in enumerate((cr, ci)):
                        mm = nc.tensor.matmul(ps[rows, 7, 0:NS], c, BSF[:, h, n, NS * q:NS * (q + 1)], start=False,
                                              stop=(n == 1), skip_group_check=True)
                mm.then_inc(s5_y, 1)

            s5_in_part(0, 0, True)
            s5_in_part(0, 1, True)
            s5_out_part(0, 0)
            with pe.Fori(1, KT // 2) as i:
                for h in range(2):
                    s5_in_part(i, h, False)
                    s5_out_part(2 * i + (h - 1), 1 - h)
            s5_out_part(KT - 1, 1)

            pe.wait_ge(s5_yg, KT)
            product(SLAB_GLU, 0, 4, YT)
            pe.wait_ge(glu_out, GROUP + 16)
            mixer_out(0, OT0, REP0)
            norm_transposes(1)
            pe.wait_ge(norm_ht, 24)
            queries(SLAB_Q0, 16, 0)
            sample_sum(0)

            norm_transposes(2)
            pe.wait_ge(norm_ht, 36)
            product(SLAB_XB, 32, 4, HT)
            pe.wait_ge(lru_xc, 1)
            pe.wait_ge(bank_read, 48 + 2)
            for s in range(4):
                slot = (SLAB_GATE + s) % WRING
                pe.wait_ge(slab_in[slot], 16 * ((SLAB_GATE + s) // WRING + 1))
                for b in range(8):
                    n = 8 * s + b
                    head = 2 * s + b // 4
                    if n >= 2:
                        pe.wait_ge(gate_ev, n - 1)
                    for e in range(2):
                        at = P * (2 * b + e)
                        mm = nc.tensor.matmul(ps[:, n % 2, 0:NT], W[:, slot, at:at + P], XC[:, 2 * head + e, :],
                                              start=(e == 0), stop=(e == 1))
                    mm.then_inc(gate_mm, 1)
                pe.drain().then_inc(slab_done, 1)
            pe.wait_ge(gate_ev, 32)
            product(SLAB_IN, 48, 4, HT)
            pe.wait_ge(lru_y, 1)
            product(SLAB_OUT, 64, 4, GT)
            pe.wait_ge(bank_read, 80 + 2)
            mixer_out(1, OT1, REP1)
            norm_transposes(3)
            pe.wait_ge(norm_ht, 48)
            queries(SLAB_Q1, 80, 1)
            sample_sum(1)

        @block.scalar
        def _(act):
            act.dma_start(CH[:].rearrange("p v k -> p (v k)"), chan).then_inc(small_in, 16)
            act.dma_start(vecs, s5_vec).then_inc(s5_in, 16)
            act.dma_start(S0[:].rearrange("p c q b -> p (c q b)"), s5_h0).then_inc(s5_in, 16)
            act.sem_inc(bank_read, 2)
            A = nc.scalar.activation
            ast = Steps()

            def norm_tile(j, t):
                layer = j // 2 - 1
                if j == 0:
                    act.wait_ge(x_in[t], 16)
                elif j % 2:
                    act.wait_ge(mix_x, 12 * (j // 2) + 4 * (t + 1))
                elif t < 2:
                    act.wait_ge(row_used, RING * ((2 * layer + 1) * ROUNDS + ROUND_AT[t + 1]) + RING)
                else:
                    act.wait_ge(peer_x, layer + 1)
                A(HN[:, t, :], X[:, t, :], ACT.Square, accum_out=nrm[:, t:t + 1]).then_inc(norm_sq, 1)
                act.wait_ge(norm_v, 6 * j + 2 * t + 1)
                A(nrm[:, 6 + t:7 + t], nrm[:, 3 + t:4 + t], ACT.Sqrt).then_inc(norm_rt, 1)

            def norm_rows(j, t):
                w = P if t < 2 else NS
                for g in range(GROUP):
                    n = 12 * j + 4 * t + g
                    act.wait_ge(norm_tp, n + 1)
                    A(HT[:, 4 * g:4 * g + 4, token_cols(t)],
                      ps[:, 2 + n % 2, 0:4 * w].rearrange("p (k n) -> p k n", k=4), ACT.Copy).then_inc(norm_ht, 1)

            def norm(j):
                norm_tile(j, 0)
                norm_tile(j, 1)
                norm_rows(j, 0)
                if j % 2:
                    norm_tile(j, 2)
                    norm_rows(j, 1)
                else:
                    norm_rows(j, 1)
                    norm_tile(j, 2)
                norm_rows(j, 2)

            def replicate(rep, src):
                return A(rep.rearrange("p (k r n) -> p k r n", k=KT, r=COPIES),
                         src[:, :, SEQ:NT].unsqueeze(2).to_broadcast([P, KT, COPIES, NS]), ACT.Copy)

            def out_rows(o, src, rep):
                replicate(rep, src).then_inc(mix_rep, 1)

            for t in range(TILES):
                norm_tile(0, t)
            lr, li, dt = vecs[:, 0:64], vecs[:, 64:128], vecs[:, 128:192]
            dte, tnh, s1, c1, sh, tmp = (par[n][:, 0:64] for n in (4, 5, 6, 7, 8, 9))
            phi, half = par[10], par[11][:, 0:64]
            lrdt = par[12][:, 0:64]
            act.wait_ge(s5_in, 32)
            A(dte, dt, ACT.Exp).then_inc(s5_pa, 1)
            act.wait_ge(s5_pv, 1)
            A(tnh, lrdt, ACT.Tanh, scale=0.5).then_inc(s5_pa, 1)
            act.wait_ge(consts, 2)
            act.wait_ge(s5_pv, 2)
            A(s1, phi[:, 0:64], ACT.Sin, scale=TWO_PI_LOW).then_inc(s5_pa, 1)
            A(sh, phi[:, 0:64], ACT.Sin, scale=TWO_PI_LOW / 2).then_inc(s5_pa, 1)
            A(tmp, phi[:, 0:64], ACT.Abs).then_inc(s5_pa, 1)
            act.wait_ge(s5_pa, 5)
            A(c1, tmp, ACT.Sin, scale=-TWO_PI_LOW, bias=cst[:, 0:1]).then_inc(s5_pa, 1)
            for t in range(TILES):
                norm_rows(0, t)
            act.wait_ge(norm_ht, 12)

            def turns(k1):
                for q in range(QK):
                    A(PRD[:, q, :], iota[:], ACT.Copy, scale=phi[:, bass.ds(k1 * QK + q, 1)])
                    ins = A(PRY[:, q, :], iota[:], ACT.Identity, scale=phi[:, bass.ds(k1 * QK + q, 1)], bias=cst[:, 1:2])
                ins.then_inc(s5_prod, 1)

            def tables(k1, slot):
                act.wait_ge(s5_f, k1 + 1)
                A(SIN[:, slot], PRD, ACT.Sin, scale=-TWO_PI_LOW).then_inc(astep, 1)
                act.wait_ge(astep, ast.next())
                A(PRD, PRD, ACT.Abs).then_inc(astep, 1)
                act.wait_ge(astep, ast.next())
                A(COS[:, slot], PRD, ACT.Sin, scale=-TWO_PI_LOW, bias=cst[:, 0:1]).then_inc(s5_tab, 1)

            def gelu_y(k):
                act.wait_ge(s5_y, k + 1)
                A(YT[:, bass.ds(k, 1), 0:SEQ].rearrange("p a n -> p (a n)"), ps[:, 5, 0:SEQ], ACT.Gelu)
                A(YT[:, bass.ds(k, 1), SEQ:NT].rearrange("p a n -> p (a n)"), ps[:, 7, 0:NS], ACT.Gelu).then_inc(s5_yg, 1)

            def spread_u(k):
                for q in range(QK):
                    rows = slice(QC * q, QC * (q + 1))
                    ins = A(UX[rows, q, :], HT[rows, bass.ds(k, 1), :].rearrange("p a n -> p (a n)"), ACT.Copy)
                ins.then_inc(s5_ux, 1)

            def negative_c(i, h):
                act.wait_ge(s5_c_in[h], (i + 1) * 16)
                A(CN[:, h, :], BC[:, h, 3, :], ACT.Copy, scale=-1.0).then_inc(s5_cn, 1)

            def s5_tile(i, h, first=False, last=False, reuse=True):
                k = 2 * i + h
                if not first:
                    act.wait_ge(s5_bu, k)
                act.wait_ge(s5_bt, k + 1)
                A(BT[:].rearrange("p c n -> p (c n)"), ps[:, 4, 0:2 * P], ACT.Copy).then_inc(s5_btc, 1)
                if not last:
                    if not first:
                        act.wait_ge(s5_p, k)
                    tables(k + 1, 1 - h)
                act.wait_ge(s5_bu, k + 1)
                if reuse:
                    act.wait_ge(s5_y, k - 1)
                A(BSF[:, h, :, :], ps[:, 6, 0:2 * P].rearrange("p (c n) -> p c n", c=2), ACT.Copy).then_inc(s5_bsc, 1)
                if not last:
                    spread_u(k + 1)
                    act.wait_ge(s5_tab, k + 2)
                    turns(k + 2)
                if not first:
                    gelu_y(k - 1)
                if not last:
                    negative_c(*((i, 1) if h == 0 else (i + 1, 0)))

            act.wait_ge(s5_pv, 3)
            turns(0)
            spread_u(0)
            negative_c(0, 0)
            tables(0, 0)
            act.wait_ge(s5_tab, 1)
            turns(1)
            s5_tile(0, 0, first=True, reuse=False)
            s5_tile(0, 1, reuse=False)
            with act.Fori(1, KT // 2 - 1) as i:
                ast.enter(i - 1, 4)
                s5_tile(i, 0)
                s5_tile(i, 1)
            ast.leave(KT // 2 - 2)
            s5_tile(KT // 2 - 1, 0)
            s5_tile(KT // 2 - 1, 1, last=True)
            gelu_y(KT - 1)

            with act.Fori(0, 4) as g:
                for r in range(GROUP):
                    act.wait_ge(slab_done, g * GROUP + (SLAB_GLU + r + 1))
                    act.wait_ge(glu_out, g * GROUP + (r + 1))
                    A(SIG[:, r, :], ps[:, r % 2, 0:NT], ACT.Sigmoid,
                      bias=CH[:, V_BGLU, bass.ds(g * GROUP + r, 1)]).then_inc(bank_read, 1)
            act.wait_ge(glu_out, GROUP + 16)
            out_rows(0, OT0, REP0)
            norm(1)

            def evacuate(slab, groups, dst):
                with act.Fori(0, groups) as g:
                    for r in range(GROUP):
                        act.wait_ge(slab_done, g * GROUP + (slab + r + 1))
                        A(dst[:, bass.ds(g * GROUP + r, 1), :].rearrange("p a n -> p (a n)"), ps[:, r % 2, 0:NT],
                          ACT.Copy).then_inc(bank_read, 1)

            def peer(layer):
                act.wait_ge(s5_zero, layer + 1)
                slab = (SLAB_Q0, SLAB_Q1)[layer]

                def head_queries(g, par):
                    for e in range(2):
                        r = 2 * par + e
                        act.wait_ge(slab_done, g * GROUP + (slab + r + 1))
                        A(QT[:, par, e, :], ps[:, e, 0:NT], ACT.Copy)
                        A(REPQ[:, par, e, :].rearrange("p (r n) -> p r n", r=COPIES),
                          ps[:, e, SEQ:NT].unsqueeze(1).to_broadcast([P, COPIES, NS]), ACT.Copy).then_inc(bank_read, 1)

                def marks(h):
                    act.wait_ge(pos_off, h + (HEADS * layer + 1))
                    A(OH, OH, ACT.Abs).then_inc(astep, 1)
                    act.wait_ge(astep, ast.next())
                    A(OH, OH, ACT.Relu, scale=-1.0, bias=1.0).then_inc(one_hot, 1)

                for par in range(2):
                    head_queries(0, par)
                for par in range(2):
                    head_queries(1, par)
                marks(0)
                with act.Fori(2, HEADS // 2) as g:
                    ast.enter(g - 2, 2)
                    for par in range(2):
                        head_queries(g, par)
                        marks(g * 2 + (par - 3))
                ast.leave(HEADS // 2 - 2)
                for h in range(HEADS - 3, HEADS):
                    marks(h)
                act.wait_ge(soft_in, layer + 1)
                A(GE, GE, ACT.Exp).then_inc(soft_exp, 1)
                act.wait_ge(dots_done, layer + 1)
                A(WG[:, 0:COLS], AV[:, 0:COLS], ACT.Gelu).then_inc(act_g, 1)

            peer(0)
            norm(2)
            lam = CH[:, V_LAM, :]
            A(LS[0], lam, ACT.Abs).then_inc(lru_sp, 1)
            act.wait_ge(lru_sp, 1)
            A(LS[1], LS[0], ACT.Exp, scale=-1.0).then_inc(lru_sp, 1)
            act.wait_ge(lru_sp, 3)
            A(LS[3], LS[2], ACT.Ln).then_inc(lru_sp, 1)
            act.wait_ge(lru_pad, 2)
            with act.Fori(0, 4) as g:
                for r in range(GROUP):
                    act.wait_ge(slab_done, g * GROUP + (SLAB_XB + r + 1))
                    A(XBP[:, bass.ds(g * GROUP + r, 1), 3:].rearrange("p a n -> p (a n)"), ps[:, r % 2, 0:SEQ], ACT.Copy)
                    A(XBS[:, bass.ds(g * GROUP + r, 1), :, 3:].rearrange("p a b n -> p (a b) n"),
                      ps[:, r % 2, SEQ:NT].rearrange("p (b n) -> p b n", b=SB), ACT.Copy).then_inc(bank_read, 1)
            for s in range(4):
                for b in range(8):
                    n = 8 * s + b
                    head, gate, jt = 2 * s + b // 4, b // 2 % 2, b % 2
                    ch = 2 * head + jt
                    act.wait_ge(gate_mm, n + 1)
                    A((RA, IG)[gate][:, ch, :], ps[:, n % 2, 0:NT], ACT.Sigmoid,
                      bias=CH[:, (V_BA, V_BI)[gate], ch:ch + 1]).then_inc(gate_ev, 1)
            act.wait_ge(lru_sp, 5)
            act.wait_ge(gate_ev, 32)
            act.wait_ge(lru_st, 1)
            for k in range(KT):
                ins = A(TH[:, k, :], RA[:, k, :], ACT.Tanh, scale=LS[5][:, k:k + 1])
            ins.then_inc(lru_th, 1)

            def gate_columns(first):
                with act.Fori(first, first + 2) as g:
                    for r in range(GROUP):
                        act.wait_ge(slab_done, g * GROUP + (SLAB_IN + r + 1))
                        A(GT[:, bass.ds(g * GROUP + r, 1), :].rearrange("p a n -> p (a n)"), ps[:, r % 2, 0:NT],
                          ACT.Gelu).then_inc(bank_read, 1)

            for k in range(KT):
                ins = A(RA[:, k, :], RA[:, k, :], ACT.Exp, scale=LS[6][:, k:k + 1])
            ins.then_inc(lru_a, 1)
            gate_columns(0)
            act.wait_ge(lru_v, 1)
            A(TH, TH, ACT.Sqrt).then_inc(lru_rt, 1)
            gate_columns(2)
            evacuate(SLAB_OUT, 4, OT1)
            act.wait_ge(bank_read, 82)
            out_rows(1, OT1, REP1)
            norm(3)
            peer(1)
            for t in range(TILES):
                norm_tile(4, t)

        @block.vector
        def _(dve):
            V = nc.vector
            st = Steps()
            dve.sem_inc(row_used, RING)
            dve.sem_inc(key_used, 2)
            dve.sem_inc(pick_read, 1)
            dve.sem_inc(glu_out, GROUP)

            def settle(ins):
                ins.then_inc(vstep, 1)
                dve.wait_ge(vstep, st.next())

            def settle_all(ins):
                settle(ins)
                dve.sem_inc(top_go, 1)

            def norm_tile(j, t):
                dve.wait_ge(norm_sq, 3 * j + t + 1)
                V.tensor_scalar(nrm[:, 3 + t:4 + t], nrm[:, t:t + 1], 1.0 / D, EPS, ALU.mult, ALU.add).then_inc(norm_v, 1)
                dve.wait_ge(norm_rt, 3 * j + t + 1)
                V.reciprocal(nrm[:, 9 + t:10 + t], nrm[:, 6 + t:7 + t]).then_inc(norm_v, 1)
                dve.wait_ge(norm_v, 6 * j + 2 * t + 2)
                if t == 0:
                    dve.wait_ge(gain_in, (32, 32, 64, 64, 80)[j])
                V.scalar_tensor_tensor(HN[:, t, :], X[:, t, :], nrm[:, 9 + t:10 + t], GB[:, j % 2, :],
                                       ALU.mult, ALU.mult).then_inc(norm_h, 1)

            def add_mixer(o, t):
                for g in range(GROUP):
                    n = 12 * o + 4 * t + g
                    dve.wait_ge(mix_tp, n + 1)
                    cols = slice(BANK * g, BANK * (g + 1))
                    V.tensor_tensor(X[:, t, cols], ps[:, 4 + n % 2, :], X[:, t, cols], ALU.add).then_inc(mix_x, 1)

            def add_and_norm(o):
                add_mixer(o, 0)
                add_mixer(o, 1)
                dve.wait_ge(mix_x, 12 * o + 8)
                norm_tile(2 * o + 1, 0)
                add_mixer(o, 2)
                norm_tile(2 * o + 1, 1)
                dve.wait_ge(mix_x, 12 * o + 12)
                norm_tile(2 * o + 1, 2)

            for t in range(TILES):
                norm_tile(0, t)
            lr, li = vecs[:, 0:64], vecs[:, 64:128]
            abr, abi, fr, fi = (par[n][:, 0:64] for n in range(4))
            dte, tnh, s1, c1, sh = (par[n][:, 0:64] for n in (4, 5, 6, 7, 8))
            phi, lrdt = par[10], par[12][:, 0:64]
            e1, den, nr, t1, t2, dec, trn, t3 = (par[n][:, 0:64] for n in range(13, 21))
            V.memset(UX, 0.0)
            V.memset(phi, 0.0).then_inc(vstep, 1)
            st.next()
            dve.wait_ge(s5_pa, 1)
            V.tensor_tensor(lrdt, lr, dte, ALU.mult).then_inc(s5_pv, 1)
            settle(V.tensor_tensor(trn, li, dte, ALU.mult))
            settle(V.tensor_scalar(trn, trn, 1.0 / (2 * PI), None, ALU.mult))
            settle(V.tensor_scalar(t1, trn, ROUND, ROUND, ALU.add, ALU.subtract))
            V.tensor_tensor(phi[:, 0:64], trn, t1, ALU.subtract).then_inc(s5_pv, 1)
            V.tensor_tensor(t3, lr, lr, ALU.mult)
            settle(V.tensor_tensor(t2, li, li, ALU.mult))
            settle(V.tensor_tensor(den, t3, t2, ALU.add))
            V.reciprocal(den, den)
            dve.wait_ge(s5_pa, 2)
            settle(V.tensor_scalar(t1, tnh, -1.0, 1.0, ALU.mult, ALU.add))
            settle(V.reciprocal(t1, t1))
            settle(V.scalar_tensor_tensor(e1, tnh, 2.0, t1, ALU.mult, ALU.mult))
            settle(V.tensor_scalar(dec, e1, 1.0, None, ALU.add))
            dve.wait_ge(s5_pa, 6)
            V.tensor_tensor(abr, dec, c1, ALU.mult)
            V.tensor_tensor(abi, dec, s1, ALU.mult)
            V.scalar_tensor_tensor(t1, sh, -2.0, sh, ALU.mult, ALU.mult)
            settle(V.tensor_tensor(nr, e1, c1, ALU.mult))
            settle(V.tensor_tensor(nr, nr, t1, ALU.add))
            V.tensor_tensor(fr, nr, lr, ALU.mult)
            V.tensor_tensor(t1, abi, li, ALU.mult)
            V.tensor_tensor(fi, abi, lr, ALU.mult)
            settle(V.tensor_tensor(t2, nr, li, ALU.mult))
            V.tensor_tensor(fr, fr, t1, ALU.add)
            settle(V.tensor_tensor(fi, fi, t2, ALU.subtract))
            V.tensor_tensor(fr, fr, den, ALU.mult)
            V.tensor_tensor(fi, fi, den, ALU.mult).then_inc(s5_pv, 1)

            def fractions(k1):
                dve.wait_ge(s5_prod, k1 + 1)
                V.scalar_tensor_tensor(PRD, PRY, ROUND, PRD, ALU.subtract, ALU.subtract).then_inc(s5_f, 1)

            def s5_tile(i, h, first=False, last=False):
                k = 2 * i + h
                if not last:
                    fractions(k + 1)
                dve.wait_ge(s5_bu, k + 1)
                dve.wait_ge(s5_tab, k + 1)
                re = ps[:, 0:2, :].rearrange("p b (q t) -> p (b q) t", q=2)
                im = ps[:, 2:4, :].rearrange("p b (q t) -> p (b q) t", q=2)
                cos, sin = COS[:, h], SIN[:, h]
                V.tensor_tensor(M[0], re, cos, ALU.mult)
                V.tensor_tensor(M[1], im, sin, ALU.mult)
                V.tensor_tensor(M[2], im, cos, ALU.mult)
                V.tensor_tensor(M[3], re, sin, ALU.mult).then_inc(s5_bur, 1)
                dve.wait_ge(s5_bur, k + 1)
                V.tensor_tensor(M[0], M[0], M[1], ALU.add)
                settle(V.tensor_tensor(M[2], M[2], M[3], ALU.subtract))
                for src, dst in ((M[0], M[1]), (M[2], M[3])):
                    for q in range(QK):
                        ins = V.tensor_tensor_scan(dst[:, q, :], dec[:, bass.ds(k * QK + q, 1)].to_broadcast([P, SEQ]),
                                                   src[:, q, :], 0.0, ALU.mult, ALU.add)
                settle(ins)
                if not first:
                    dve.wait_ge(s5_y, k)
                V.tensor_tensor(PR[0], cos, M[1], ALU.mult)
                V.scalar_tensor_tensor(PR[1], sin, -1.0, M[3], ALU.mult, ALU.mult)
                V.tensor_tensor(PR[2], sin, M[1], ALU.mult)
                V.tensor_tensor(PR[3], cos, M[3], ALU.mult).then_inc(s5_p, 1)
                dve.wait_ge(s5_p, k + 1)
                end = [w[:, :, SEQ - 1:SEQ].rearrange("p q a -> p (q a)") for w in PR]
                V.tensor_tensor(SF[:, 0, bass.ds(k * QK, QK)], end[0], end[1], ALU.add)
                V.tensor_tensor(SF[:, 1, bass.ds(k * QK, QK)], end[2], end[3], ALU.add)

            dve.wait_ge(norm_tp, 12)
            fractions(0)
            s5_tile(0, 0, first=True)
            s5_tile(0, 1)
            with dve.Fori(1, KT // 2 - 1) as i:
                st.enter(i - 1, 4)
                s5_tile(i, 0)
                s5_tile(i, 1)
            st.leave(KT // 2 - 2)
            s5_tile(KT // 2 - 1, 0)
            s5_tile(KT // 2 - 1, 1, last=True)
            dve.drain().then_inc(s5_sf, 1)

            dve.wait_ge(s5_y, KT)
            with dve.Fori(0, 4) as g:
                for r in range(GROUP):
                    dve.wait_ge(bank_read, g * GROUP + (r + 3))
                    n = g * GROUP + r
                    V.tensor_tensor(OT0[:, bass.ds(n, 1), :].rearrange("p a n -> p (a n)"), SIG[:, r, :],
                                    YT[:, bass.ds(n, 1), :].rearrange("p a n -> p (a n)"), ALU.mult).then_inc(glu_out, 1)
            add_and_norm(0)

            def top16(lists):
                for values, best, places, left in lists:
                    ins = V.max(best[:, 0:8], values)
                settle_all(ins)
                for values, best, places, left in lists:
                    V.max_index(places[:, 0:8], best[:, 0:8], values)
                    ins = V.match_replace(left, best[:, 0:8], values, LOWEST)
                settle_all(ins)
                for values, best, places, left in lists:
                    ins = V.max(best[:, 8:16], left)
                settle_all(ins)
                for values, best, places, left in lists:
                    ins = V.max_index(places[:, 8:16], best[:, 8:16], left)
                settle_all(ins)

            tv4 = TV.rearrange("p (t s k) -> p t s k", t=TILES, s=2)
            ge4 = GE.rearrange("p (t h k) -> p t h k", t=TILES, h=HEADS)
            gi4 = GI.rearrange("p (t h k) -> p t h k", t=TILES, h=HEADS)

            def as_cube(ap):
                return ap.rearrange("p (t a b) -> p t a b", t=TILES, a=TOPK)

            def key_lists(par):
                for j in range(2 * TILES):
                    t, e = j // 2, j % 2
                    at = 256 * (t % 2) + P * e
                    out = slice(TOPK * j, TOPK * (j + 1))
                    yield ps[:, 4 + 2 * par + t // 2, at:at + P], TV[:, out], TI[:, out], LEFT[:, P * j:P * (j + 1)]

            def candidate_lists():
                for t in range(TILES):
                    out, at = slice(TOPK * t, TOPK * (t + 1)), slice(CANDS * t, CANDS * (t + 1))
                    yield C[:, at], BV[:, out], BP[:, out], LEFT_OF[t]

            def choose(layer, h, par, keyed=True, cands=True, experts=True):
                if keyed:
                    dve.wait_ge(key_mm, h + (HEADS * layer + 1))
                if keyed or cands:
                    dve.sem_inc(top_go, 1)
                    top16([*(key_lists(par) if keyed else ()), *(candidate_lists() if cands else ())])
                if experts:
                    dve.wait_ge(picked, h - 2 + (HEADS * layer + 1))
                    ins = V.tensor_reduce(II, OH.rearrange("p (a b) -> p a b", b=TOPK), AX_X, ALU.add)
                if cands:
                    bv = BV.rearrange("p (t k) -> p t k", t=TILES)
                    V.tensor_scalar(AB[:, 0:3 * TOPK], BP, 4, None, ALU.logical_shift_right)
                    V.tensor_scalar(AB[:, 3 * TOPK:], BP, 15, None, ALU.bitwise_and)
                    ins = V.tensor_tensor(ge4[:, :, bass.ds(h - 1, 1), :].rearrange("p t a k -> p t (a k)"), bv,
                                          bv[:, :, 0:1].to_broadcast([P, TILES, TOPK]), ALU.subtract)
                if keyed:
                    dve.sem_inc(key_used, 1)
                    V.tensor_copy(TF[par], TI)
                    ins = V.tensor_tensor(as_cube(C), tv4[:, :, 0, :].unsqueeze(3).to_broadcast(cube),
                                          tv4[:, :, 1, :].unsqueeze(2).to_broadcast(cube), ALU.add)
                settle(ins)
                if experts:
                    dve.sem_inc(pick_read, 1)
                    ii = II.rearrange("p (s t k) -> p s t k", s=2, t=TILES)
                    V.scalar_tensor_tensor(gi4[:, :, bass.ds(h - 2, 1), :].rearrange("p t a k -> p t (a k)"), ii[:, 0],
                                           float(NKEYS), ii[:, 1], ALU.mult, ALU.add).then_inc(experts_set, 1)
                if cands:
                    V.tensor_copy(ABF[1 - par], AB).then_inc(pos_set, 1)

            def dots(layer, t, start, end):
                with dve.Fori(start, end) as i:
                    first = 2 * layer * ROUNDS + ROUND_AT[t]
                    for r in range(RING):
                        dve.wait_ge(row_in[r], i * 16 + 16 * (first + 1))
                        V.tensor_tensor_reduce(ring[:, r, :], ring[:, r, :], HN[:, t, :], 1.0, 0.0, ALU.mult, ALU.add,
                                               A8[:, r:r + 1]).then_inc(row_used, 1)
                    dve.wait_ge(row_used, i * RING + (RING * (first + 1) + RING))
                    st.enter(i - start, 1)
                    settle(V.tensor_copy(AV[:, bass.ds(i * RING + ROUND_AT[t] * RING, RING)], A8))
                st.leave(end - start)

            def peer(layer):
                dve.wait_ge(bank_read, (16, 80)[layer] + 3)
                choose(layer, 0, 0, cands=False, experts=False)
                choose(layer, 1, 1, experts=False)
                with dve.Fori(1, HEADS // 2) as i:
                    st.enter(i - 1, 2 * 5)
                    choose(layer, i * 2, 0)
                    choose(layer, i * 2 + 1, 1)
                st.leave(HEADS // 2 - 1)
                choose(layer, HEADS, 0, keyed=False)
                dots(layer, 0, 0, 1)
                choose(layer, HEADS + 1, 1, keyed=False, cands=False)
                dve.sem_inc(soft_in, 1)
                dve.wait_ge(experts_set, HEADS * (layer + 1))
                for c in range(1, COPIES):
                    rows, src = slice(NS * c, NS * (c + 1)), slice(2 * PICKS + NS * c, 2 * PICKS + NS * (c + 1))
                    ins = V.tensor_copy(GI[rows, 2 * PICKS:COLS], GI[rows, src])
                ins.then_inc(picks_ready, 1)
                dots(layer, 0, 1, ROUNDS_OF[0])
                dve.wait_ge(soft_exp, layer + 1)
                ge = GE.rearrange("p (g k) -> p g k", k=TOPK)
                groups = TILES * HEADS
                settle(V.tensor_reduce(GS[:, 0:groups], ge, AX_X, ALU.add))
                settle(V.reciprocal(GS[:, groups:], GS[:, 0:groups]))
                settle(V.tensor_tensor(GG.rearrange("p (g k) -> p g k", k=TOPK), ge,
                                       GS[:, groups:].unsqueeze(2).to_broadcast([P, groups, TOPK]), ALU.mult))
                for c in range(1, COPIES):
                    rows, src = slice(NS * c, NS * (c + 1)), slice(2 * PICKS + NS * c, 2 * PICKS + NS * (c + 1))
                    V.tensor_copy(GG[rows, 2 * PICKS:COLS], GG[rows, src])
                settle(V.memset(ACC, 0.0))
                for t in range(1, TILES):
                    dots(layer, t, 0, ROUNDS_OF[t])
                dve.sem_inc(dots_done, 1)
                dve.wait_ge(act_g, layer + 1)
                settle(V.tensor_tensor(WG[:, 0:COLS], WG[:, 0:COLS], GG[:, 0:COLS], ALU.mult))
                base = (2 * layer + 1) * ROUNDS
                for t in range(TILES):
                    to = X[:, t, :] if t < 2 else ACC
                    with dve.Fori(0, ROUNDS_OF[t]) as i:
                        first = base + ROUND_AT[t]
                        for r in range(RING):
                            dve.wait_ge(row_in[r], i * 16 + 16 * (first + 1))
                            dve.wait_ge(row_used, i * RING + (RING * first + RING + r))
                            V.scalar_tensor_tensor(to, ring[:, r, :], WG[:, bass.ds(i * RING + (ROUND_AT[t] * RING + r), 1)],
                                                   to, ALU.mult, ALU.add).then_inc(row_used, 1)
                    if t == 1:
                        for n in range(2):
                            norm_tile(2 * layer + 2, n)
                dve.wait_ge(row_used, RING * (base + ROUNDS) + RING)
                dve.sem_inc(peer_acc, 1)
                dve.wait_ge(peer_sum, layer + 1)
                V.tensor_tensor(X[:, 2, :], ps[:, 4:8, :].rearrange("p b n -> p (b n)"), X[:, 2, :], ALU.add).then_inc(peer_x, 1)
                dve.wait_ge(peer_x, layer + 1)
                norm_tile(2 * layer + 2, 2)

            peer(0)
            lam = CH[:, V_LAM, :]
            dve.wait_ge(lru_sp, 2)
            V.tensor_scalar(LS[2], LS[1], 1.0, None, ALU.add).then_inc(lru_sp, 1)
            dve.wait_ge(lru_sp, 4)
            settle(V.tensor_scalar(LS[4], LS[2], -1.0, None, ALU.add))
            settle(V.tensor_scalar(LS[7], LS[4], 0.0, None, ALU.is_equal))
            settle(V.tensor_tensor(LS[4], LS[4], LS[7], ALU.add))
            settle(V.reciprocal(LS[4], LS[4]))
            settle(V.tensor_tensor(LS[3], LS[3], LS[7], ALU.add))
            settle(V.tensor_tensor(LS[3], LS[3], LS[4], ALU.mult))
            settle(V.tensor_tensor(LS[3], LS[3], LS[1], ALU.mult))
            settle(V.tensor_scalar(LS[4], lam, -1.0, 0.0, ALU.mult, ALU.max))
            settle(V.tensor_tensor(LS[3], LS[3], LS[4], ALU.add))
            V.tensor_scalar(LS[5], LS[3], 8.0, None, ALU.mult)
            V.tensor_scalar(LS[6], LS[3], -8.0, None, ALU.mult).then_inc(lru_sp, 1)
            cw = [CH[:, V_CW + n, :] for n in range(4)]
            with dve.Fori(0, KT) as k:
                dve.wait_ge(bank_read, k + (32 + 3))
                st.enter(k, 4)
                xp = XBP[:, bass.ds(k, 1), :].rearrange("p a n -> p (a n)")
                xs = XBS[:, bass.ds(k, 1), :, :].rearrange("p a b n -> p (a b) n")
                op = XC[:, bass.ds(k, 1), 0:SEQ].rearrange("p a n -> p (a n)")
                os_ = XC[:, bass.ds(k, 1), SEQ:NT].rearrange("p a (b n) -> p (a b) n", b=SB)
                one = bass.ds(k, 1)
                V.tensor_scalar(op, xp[:, 0:SEQ], cw[0][:, one], CH[:, V_CB, one], ALU.mult, ALU.add)
                settle(V.tensor_scalar(os_, xs[:, :, 0:ST], cw[0][:, one], CH[:, V_CB, one], ALU.mult, ALU.add))
                for n in range(1, 4):
                    V.scalar_tensor_tensor(op, xp[:, n:n + SEQ], cw[n][:, one], op, ALU.mult, ALU.add)
                    settle(V.scalar_tensor_tensor(os_, xs[:, :, n:n + ST], cw[n][:, one], os_, ALU.mult, ALU.add))
            st.leave(KT)
            V.tensor_copy(LOUT[:, 16:64].rearrange("p (k n) -> p k n", k=KT), XBP[:, :, SEQ:SEQ + 3])
            V.tensor_copy(LOUT[:, 192:576].rearrange("p (k b n) -> p k b n", k=KT, b=SB), XBS[:, :, :, 4:7]).then_inc(lru_st, 1)
            dve.sem_inc(lru_xc, 1)
            dve.wait_ge(gate_ev, 32)
            V.tensor_tensor(IG, IG, XC, ALU.mult)
            dve.wait_ge(lru_th, 1)
            for half in range(2):
                th = TH[:, KT // 2 * half:KT // 2 * (half + 1), :]
                settle(V.tensor_scalar(LV, th, 1.0, None, ALU.add))
                settle(V.reciprocal(LV, LV))
                ins = V.scalar_tensor_tensor(th, th, 2.0, LV, ALU.mult, ALU.mult)
                if half == 0:
                    settle(ins)
            ins.then_inc(lru_v, 1)
            dve.wait_ge(lru_rt, 1)
            settle(V.tensor_tensor(IG, IG, TH, ALU.mult))
            dve.wait_ge(lru_a, 1)
            with dve.Fori(0, KT) as k:
                one = bass.ds(k, 1)
                V.tensor_tensor_scan(XC[:, one, 0:SEQ].rearrange("p a n -> p (a n)"),
                                     RA[:, one, 0:SEQ].rearrange("p a n -> p (a n)"),
                                     IG[:, one, 0:SEQ].rearrange("p a n -> p (a n)"), 0.0, ALU.mult, ALU.add)
            ra_s = RA[:, :, SEQ:NT].rearrange("p k (b t) -> p k b t", b=SB)
            bx_s = IG[:, :, SEQ:NT].rearrange("p k (b t) -> p k b t", b=SB)
            hs_s = XC[:, :, SEQ:NT].rearrange("p k (b t) -> p k b t", b=SB)
            prev = LH0
            for n in range(ST):
                settle(V.tensor_tensor(LT, ra_s[:, :, :, n], prev, ALU.mult))
                settle(V.tensor_tensor(hs_s[:, :, :, n], bx_s[:, :, :, n], LT, ALU.add))
                prev = hs_s[:, :, :, n]
            V.tensor_copy(LOUT[:, 0:16], XC[:, :, SEQ - 1])
            V.tensor_copy(LOUT[:, 64:192].rearrange("p (k b) -> p k b", k=KT), prev).then_inc(lru_hs, 1)
            dve.wait_ge(bank_read, 64 + 2)
            dve.wait_ge(lru_hs, 1)
            V.tensor_tensor(GT, GT, XC, ALU.mult).then_inc(lru_y, 1)
            dve.wait_ge(bank_read, 82)
            add_and_norm(1)
            peer(1)


def kernel(**inputs):
    import numpy as np
    import concourse.bacc as _bacc
    from concourse import mybir as _mybir
    from concourse.bass_utils import run_bass_kernel_spmd as _run

    a = {k: np.asarray(v) for k, v in inputs.items()}

    def column_slabs(w):
        n = w.shape[1] // P
        return w.reshape(KT, P, n, P).transpose(2, 1, 0, 3).reshape(n, P, D)

    gates = np.stack([a["lru_w_a"][0], a["lru_w_i"][0]]).reshape(2, 4, 2, 2, P, 2, P)
    keys = a["peer_sub_keys"].reshape(2, 2 * HEADS, NKEYS, P).transpose(0, 3, 1, 2).reshape(2, P, D)
    slabs = np.concatenate([
        column_slabs(a["s5_w_glu"][0]), column_slabs(a["peer_w_q"][0]),
        column_slabs(a["lru_w_in"][0][:, D:]), gates.transpose(1, 4, 2, 0, 5, 3, 6).reshape(4, P, D),
        column_slabs(a["lru_w_in"][0][:, :D]), column_slabs(a["lru_w_out"][0]),
        column_slabs(a["peer_w_q"][1])])

    def channels(v):
        return v.reshape(KT, P).T

    chan = np.concatenate([channels(v) for v in (
        a["s5_d"][0], a["s5_b_glu"][0], *a["lru_conv_w"][0], a["lru_conv_b"][0],
        a["lru_b_a"][0].reshape(-1), a["lru_b_i"][0].reshape(-1), a["lru_lam"][0])], axis=1)

    def states(v):
        return v.reshape(S5_Q, 2, 64, *v.shape[2:]).transpose(1, 2, 0, *range(3, v.ndim + 1)).reshape(P, S5_Q, *v.shape[2:])

    log_dt = np.repeat(a["s5_log_dt"][0][:, None], 64, axis=1)
    s5_vec = np.concatenate([states(a["s5_lam_re"][0]), states(a["s5_lam_im"][0]), states(log_dt)], axis=1)

    def by_group(v):
        out = np.zeros((2, 64, S5_Q, 2, 16), v.dtype)
        w = v.reshape(2, 64, S5_Q, 16)
        out[0, :, :, 0], out[1, :, :, 1] = w[0], w[1]
        return out.reshape(P, KT, P)

    bc = [by_group(states(v)) for v in (a["s5_b_re"][0], a["s5_b_im"][0], a["s5_c_re"][0].transpose(0, 2, 1),
                                        a["s5_c_im"][0].transpose(0, 2, 1))]
    s5_bc = np.stack(bc, axis=2).transpose(1, 0, 2, 3).reshape(KT, P, 4 * P)
    s5_h0 = np.concatenate([states(v[0].transpose(1, 2, 0)).reshape(P, -1) for v in (a["state_s5_re"], a["state_s5_im"])], axis=1)
    conv = a["state_lru_conv"][0].reshape(SB, 3, KT, P).transpose(3, 2, 0, 1).reshape(P, -1)
    h0 = a["state_lru_h"][0].reshape(SB, KT, P).transpose(2, 1, 0).reshape(P, -1)
    sample = a["x_sample"].reshape(NS, D)
    arrays = {
        "x": np.concatenate([a["x_prompt"].reshape(2, P, D), np.tile(sample, (COPIES, 1))[None]]),
        "norms": np.stack([a["norm_mix"][0], a["norm_ffn"][0], a["norm_mix"][1], a["norm_ffn"][1], a["norm_final"]]),
        "slabs": slabs, "keys": keys, "chan": chan, "s5_vec": s5_vec, "s5_bc": s5_bc, "s5_h0": s5_h0,
        "lru_in": np.concatenate([conv, h0], axis=1),
        "u0": a["peer_u"][0], "v0": a["peer_v"][0], "u1": a["peer_u"][1], "v1": a["peer_v"][1],
    }
    outs = {"y": (2, P, D), "ys": (NS, D), "s5p": (P, 2 * S5_Q), "s5s": (P, 2 * S5_Q * SB), "lru": (P, 576)}

    nc = _bacc.Bacc("TRN2", target_bir_lowering=False, num_devices=1)
    args, in_map = [], {}
    for name, v in arrays.items():
        v = np.ascontiguousarray(v)
        in_map[f"in_{name}_dram"] = v
        args.append(nc.dram_tensor(f"in_{name}_dram", v.shape, _mybir.dt.from_np(v.dtype), kind="ExternalInput").ap())
    for name, shape in outs.items():
        args.append(nc.dram_tensor(f"out_{name}_dram", shape, F32, kind="ExternalOutput").ap())
    hybrid_step(nc, *args)
    r = _run(nc, [in_map], core_ids=[0]).results[0]
    y, ys, s5p, s5s, lru = (np.asarray(r[f"out_{name}_dram"]) for name in outs)

    def groups(v):
        return v.reshape(2, 64, S5_Q, -1).transpose(3, 2, 0, 1).reshape(-1, 2 * S5_Q, 64)

    s5p = s5p.reshape(P, 2, S5_Q)
    s5s = s5s.reshape(P, 2, S5_Q, SB)
    hp, cp, hs, cs = lru[:, 0:16], lru[:, 16:64], lru[:, 64:192], lru[:, 192:576]
    return (y.reshape(1, SEQ, D), ys.reshape(SB, ST, D),
            groups(s5p[:, 0])[None], groups(s5p[:, 1])[None], groups(s5s[:, 0])[None], groups(s5s[:, 1])[None],
            hp.T.reshape(1, 1, D), cp.reshape(P, KT, 3).transpose(2, 1, 0).reshape(1, 1, 3, D),
            hs.reshape(P, KT, SB).transpose(2, 1, 0).reshape(1, SB, D),
            cs.reshape(P, KT, SB, 3).transpose(2, 3, 1, 0).reshape(1, SB, 3, D))
```

```python
from contextlib import ExitStack

import concourse.bass as bass
from concourse import mybir

F32 = mybir.dt.float32
I32 = mybir.dt.int32
U32 = mybir.dt.uint32
ALU = mybir.AluOpType
ACT = mybir.ActivationFunctionType
AX_X = mybir.AxisListType.X

P = 128
D = 2048
KT = D // P
SEQ = 256
SB, ST = 8, 4
NS = SB * ST
NT = SEQ + NS
TILES = 3
PAIR = 2
COPIES = P // NS
BANK = 512
GROUP = 4
PI = 3.14159265358979
TWO_PI_LOW = 6.283185
ROUND = 12582912.0
EPS = 1e-6
LOWEST = -3.0e38

S5_Q = 64
QK = 4
QC = 32

SLAB_GLU, SLAB_Q0, SLAB_XB, SLAB_GATE, SLAB_IN, SLAB_OUT, SLAB_Q1, SLABS = 0, 16, 32, 48, 52, 68, 84, 100
WRING = 4

HEADS, TOPK, NKEYS = 8, 16, 128
CANDS = TOPK * TOPK
PICKS = HEADS * TOPK
RING = 8
EARLY = 6
COLS = 2 * PICKS + PICKS // COPIES
ROUNDS_OF = [PICKS // RING, PICKS // RING, PICKS // COPIES // RING]
ROUND_AT = [0, PICKS // RING, 2 * PICKS // RING]
ROUNDS = COLS // RING
LAST_HEAD_AT = 4

V_D, V_BGLU, V_CW, V_CB, V_BA, V_BI, V_LAM, V_N = 0, 1, 2, 6, 7, 8, 9, 10


def token_cols(t):
    return slice(t * P, (t + 1) * P) if t < 2 else slice(SEQ, NT)


class Steps:

    def __init__(self):
        self.base, self.i, self.per, self.n = 0, 0, 0, 0

    def enter(self, i, per):
        self.base, self.i, self.per, self.n = self.base + self.n, i, per, 0

    def leave(self, rounds):
        assert self.n == self.per, (self.n, self.per)
        self.base, self.i, self.per, self.n = self.base + rounds * self.per, 0, 0, 0

    def next(self):
        self.n += 1
        return self.i * self.per + (self.base + self.n)


def hybrid_step(nc, x, norms, slabs, keys, chan, s5_vec, s5_bc, s5_h0, lru_in, u0, v0, u1, v1,
                y_out, ys_out, s5p_out, s5s_out, lru_out):
    experts_u, experts_v = [u0, u1], [v0, v1]
    with ExitStack() as ctx:
        def sb(name, shape, dt=F32):
            return ctx.enter_context(nc.sbuf_tensor(name, shape, dt))

        def sem(name):
            return ctx.enter_context(nc.semaphore(name))

        X = sb("X", [P, TILES, D])
        HN = sb("HN", [P, TILES, D])
        HT = sb("HT", [P, KT, NT])
        W = sb("W", [P, WRING, D])
        GB = sb("GB", [P, 2, D])
        CH = sb("CH", [P, V_N, KT])
        arena = sb("arena", [P, 22528])
        ident = sb("ident", [P, P])
        repsum = sb("repsum", [P, P])
        iota = sb("iota", [P, SEQ])
        zeros = sb("zeros", [P, P])
        cst = sb("cst", [P, 2])
        ixs = sb("ixs", [P, RING], I32)
        nrm = sb("nrm", [P, 12])
        ps = ctx.enter_context(nc.psum_tensor("ps", [P, 8, BANK], F32))
        hn_flat = HN[:].rearrange("p a b -> p (a b)")

        def view(at, n, base=None):
            return (arena if base is None else base)[:, at:at + n]

        YT = view(0, KT * NT).rearrange("p (k n) -> p k n", k=KT)
        SSO = view(4608, 1024).rearrange("p (c q b) -> p c q b", c=2, q=S5_Q)
        S0 = view(5632, 1024).rearrange("p (c q b) -> p c q b", c=2, q=S5_Q)
        par = [view(6656 + 68 * n, 68) for n in range(24)]
        BC = view(8320, 1024).rearrange("p (h c n) -> p h c n", h=2, c=4)
        BX = view(9344, 256).rearrange("p (c n) -> p c n", c=2)
        BT = view(9600, 256).rearrange("p (c n) -> p c n", c=2)
        CN = view(9856, 256).rearrange("p (h n) -> p h n", h=2)
        DD = view(10112, 256).rearrange("p (h n) -> p h n", h=2)
        BS = view(10368, 512).rearrange("p (h c q b t) -> p h c q b t", h=2, c=2, q=QK, b=SB)
        BSF = view(10368, 512).rearrange("p (h c n) -> p h c n", h=2, c=2)
        SF = view(10880, 128).rearrange("p (c q) -> p c q", c=2)
        PT = view(11008, 512).rearrange("p (n m) -> p n m", n=4)
        UX = view(11520, QK * NT).rearrange("p (q n) -> p q n", q=QK)
        PRD = view(12672, 1024).rearrange("p (q t) -> p q t", q=QK)
        COS = view(13696, 2048).rearrange("p (h q t) -> p h q t", h=2, q=QK)
        SIN = view(15744, 2048).rearrange("p (h q t) -> p h q t", h=2, q=QK)
        M = [view(17792 + 1024 * n, 1024).rearrange("p (q t) -> p q t", q=QK) for n in range(4)]
        PR = [hn_flat[:, 1024 * n:1024 * (n + 1)].rearrange("p (q t) -> p q t", q=QK) for n in range(4)]
        PRY = hn_flat[:, 4096:5120].rearrange("p (q t) -> p q t", q=QK)
        vecs = view(21888, 192)
        SIG = view(17792, 4 * NT).rearrange("p (n m) -> p n m", n=4)
        OT0 = view(13056, KT * NT).rearrange("p (k n) -> p k n", k=KT)
        REP0 = view(18944, D)
        GT = view(0, KT * NT).rearrange("p (k n) -> p k n", k=KT)
        XC = view(4608, KT * NT).rearrange("p (k n) -> p k n", k=KT)
        XBP = view(9216, KT * (SEQ + 3)).rearrange("p (k n) -> p k n", k=KT)
        XBS = view(9216 + KT * (SEQ + 3), KT * SB * 7).rearrange("p (k b n) -> p k b n", k=KT, b=SB)
        TH = view(9216, KT * NT).rearrange("p (k n) -> p k n", k=KT)
        RA = view(14256, KT * NT).rearrange("p (k n) -> p k n", k=KT)
        IG = hn_flat[:, 0:KT * NT].rearrange("p (k n) -> p k n", k=KT)
        LIN = view(18864, 512)
        LCONV = view(18864, 384).rearrange("p (k b n) -> p k b n", k=KT, b=SB)
        LH0 = view(18864 + 384, 128).rearrange("p (k b) -> p k b", k=KT)
        LOUT = view(19376, 576)
        LT = view(19952, 128).rearrange("p (k b) -> p k b", k=KT)
        LS = [view(20080 + 16 * n, 16) for n in range(8)]
        LV = view(20208, KT // 2 * NT).rearrange("p (k n) -> p k n", k=KT // 2)
        OT1 = XC
        REP1 = view(14256, D)
        KEYS = view(EARLY * D, D)
        QT = view((EARLY + 1) * D, 4 * NT).rearrange("p (h s n) -> p h s n", h=2, s=2)
        REPQ = view((EARLY + 1) * D + 4 * NT, 4 * P).rearrange("p (h s n) -> p h s n", h=2, s=2)
        at = RING * D
        small = {}
        for name, n in (("TV", 2 * PAIR * TOPK), ("TI", 2 * PAIR * TOPK), ("TF", 4 * PAIR * TOPK), ("C", PAIR * CANDS),
                        ("LEFT", PAIR * CANDS), ("LEFT_C", PAIR * CANDS), ("BV", PAIR * TOPK), ("BP", PAIR * TOPK),
                        ("AB", 2 * PAIR * TOPK), ("ABF", 4 * PAIR * TOPK), ("OH", 2 * PAIR * CANDS),
                        ("II", 2 * PAIR * TOPK), ("GS", 2 * COLS // TOPK)):
            small[name] = view(at, n)
            at += n
        assert at <= RING * D + 2 * D
        GE = view(22032, COLS)
        TV, TI, TF, C, LEFT, LEFT_C = (small[n] for n in ("TV", "TI", "TF", "C", "LEFT", "LEFT_C"))
        BV, BP, AB, ABF, OH, II, GS = (small[n] for n in ("BV", "BP", "AB", "ABF", "OH", "II", "GS"))
        TI, BP, AB = (w.bitcast(U32) for w in (TI, BP, AB))
        TF, ABF = ([w[:, 2 * PAIR * TOPK * n:2 * PAIR * TOPK * (n + 1)] for n in range(2)] for w in (TF, ABF))
        cube = [P, PAIR, TOPK, TOPK]
        ring = view(0, RING * D).rearrange("p (r d) -> p r d", r=RING)
        ACC = view(18432, D)
        GI = view(20480, 384).bitcast(I32)
        GG = view(20864, 384)
        AV = view(21248, 384)
        WG = view(21632, 384)
        A8 = view(22016, RING)

        x_in = [sem(f"x_in{t}") for t in range(TILES)]
        small_in = sem("small_in")
        s5_in, s5_h0_in = sem("s5_in"), sem("s5_h0_in")
        lru_in_sem = sem("lru_in_sem")
        gain_in = sem("gain_in")
        consts = sem("consts")
        slab_in = [sem(f"slab_in{r}") for r in range(WRING)]
        slab_done = sem("slab_done")
        bank_read = sem("bank_read")
        norm_sq, norm_v, norm_rt, norm_h = sem("norm_sq"), sem("norm_v"), sem("norm_rt"), sem("norm_h")
        norm_tp, norm_ht = sem("norm_tp"), sem("norm_ht")
        glu_out = sem("glu_out")
        mix_rep, mix_tp, mix_x = sem("mix_rep"), sem("mix_tp"), sem("mix_x")
        vstep, pstep, astep = sem("vstep"), sem("pstep"), sem("astep")
        s5_pa, s5_pv = sem("s5_pa"), sem("s5_pv")
        s5_b_in, s5_c_in = [sem("s5_b_in0"), sem("s5_b_in1")], [sem("s5_c_in0"), sem("s5_c_in1")]
        s5_bx, s5_bt, s5_btc, s5_ux = sem("s5_bx"), sem("s5_bt"), sem("s5_btc"), sem("s5_ux")
        s5_cn, s5_dd, s5_bu, s5_bur = sem("s5_cn"), sem("s5_dd"), sem("s5_bu"), sem("s5_bur")
        s5_bsc, s5_bsd, s5_prod, s5_f = sem("s5_bsc"), sem("s5_bsd"), sem("s5_prod"), sem("s5_f")
        s5_tab, s5_p, s5_y, s5_yg = sem("s5_tab"), sem("s5_p"), sem("s5_y"), sem("s5_yg")
        s5_wi = sem("s5_wi")
        s5_sf, s5_zero, stores = sem("s5_sf"), sem("s5_zero"), sem("stores")
        y_stored, top_go, pool_go = sem("y_stored"), sem("top_go"), sem("pool_go")
        lru_pad, lru_xc, lru_st = sem("lru_pad"), sem("lru_xc"), sem("lru_st")
        gate_mm, gate_ev, lru_sp, lru_a = sem("gate_mm"), sem("gate_ev"), sem("lru_sp"), sem("lru_a")
        lru_th, lru_v, lru_rt, lru_y = sem("lru_th"), sem("lru_v"), sem("lru_rt"), sem("lru_y")
        lru_hs = sem("lru_hs")
        pos_set, pos_off, one_hot = sem("pos_set"), sem("pos_off"), sem("one_hot")
        picked, pick_read, experts_set = sem("picked"), sem("pick_read"), sem("experts_set")
        sample_picks = sem("sample_picks")
        keys_in, key_mm, key_used = sem("keys_in"), sem("key_mm"), sem("key_used")
        soft_in, soft_exp, picks_ready = sem("soft_in"), sem("soft_exp"), sem("picks_ready")
        row_in = [sem(f"row_in{r}") for r in range(RING)]
        row_used, index_set, gather_go = sem("row_used"), sem("index_set"), sem("gather_go")
        dots_done, act_g, peer_acc, peer_sum, peer_x = sem("dots_done"), sem("act_g"), sem("peer_acc"), sem("peer_sum"), sem("peer_x")

        block = ctx.enter_context(nc.Block())

        @block.sync
        def _(sp):
            sp.wait_ge(s5_in, 16)
            for t in range(TILES):
                sp.dma_start(X[:, t, :], x[t]).then_inc(x_in[t], 16)
            def s5_bc_tile(i, h, first):
                k = 2 * i + h
                for part, slot_in, used in ((0, s5_b_in, s5_bx), (1, s5_c_in, s5_y)):
                    if not first:
                        sp.wait_ge(used, k - 1)
                    sp.dma_start(BC[:, h, 2 * part:2 * part + 2, :].rearrange("p c n -> p (c n)"),
                                 s5_bc[bass.ds(k, 1), :, 2 * P * part:2 * P * (part + 1)].rearrange("a p n -> p (a n)")
                                 ).then_inc(slot_in[h], 16)

            for h in range(2):
                s5_bc_tile(0, h, True)
            sp.dma_start(S0[:].rearrange("p c q b -> p (c q b)"), s5_h0).then_inc(s5_h0_in, 16)
            with sp.Fori(1, KT // 2) as i:
                for h in range(2):
                    s5_bc_tile(i, h, False)
            for r in range(WRING):
                sp.dma_start(W[:, r, :], slabs[r]).then_inc(slab_in[r], 16)
            with sp.Fori(1, SLABS // WRING) as g:
                for r in range(WRING):
                    sp.wait_ge(slab_done, g * WRING + (r - WRING + 1))
                    sp.dma_start(W[:, r, :], slabs[bass.ds(g * WRING + r, 1)].rearrange("a p n -> p (a n)")).then_inc(slab_in[r], 16)
            for n in range(SLABS // WRING * WRING, SLABS):
                sp.wait_ge(slab_done, n - WRING + 1)
                sp.dma_start(W[:, n % WRING, :], slabs[n]).then_inc(slab_in[n % WRING], 16)
            for t in range(2):
                sp.wait_ge(norm_h, 12 + t + 1)
                sp.dma_start(y_out[t], HN[:, t, :]).then_inc(y_stored, 16)
            sp.wait_ge(norm_h, 15)
            sp.dma_start(ys_out, HN[0:NS, 2, :]).then_inc(y_stored, 16)
            sp.wait_ge(y_stored, 16 * 3)

        @block.gpsimd
        def _(pool):
            st = Steps()
            for n in range(2):
                pool.dma_start(GB[:, n, :], norms[n:n + 1, :].partition_broadcast(P)).then_inc(gain_in, 16)
            nc.gpsimd.memset(ident[:], 0.0).then_inc(pstep, 1)
            nc.gpsimd.memset(repsum[:], 0.0).then_inc(pstep, 1)
            nc.gpsimd.memset(zeros[:], 0.0).then_inc(pstep, 1)
            nc.gpsimd.memset(cst[:, 0:1], PI / 2).then_inc(pstep, 1)
            nc.gpsimd.memset(cst[:, 1:2], ROUND).then_inc(pstep, 1)
            nc.gpsimd.iota(iota[:], [[1, SEQ]], base=0, channel_multiplier=0,
                           allow_small_or_imprecise_dtypes=True).then_inc(pstep, 1)
            for _ in range(5):
                st.next()
            pool.wait_ge(pstep, st.next())
            nc.gpsimd.affine_select(out=ident[:], in_=ident[:], compare_op=ALU.not_equal, fill=1.0, base=0,
                                    pattern=[[-1, P]], channel_multiplier=1).then_inc(consts, 1)
            for c in range(-COPIES + 1, COPIES):
                nc.gpsimd.affine_select(out=repsum[:], in_=repsum[:], compare_op=ALU.not_equal, fill=1.0,
                                        base=-NS * c, pattern=[[-1, P]], channel_multiplier=1).then_inc(pstep, 1)
                pool.wait_ge(pstep, st.next())
            pool.sem_inc(consts, 1)

            abr, abi, fr, fi = par[0], par[1], par[2], par[3]

            def diagonal(i, h):
                nc.gpsimd.tensor_tensor(DD[:, h, :], ident[:], CH[:, V_D, bass.ds(2 * i + h, 1)].to_broadcast([P, P]),
                                        ALU.mult).then_inc(s5_dd, 1)

            def discrete_b(i, h, first):
                k = 2 * i + h
                pool.wait_ge(s5_b_in[h], (i + 1) * 16)
                pool.sem_inc(pool_go, 1)
                b = [BC[:, h, c, :].rearrange("p (q n) -> p q n", q=QK) for c in range(2)]
                f = [w[:, bass.ds(k * QK, QK)].unsqueeze(2).to_broadcast([P, QK, QC]) for w in (fr, fi)]
                t = [PT[:, n, :].rearrange("p (q n) -> p q n", q=QK) for n in range(4)]
                for n, (c, e) in enumerate([(0, 0), (1, 1), (0, 1), (1, 0)]):
                    ins = nc.gpsimd.tensor_tensor(t[n], b[c], f[e], ALU.mult)
                ins.then_inc(pstep, 1)
                pool.wait_ge(pstep, st.next())
                if not first:
                    pool.wait_ge(s5_bt, k)
                nc.gpsimd.tensor_tensor(BX[:, 0, :], PT[:, 0, :], PT[:, 1, :], ALU.subtract)
                nc.gpsimd.tensor_tensor(BX[:, 1, :], PT[:, 2, :], PT[:, 3, :], ALU.add).then_inc(s5_bx, 1)
                pool.wait_ge(s5_bx, k + 1)

            def sample_states(i, h):
                k = 2 * i + h
                pool.wait_ge(s5_bsc, k + 1)
                pool.sem_inc(pool_go, 1)
                a = [w[:, bass.ds(k * QK, QK)].unsqueeze(2).to_broadcast([P, QK, SB]) for w in (abr, abi)]
                s = [S0[:, c, bass.ds(k * QK, QK), :] for c in range(2)]
                t = [PT[:, n, 0:QK * SB].rearrange("p (q b) -> p q b", q=QK) for n in range(4)]
                for step in range(ST):
                    for n, (c, e) in enumerate([(0, 0), (1, 1), (0, 1), (1, 0)]):
                        ins = nc.gpsimd.tensor_tensor(t[n], a[c], s[e], ALU.mult)
                    ins.then_inc(pstep, 1)
                    pool.wait_ge(pstep, st.next())
                    nc.gpsimd.tensor_tensor(t[0], t[0], t[1], ALU.subtract)
                    nc.gpsimd.tensor_tensor(t[2], t[2], t[3], ALU.add).then_inc(pstep, 1)
                    pool.wait_ge(pstep, st.next())
                    s = [BS[:, h, c, :, :, step] for c in range(2)]
                    nc.gpsimd.tensor_tensor(s[0], s[0], t[0], ALU.add)
                    ins = nc.gpsimd.tensor_tensor(s[1], s[1], t[2], ALU.add)
                    if step < ST - 1:
                        ins.then_inc(pstep, 1)
                        pool.wait_ge(pstep, st.next())
                        pool.sem_inc(pool_go, 1)
                ins.then_inc(s5_bsd, 1)
                pool.wait_ge(s5_bsd, k + 1)
                pool.sem_inc(pool_go, 1)
                for c in range(2):
                    ins = nc.gpsimd.tensor_copy(SSO[:, c, bass.ds(k * QK, QK), :], s[c])
                ins.then_inc(pstep, 1)
                pool.wait_ge(pstep, st.next())

            def s5_tile(i, h, first=False, last=False):
                nxt = (i, 1) if h == 0 else (i + 1, 0)
                if not last:
                    discrete_b(*nxt, False)
                pool.wait_ge(s5_bur, 2 * i + h + 1)
                nc.gpsimd.tensor_tensor(M[2], M[2], M[3], ALU.subtract).then_inc(s5_wi, 1)
                sample_states(i, h)
                if not last:
                    if not first:
                        pool.wait_ge(s5_y, 2 * i + h)
                        pool.sem_inc(pool_go, 1)
                    diagonal(*nxt)

            pool.wait_ge(small_in, 16)
            pool.wait_ge(s5_h0_in, 16)
            pool.wait_ge(s5_pv, 3)
            diagonal(0, 0)
            discrete_b(0, 0, True)
            per_tile = 1 + 3 * ST
            s5_tile(0, 0, True)
            s5_tile(0, 1)
            with pool.Fori(1, KT // 2 - 1) as i:
                st.enter(i - 1, 2 * per_tile)
                s5_tile(i, 0)
                s5_tile(i, 1)
            st.leave(KT // 2 - 2)
            s5_tile(KT // 2 - 1, 0)
            s5_tile(KT // 2 - 1, 1, last=True)
            pool.dma_start(s5s_out, SSO[:].rearrange("p c q b -> p (c q b)")).then_inc(stores, 16)
            pool.wait_ge(s5_sf, 1)
            pool.dma_start(s5p_out, SF[:].rearrange("p c q -> p (c q)")).then_inc(stores, 16)
            pool.wait_ge(stores, 32)
            pool.sem_inc(s5_zero, 1)
            pool.wait_ge(mix_x, 12)
            pool.dma_start(KEYS, keys[0]).then_inc(keys_in, 16)

            def gather(table, base, i, r):
                pool.wait_ge(row_used, i * RING + (base * RING + r + 1))
                nc.gpsimd.tensor_copy(ixs[:, r:r + 1], GI[:, bass.ds(i * RING + r, 1)]).then_inc(index_set, 1)
                pool.wait_ge(index_set, i * RING + (base * RING + r + 1))
                pool.sem_inc(gather_go, 1)
                pool.indirect_dma_start(ring[:, r, :], None, table,
                                        bass.IndirectOffsetOnAxis(ap=ixs[:, r:r + 1], axis=0)).then_inc(row_in[r], 16)

            def one_head(layer, h, par):
                oh = [OH[:, PAIR * CANDS * s:PAIR * CANDS * (s + 1)] for s in range(2)]
                pool.wait_ge(pos_set, h + (HEADS * layer + 1))
                pool.wait_ge(pick_read, h + (HEADS * layer + 1))
                for s in range(2):
                    part = ABF[par][:, PAIR * TOPK * s:PAIR * TOPK * (s + 1)]
                    ins = nc.gpsimd.tensor_tensor(oh[s].rearrange("p (a b) -> p a b", b=TOPK),
                                                  part.unsqueeze(2).to_broadcast([P, PAIR * TOPK, TOPK]),
                                                  iota[:, 0:TOPK].unsqueeze(1).to_broadcast([P, PAIR * TOPK, TOPK]),
                                                  ALU.subtract)
                ins.then_inc(pos_off, 1)
                pool.wait_ge(one_hot, h + (HEADS * layer + 1))
                tf4 = TF[par].rearrange("p (t s k) -> p t s k", t=PAIR, s=2)
                for s in range(2):
                    cells = oh[s].rearrange("p (t a b) -> p t a b", t=PAIR, a=TOPK)
                    ins = nc.gpsimd.tensor_tensor(cells, cells, tf4[:, :, s, :].unsqueeze(2).to_broadcast(cube), ALU.mult)
                ins.then_inc(picked, 1)

            def index_parts(layer):
                def first_rounds(i, rows):
                    for r in rows:
                        gather(experts_u[layer], 2 * layer * ROUNDS, i, r)

                one_head(layer, 0, 0)
                one_head(layer, 1, 1)
                pool.wait_ge(experts_set, HEADS * layer + 1)
                first_rounds(0, range(EARLY))
                with pool.Fori(1, HEADS // 2 - 2) as i:
                    one_head(layer, i * 2, 0)
                    one_head(layer, i * 2 + 1, 1)
                one_head(layer, HEADS - 4, 0)
                pool.wait_ge(key_mm, HEADS * (layer + 1))
                first_rounds(0, range(EARLY, RING))
                first_rounds(1, range(2))
                one_head(layer, HEADS - 3, 1)
                first_rounds(1, range(2, EARLY))
                one_head(layer, HEADS - 2, 0)
                first_rounds(1, range(EARLY, RING))

            def gathers(layer):
                for n in ((2, 3) if layer == 0 else (4,)):
                    pool.wait_ge(norm_h, 3 * (n - 1))
                    pool.dma_start(GB[:, n % 2, :], norms[n:n + 1, :].partition_broadcast(P)).then_inc(gain_in, 16)
                index_parts(layer)
                base = 2 * layer * ROUNDS
                known = (HEADS - 2) * TOPK // RING
                pool.wait_ge(experts_set, HEADS * layer + HEADS - 2)
                with pool.Fori(2, LAST_HEAD_AT + 1) as i:
                    for r in range(RING):
                        gather(experts_u[layer], base, i, r)
                one_head(layer, HEADS - 1, 1)
                with pool.Fori(LAST_HEAD_AT + 1, known) as i:
                    for r in range(RING):
                        gather(experts_u[layer], base, i, r)
                pool.wait_ge(picks_ready, layer + 1)
                with pool.Fori(known, ROUND_AT[2]) as i:
                    for r in range(RING):
                        gather(experts_u[layer], base, i, r)
                pool.wait_ge(sample_picks, layer + 1)
                with pool.Fori(ROUND_AT[2], ROUNDS) as i:
                    for r in range(RING):
                        gather(experts_u[layer], base, i, r)
                with pool.Fori(0, ROUNDS) as i:
                    for r in range(RING):
                        gather(experts_v[layer], base + ROUNDS, i, r)

            gathers(0)
            pool.wait_ge(peer_x, 1)
            pool.dma_start(LIN, lru_in).then_inc(lru_in_sem, 16)
            nc.gpsimd.memset(XBP[:, :, 0:3], 0.0).then_inc(lru_pad, 1)
            pool.wait_ge(lru_in_sem, 16)
            nc.gpsimd.tensor_copy(XBS[:, :, :, 0:3], LCONV).then_inc(lru_pad, 1)
            pool.wait_ge(lru_hs, 1)
            pool.dma_start(lru_out, LOUT).then_inc(stores, 16)
            pool.wait_ge(stores, 48)
            pool.sem_inc(s5_zero, 1)
            pool.wait_ge(mix_x, 24)
            pool.dma_start(KEYS, keys[1]).then_inc(keys_in, 16)
            gathers(1)

        @block.tensor
        def _(pe):
            def norm_transposes(j):
                for t in range(TILES):
                    pe.wait_ge(norm_h, 3 * j + t + 1)
                    rows = P if t < 2 else NS
                    for g in range(GROUP):
                        n = 12 * j + 4 * t + g
                        if n >= 2:
                            pe.wait_ge(norm_ht, n - 1)
                        for e in range(4):
                            k = 4 * g + e
                            mm = nc.tensor.transpose(ps[:, 2 + n % 2, rows * e:rows * (e + 1)],
                                                     HN[0:rows, t, P * k:P * (k + 1)], ident[0:rows, 0:rows])
                        mm.then_inc(norm_tp, 1)

            def product(slab, n0, groups, rhs):
                with pe.Fori(0, groups) as g:
                    for r in range(GROUP):
                        slot = (slab + r) % WRING
                        pe.wait_ge(slab_in[slot], g * 16 + 16 * ((slab + r) // WRING + 1))
                        pe.wait_ge(bank_read, g * GROUP + (n0 + r + 1))
                        for k in range(KT):
                            mm = nc.tensor.matmul(ps[:, r % 2, 0:NT], W[:, slot, P * k:P * (k + 1)], rhs[:, k, :],
                                                  start=(k == 0), stop=(k == KT - 1))
                        mm.then_inc(slab_done, 1)

            def mixer_out(o, src, rep):
                for t in range(TILES):
                    if t == 2:
                        pe.wait_ge(mix_rep, o + 1)
                    for g in range(GROUP):
                        n = 12 * o + 4 * t + g
                        if n >= 2:
                            pe.wait_ge(mix_x, n - 1)
                        for e in range(4):
                            k = 4 * g + e
                            part = src[:, k, t * P:(t + 1) * P] if t < 2 else rep[:, P * k:P * (k + 1)]
                            mm = nc.tensor.transpose(ps[:, 4 + n % 2, P * e:P * (e + 1)], part, ident[:])
                        mm.then_inc(mix_tp, 1)

            def queries(slab, n0, layer):
                def scores(h, par):
                    pe.wait_ge(bank_read, h * 2 + (n0 + 4))
                    pe.wait_ge(key_used, h + (8 * layer + 1))
                    for e in range(2):
                        key = KEYS[:, bass.ds(h * 256 + P * e, P)]
                        for t in range(PAIR):
                            nc.tensor.matmul(ps[:, 4 + par, 256 * t + P * e:256 * t + P * (e + 1)],
                                             QT[:, par, e, t * P:(t + 1) * P], key, start=True, stop=True)
                        mm = nc.tensor.matmul(ps[:, 6, 256 * par + P * e:256 * par + P * (e + 1)], REPQ[:, par, e, :], key,
                                              start=False, stop=True, skip_group_check=True)
                    mm.then_inc(key_mm, 1)

                def slab_product(g, r):
                    slot = (slab + r) % WRING
                    pe.wait_ge(slab_in[slot], g * 16 + 16 * ((slab + r) // WRING + 1))
                    pe.wait_ge(bank_read, g * GROUP + (n0 + r + 1))
                    for k in range(KT):
                        mm = nc.tensor.matmul(ps[:, r % 2, 0:NT], W[:, slot, P * k:P * (k + 1)], HT[:, k, :],
                                              start=(k == 0), stop=(k == KT - 1))
                    mm.then_inc(slab_done, 1)

                pe.wait_ge(keys_in, 16 * (layer + 1))
                nc.tensor.matmul(ps[:, 6, :], zeros[:], KEYS[:, 0:BANK], start=True, stop=False, skip_group_check=True)
                for r in range(GROUP):
                    slab_product(0, r)
                    if r == 2:
                        scores(0, 0)
                with pe.Fori(1, 4) as g:
                    slab_product(g, 0)
                    scores(g * 2 - 1, 1)
                    slab_product(g, 1)
                    slab_product(g, 2)
                    scores(g * 2, 0)
                    slab_product(g, 3)
                scores(HEADS - 1, 1)

            def sample_sum(layer):
                pe.wait_ge(peer_acc, layer + 1)
                for c in range(4):
                    nc.tensor.matmul(ps[:, 4 + c, :], repsum[:], ACC[:, BANK * c:BANK * (c + 1)],
                                     start=True, stop=True).then_inc(peer_sum, 1)

            pe.wait_ge(consts, 2)
            norm_transposes(0)

            def s5_in_part(i, h):
                k = 2 * i + h
                pe.wait_ge(s5_bx, k + 1)
                pe.wait_ge(s5_btc, k)
                for c in range(2):
                    mm = nc.tensor.transpose(ps[:, 4, P * c:P * (c + 1)], BX[:, c, :], ident[:])
                mm.then_inc(s5_bt, 1)
                pe.wait_ge(s5_btc, k + 1)
                pe.wait_ge(s5_ux, k + 1)
                pe.wait_ge(s5_bur, k)
                pe.wait_ge(s5_bsc, k)
                for c in range(2):
                    for e in range(2):
                        nc.tensor.matmul(ps[:, 2 * c + e, :], BT[:, c, :], UX[:, 2 * e:2 * e + 2, 0:SEQ],
                                         start=True, stop=True)
                    mm = nc.tensor.matmul(ps[:, 6, P * c:P * (c + 1)], BT[:, c, :], UX[:, :, SEQ:NT],
                                          start=True, stop=True)
                mm.then_inc(s5_bu, 1)

            def s5_out_part(k, h):
                pe.wait_ge(s5_dd, k + 1)
                pe.wait_ge(s5_cn, k + 1)
                pe.wait_ge(s5_p, k + 1)
                pe.wait_ge(s5_bsd, k + 1)
                pe.wait_ge(s5_yg, k)
                nc.tensor.matmul(ps[:, 5, 0:SEQ], DD[:, h, :], HT[:, bass.ds(k, 1), 0:SEQ].rearrange("p a n -> p (a n)"),
                                 start=True, stop=False, skip_group_check=True)
                nc.tensor.matmul(ps[:, 7, 0:NS], DD[:, h, :], HT[:, bass.ds(k, 1), SEQ:NT].rearrange("p a n -> p (a n)"),
                                 start=True, stop=False, skip_group_check=True)
                for q in range(QK):
                    rows = slice(QC * q, QC * (q + 1))
                    cr, ci = BC[:, h, 2, rows], CN[:, h, rows]
                    for n, c in enumerate((cr, cr, ci, ci)):
                        nc.tensor.matmul(ps[rows, 5, 0:SEQ], c, PR[n][:, q, :], start=False, stop=(n == 3), skip_group_check=True)
                    for n, c in enumerate((cr, ci)):
                        mm = nc.tensor.matmul(ps[rows, 7, 0:NS], c, BSF[:, h, n, NS * q:NS * (q + 1)], start=False,
                                              stop=(n == 1), skip_group_check=True)
                mm.then_inc(s5_y, 1)

            s5_in_part(0, 0)
            s5_in_part(0, 1)
            s5_out_part(0, 0)
            with pe.Fori(1, KT // 2) as i:
                for h in range(2):
                    s5_in_part(i, h)
                    s5_out_part(2 * i + (h - 1), 1 - h)
            s5_out_part(KT - 1, 1)

            pe.wait_ge(s5_yg, KT)
            product(SLAB_GLU, 0, 4, YT)
            pe.wait_ge(glu_out, GROUP + 16)
            mixer_out(0, OT0, REP0)
            norm_transposes(1)
            pe.wait_ge(norm_ht, 24)
            queries(SLAB_Q0, 16, 0)
            sample_sum(0)

            norm_transposes(2)
            pe.wait_ge(norm_ht, 36)
            product(SLAB_XB, 32, 4, HT)
            pe.wait_ge(lru_xc, 1)
            pe.wait_ge(bank_read, 48 + 2)
            for s in range(4):
                slot = (SLAB_GATE + s) % WRING
                pe.wait_ge(slab_in[slot], 16 * ((SLAB_GATE + s) // WRING + 1))
                for b in range(8):
                    n = 8 * s + b
                    head = 2 * s + b // 4
                    if n >= 2:
                        pe.wait_ge(gate_ev, n - 1)
                    for e in range(2):
                        at = P * (2 * b + e)
                        mm = nc.tensor.matmul(ps[:, n % 2, 0:NT], W[:, slot, at:at + P], XC[:, 2 * head + e, :],
                                              start=(e == 0), stop=(e == 1))
                    mm.then_inc(gate_mm, 1)
                pe.drain().then_inc(slab_done, 1)
            pe.wait_ge(gate_ev, 32)
            product(SLAB_IN, 48, 4, HT)
            pe.wait_ge(lru_y, 1)
            product(SLAB_OUT, 64, 4, GT)
            pe.wait_ge(bank_read, 80 + 2)
            mixer_out(1, OT1, REP1)
            norm_transposes(3)
            pe.wait_ge(norm_ht, 48)
            queries(SLAB_Q1, 80, 1)
            sample_sum(1)

        @block.scalar
        def _(act):
            act.dma_start(vecs, s5_vec).then_inc(s5_in, 16)
            act.dma_start(CH[:].rearrange("p v k -> p (v k)"), chan).then_inc(small_in, 16)
            act.sem_inc(bank_read, 2)
            A = nc.scalar.activation
            ast = Steps()

            def norm_tile(j, t):
                layer = j // 2 - 1
                if j == 0:
                    act.wait_ge(x_in[t], 16)
                elif j % 2:
                    act.wait_ge(mix_x, 12 * (j // 2) + 4 * (t + 1))
                elif t < 2:
                    act.wait_ge(row_used, RING * ((2 * layer + 1) * ROUNDS + ROUND_AT[t + 1]) + RING)
                else:
                    act.wait_ge(peer_x, layer + 1)
                A(HN[:, t, :], X[:, t, :], ACT.Square, accum_out=nrm[:, t:t + 1]).then_inc(norm_sq, 1)
                act.wait_ge(norm_v, 6 * j + 2 * t + 1)
                A(nrm[:, 6 + t:7 + t], nrm[:, 3 + t:4 + t], ACT.Sqrt).then_inc(norm_rt, 1)

            def norm_rows(j, t):
                w = P if t < 2 else NS
                for g in range(GROUP):
                    n = 12 * j + 4 * t + g
                    act.wait_ge(norm_tp, n + 1)
                    A(HT[:, 4 * g:4 * g + 4, token_cols(t)],
                      ps[:, 2 + n % 2, 0:4 * w].rearrange("p (k n) -> p k n", k=4), ACT.Copy).then_inc(norm_ht, 1)

            def norm(j):
                norm_tile(j, 0)
                norm_tile(j, 1)
                norm_rows(j, 0)
                if j % 2:
                    norm_tile(j, 2)
                    norm_rows(j, 1)
                else:
                    norm_rows(j, 1)
                    norm_tile(j, 2)
                norm_rows(j, 2)

            def replicate(rep, src):
                return A(rep.rearrange("p (k r n) -> p k r n", k=KT, r=COPIES),
                         src[:, :, SEQ:NT].unsqueeze(2).to_broadcast([P, KT, COPIES, NS]), ACT.Copy)

            def out_rows(o, src, rep):
                replicate(rep, src).then_inc(mix_rep, 1)

            lr, li, dt = vecs[:, 0:64], vecs[:, 64:128], vecs[:, 128:192]
            dte, tnh, s1, c1, sh, tmp = (par[n][:, 0:64] for n in (4, 5, 6, 7, 8, 9))
            phi, half = par[10], par[11][:, 0:64]
            lrdt = par[12][:, 0:64]
            act.wait_ge(s5_in, 16)
            A(dte, dt, ACT.Exp).then_inc(s5_pa, 1)
            act.wait_ge(s5_pv, 1)
            A(tnh, lrdt, ACT.Tanh, scale=0.5).then_inc(s5_pa, 1)
            act.wait_ge(consts, 2)
            act.wait_ge(s5_pv, 2)
            A(s1, phi[:, 0:64], ACT.Sin, scale=TWO_PI_LOW).then_inc(s5_pa, 1)
            A(sh, phi[:, 0:64], ACT.Sin, scale=TWO_PI_LOW / 2).then_inc(s5_pa, 1)
            A(tmp, phi[:, 0:64], ACT.Abs).then_inc(s5_pa, 1)
            act.wait_ge(s5_pa, 5)
            A(c1, tmp, ACT.Sin, scale=-TWO_PI_LOW, bias=cst[:, 0:1]).then_inc(s5_pa, 1)

            def turns(k1, plus=PRY):
                for q in range(QK):
                    A(PRD[:, q, :], iota[:], ACT.Copy, scale=phi[:, bass.ds(k1 * QK + q, 1)])
                    ins = A(plus[:, q, :], iota[:], ACT.Identity, scale=phi[:, bass.ds(k1 * QK + q, 1)], bias=cst[:, 1:2])
                ins.then_inc(s5_prod, 1)

            def tables(k1, slot):
                act.wait_ge(s5_f, k1 + 1)
                A(SIN[:, slot], PRD, ACT.Sin, scale=-TWO_PI_LOW).then_inc(astep, 1)
                act.wait_ge(astep, ast.next())
                A(PRD, PRD, ACT.Abs).then_inc(astep, 1)
                act.wait_ge(astep, ast.next())
                A(COS[:, slot], PRD, ACT.Sin, scale=-TWO_PI_LOW, bias=cst[:, 0:1]).then_inc(s5_tab, 1)

            def gelu_y(k):
                act.wait_ge(s5_y, k + 1)
                A(YT[:, bass.ds(k, 1), 0:SEQ].rearrange("p a n -> p (a n)"), ps[:, 5, 0:SEQ], ACT.Gelu)
                A(YT[:, bass.ds(k, 1), SEQ:NT].rearrange("p a n -> p (a n)"), ps[:, 7, 0:NS], ACT.Gelu).then_inc(s5_yg, 1)

            def spread_u(k):
                for q in range(QK):
                    rows = slice(QC * q, QC * (q + 1))
                    ins = A(UX[rows, q, :], HT[rows, bass.ds(k, 1), :].rearrange("p a n -> p (a n)"), ACT.Copy)
                ins.then_inc(s5_ux, 1)

            def negative_c(i, h):
                act.wait_ge(s5_c_in[h], (i + 1) * 16)
                A(CN[:, h, :], BC[:, h, 3, :], ACT.Copy, scale=-1.0).then_inc(s5_cn, 1)

            def matrices(k):
                act.wait_ge(s5_bt, k + 1)
                A(BT[:].rearrange("p c n -> p (c n)"), ps[:, 4, 0:2 * P], ACT.Copy).then_inc(s5_btc, 1)

            def s5_tile(i, h, first=False, last=False, reuse=True):
                k = 2 * i + h
                if not last:
                    if not first:
                        act.wait_ge(s5_p, k)
                    tables(k + 1, 1 - h)
                act.wait_ge(s5_bu, k + 1)
                if reuse:
                    act.wait_ge(s5_y, k - 1)
                A(BSF[:, h, :, :], ps[:, 6, 0:2 * P].rearrange("p (c n) -> p c n", c=2), ACT.Copy).then_inc(s5_bsc, 1)
                if not last:
                    spread_u(k + 1)
                    matrices(k + 1)
                    act.wait_ge(s5_tab, k + 2)
                    turns(k + 2)
                if not first:
                    gelu_y(k - 1)
                if not last:
                    negative_c(*((i, 1) if h == 0 else (i + 1, 0)))

            act.wait_ge(s5_pv, 3)
            turns(0, M[3])
            norm_tile(0, 0)
            tables(0, 0)
            norm_tile(0, 1)
            norm_rows(0, 0)
            norm_tile(0, 2)
            norm_rows(0, 1)
            norm_rows(0, 2)
            act.wait_ge(norm_ht, 12)
            spread_u(0)
            negative_c(0, 0)
            matrices(0)
            act.wait_ge(s5_tab, 1)
            turns(1)
            s5_tile(0, 0, first=True, reuse=False)
            s5_tile(0, 1, reuse=False)
            with act.Fori(1, KT // 2 - 1) as i:
                ast.enter(i - 1, 4)
                s5_tile(i, 0)
                s5_tile(i, 1)
            ast.leave(KT // 2 - 2)
            s5_tile(KT // 2 - 1, 0)
            s5_tile(KT // 2 - 1, 1, last=True)
            gelu_y(KT - 1)

            with act.Fori(0, 4) as g:
                for r in range(GROUP):
                    act.wait_ge(slab_done, g * GROUP + (SLAB_GLU + r + 1))
                    act.wait_ge(glu_out, g * GROUP + (r + 1))
                    A(SIG[:, r, :], ps[:, r % 2, 0:NT], ACT.Sigmoid,
                      bias=CH[:, V_BGLU, bass.ds(g * GROUP + r, 1)]).then_inc(bank_read, 1)
            act.wait_ge(glu_out, GROUP + 16)
            out_rows(0, OT0, REP0)
            norm(1)

            def evacuate(slab, groups, dst):
                with act.Fori(0, groups) as g:
                    for r in range(GROUP):
                        act.wait_ge(slab_done, g * GROUP + (slab + r + 1))
                        A(dst[:, bass.ds(g * GROUP + r, 1), :].rearrange("p a n -> p (a n)"), ps[:, r % 2, 0:NT],
                          ACT.Copy).then_inc(bank_read, 1)

            def peer(layer):
                act.wait_ge(s5_zero, layer + 1)
                slab = (SLAB_Q0, SLAB_Q1)[layer]

                def head_queries(g, par, clear=True):
                    for e in range(2):
                        r = 2 * par + e
                        act.wait_ge(slab_done, g * GROUP + (slab + r + 1))
                        A(QT[:, par, e, :], ps[:, e, 0:NT], ACT.Copy)
                        copy = REPQ[:, par, e, bass.ds(g * NS, NS)]
                        if clear:
                            A(REPQ[:, par, e, bass.ds(g * NS - NS, NS)], zeros[:, 0:NS], ACT.Copy)
                        A(copy, ps[:, e, SEQ:NT], ACT.Copy).then_inc(bank_read, 1)

                def marks(h):
                    act.wait_ge(pos_off, h + (HEADS * layer + 1))
                    A(OH, OH, ACT.Abs).then_inc(astep, 1)
                    act.wait_ge(astep, ast.next())
                    A(OH, OH, ACT.Relu, scale=-1.0, bias=1.0).then_inc(one_hot, 1)

                A(REPQ, zeros[:].unsqueeze(1).unsqueeze(1).to_broadcast([P, 2, 2, P]), ACT.Copy).then_inc(astep, 1)
                act.wait_ge(astep, ast.next())
                for par in range(2):
                    head_queries(0, par, clear=False)
                for par in range(2):
                    head_queries(1, par)
                marks(0)
                with act.Fori(2, HEADS // 2) as g:
                    ast.enter(g - 2, 2)
                    for par in range(2):
                        head_queries(g, par)
                        marks(g * 2 + (par - 3))
                ast.leave(HEADS // 2 - 2)
                for h in range(HEADS - 3, HEADS):
                    marks(h)
                act.wait_ge(soft_in, layer + 1)
                A(GE, GE, ACT.Exp).then_inc(soft_exp, 1)
                act.wait_ge(dots_done, layer + 1)
                A(WG[:, 0:COLS], AV[:, 0:COLS], ACT.Gelu).then_inc(act_g, 1)

            peer(0)
            norm(2)
            lam = CH[:, V_LAM, :]
            A(LS[0], lam, ACT.Abs).then_inc(lru_sp, 1)
            act.wait_ge(lru_sp, 1)
            A(LS[1], LS[0], ACT.Exp, scale=-1.0).then_inc(lru_sp, 1)
            act.wait_ge(lru_sp, 3)
            A(LS[3], LS[2], ACT.Ln).then_inc(lru_sp, 1)
            act.wait_ge(lru_pad, 2)
            with act.Fori(0, 4) as g:
                for r in range(GROUP):
                    act.wait_ge(slab_done, g * GROUP + (SLAB_XB + r + 1))
                    A(XBP[:, bass.ds(g * GROUP + r, 1), 3:].rearrange("p a n -> p (a n)"), ps[:, r % 2, 0:SEQ], ACT.Copy)
                    A(XBS[:, bass.ds(g * GROUP + r, 1), :, 3:].rearrange("p a b n -> p (a b) n"),
                      ps[:, r % 2, SEQ:NT].rearrange("p (b n) -> p b n", b=SB), ACT.Copy).then_inc(bank_read, 1)
            for s in range(4):
                for b in range(8):
                    n = 8 * s + b
                    head, gate, jt = 2 * s + b // 4, b // 2 % 2, b % 2
                    ch = 2 * head + jt
                    act.wait_ge(gate_mm, n + 1)
                    A((RA, IG)[gate][:, ch, :], ps[:, n % 2, 0:NT], ACT.Sigmoid,
                      bias=CH[:, (V_BA, V_BI)[gate], ch:ch + 1]).then_inc(gate_ev, 1)
            act.wait_ge(lru_sp, 5)
            act.wait_ge(gate_ev, 32)
            act.wait_ge(lru_st, 1)
            for k in range(KT):
                ins = A(TH[:, k, :], RA[:, k, :], ACT.Tanh, scale=LS[5][:, k:k + 1])
            ins.then_inc(lru_th, 1)

            def gate_columns(first):
                with act.Fori(first, first + 2) as g:
                    for r in range(GROUP):
                        act.wait_ge(slab_done, g * GROUP + (SLAB_IN + r + 1))
                        A(GT[:, bass.ds(g * GROUP + r, 1), :].rearrange("p a n -> p (a n)"), ps[:, r % 2, 0:NT],
                          ACT.Gelu).then_inc(bank_read, 1)

            for k in range(KT):
                ins = A(RA[:, k, :], RA[:, k, :], ACT.Exp, scale=LS[6][:, k:k + 1])
            ins.then_inc(lru_a, 1)
            gate_columns(0)
            act.wait_ge(lru_v, 1)
            A(TH, TH, ACT.Sqrt).then_inc(lru_rt, 1)
            gate_columns(2)
            evacuate(SLAB_OUT, 4, OT1)
            act.wait_ge(bank_read, 82)
            out_rows(1, OT1, REP1)
            norm(3)
            peer(1)
            for t in range(TILES):
                norm_tile(4, t)

        @block.vector
        def _(dve):
            V = nc.vector
            st = Steps()
            dve.sem_inc(row_used, RING)
            dve.sem_inc(key_used, 2)
            dve.sem_inc(pick_read, 1)
            dve.sem_inc(glu_out, GROUP)

            def settle(ins):
                ins.then_inc(vstep, 1)
                dve.wait_ge(vstep, st.next())

            def settle_all(ins):
                settle(ins)
                dve.sem_inc(top_go, 1)

            def norm_tile(j, t):
                dve.wait_ge(norm_sq, 3 * j + t + 1)
                V.tensor_scalar(nrm[:, 3 + t:4 + t], nrm[:, t:t + 1], 1.0 / D, EPS, ALU.mult, ALU.add).then_inc(norm_v, 1)
                dve.wait_ge(norm_rt, 3 * j + t + 1)
                V.reciprocal(nrm[:, 9 + t:10 + t], nrm[:, 6 + t:7 + t]).then_inc(norm_v, 1)
                dve.wait_ge(norm_v, 6 * j + 2 * t + 2)
                if t == 0:
                    dve.wait_ge(gain_in, (32, 32, 64, 64, 80)[j])
                V.scalar_tensor_tensor(HN[:, t, :], X[:, t, :], nrm[:, 9 + t:10 + t], GB[:, j % 2, :],
                                       ALU.mult, ALU.mult).then_inc(norm_h, 1)

            def add_mixer(o, t):
                for g in range(GROUP):
                    n = 12 * o + 4 * t + g
                    dve.wait_ge(mix_tp, n + 1)
                    cols = slice(BANK * g, BANK * (g + 1))
                    V.tensor_tensor(X[:, t, cols], ps[:, 4 + n % 2, :], X[:, t, cols], ALU.add).then_inc(mix_x, 1)

            def add_and_norm(o):
                add_mixer(o, 0)
                add_mixer(o, 1)
                dve.wait_ge(mix_x, 12 * o + 8)
                norm_tile(2 * o + 1, 0)
                add_mixer(o, 2)
                norm_tile(2 * o + 1, 1)
                dve.wait_ge(mix_x, 12 * o + 12)
                norm_tile(2 * o + 1, 2)

            lr, li = vecs[:, 0:64], vecs[:, 64:128]
            abr, abi, fr, fi = (par[n][:, 0:64] for n in range(4))
            dte, tnh, s1, c1, sh = (par[n][:, 0:64] for n in (4, 5, 6, 7, 8))
            phi, lrdt = par[10], par[12][:, 0:64]
            e1, den, nr, t1, t2, dec, trn, t3 = (par[n][:, 0:64] for n in range(13, 21))
            V.memset(UX, 0.0)
            V.memset(phi, 0.0).then_inc(vstep, 1)
            st.next()
            dve.wait_ge(s5_pa, 1)
            V.tensor_tensor(lrdt, lr, dte, ALU.mult).then_inc(s5_pv, 1)
            settle(V.tensor_tensor(trn, li, dte, ALU.mult))
            settle(V.tensor_scalar(trn, trn, 1.0 / (2 * PI), None, ALU.mult))
            settle(V.tensor_scalar(t1, trn, ROUND, ROUND, ALU.add, ALU.subtract))
            V.tensor_tensor(phi[:, 0:64], trn, t1, ALU.subtract).then_inc(s5_pv, 1)
            V.tensor_tensor(t3, lr, lr, ALU.mult)
            settle(V.tensor_tensor(t2, li, li, ALU.mult))
            settle(V.tensor_tensor(den, t3, t2, ALU.add))
            V.reciprocal(den, den)
            dve.wait_ge(s5_pa, 2)
            settle(V.tensor_scalar(t1, tnh, -1.0, 1.0, ALU.mult, ALU.add))
            settle(V.reciprocal(t1, t1))
            settle(V.scalar_tensor_tensor(e1, tnh, 2.0, t1, ALU.mult, ALU.mult))
            settle(V.tensor_scalar(dec, e1, 1.0, None, ALU.add))
            dve.wait_ge(s5_pa, 6)
            V.tensor_tensor(abr, dec, c1, ALU.mult)
            V.tensor_tensor(abi, dec, s1, ALU.mult)
            V.scalar_tensor_tensor(t1, sh, -2.0, sh, ALU.mult, ALU.mult)
            settle(V.tensor_tensor(nr, e1, c1, ALU.mult))
            settle(V.tensor_tensor(nr, nr, t1, ALU.add))
            V.tensor_tensor(fr, nr, lr, ALU.mult)
            V.tensor_tensor(t1, abi, li, ALU.mult)
            V.tensor_tensor(fi, abi, lr, ALU.mult)
            settle(V.tensor_tensor(t2, nr, li, ALU.mult))
            V.tensor_tensor(fr, fr, t1, ALU.add)
            settle(V.tensor_tensor(fi, fi, t2, ALU.subtract))
            V.tensor_tensor(fr, fr, den, ALU.mult)
            V.tensor_tensor(fi, fi, den, ALU.mult).then_inc(s5_pv, 1)

            def fractions(k1, plus=PRY):
                dve.wait_ge(s5_prod, k1 + 1)
                V.scalar_tensor_tensor(PRD, plus, ROUND, PRD, ALU.subtract, ALU.subtract).then_inc(s5_f, 1)

            def s5_tile(i, h, first=False, last=False):
                k = 2 * i + h
                if not last:
                    fractions(k + 1)
                if not first:
                    final_states(k - 1)
                dve.wait_ge(s5_bu, k + 1)
                dve.wait_ge(s5_tab, k + 1)
                re = ps[:, 0:2, :].rearrange("p b (q t) -> p (b q) t", q=2)
                im = ps[:, 2:4, :].rearrange("p b (q t) -> p (b q) t", q=2)
                cos, sin = COS[:, h], SIN[:, h]
                V.tensor_tensor(M[0], re, cos, ALU.mult)
                V.tensor_tensor(M[1], im, sin, ALU.mult)
                V.tensor_tensor(M[2], im, cos, ALU.mult)
                V.tensor_tensor(M[3], re, sin, ALU.mult).then_inc(s5_bur, 1)
                dve.wait_ge(s5_bur, k + 1)
                settle(V.tensor_tensor(M[0], M[0], M[1], ALU.add))
                for src, dst in ((M[0], M[1]), (M[2], M[3])):
                    if src is M[2]:
                        dve.wait_ge(s5_wi, k + 1)
                    for q in range(QK):
                        ins = V.tensor_tensor_scan(dst[:, q, :], dec[:, bass.ds(k * QK + q, 1)].to_broadcast([P, SEQ]),
                                                   src[:, q, :], 0.0, ALU.mult, ALU.add)
                settle(ins)
                if not first:
                    dve.wait_ge(s5_y, k)
                V.tensor_tensor(PR[0], cos, M[1], ALU.mult)
                V.scalar_tensor_tensor(PR[1], sin, -1.0, M[3], ALU.mult, ALU.mult)
                V.tensor_tensor(PR[2], sin, M[1], ALU.mult)
                V.tensor_tensor(PR[3], cos, M[3], ALU.mult).then_inc(s5_p, 1)

            def final_states(k):
                dve.wait_ge(s5_p, k + 1)
                end = [w[:, :, SEQ - 1:SEQ].rearrange("p q a -> p (q a)") for w in PR]
                V.tensor_tensor(SF[:, 0, bass.ds(k * QK, QK)], end[0], end[1], ALU.add)
                V.tensor_tensor(SF[:, 1, bass.ds(k * QK, QK)], end[2], end[3], ALU.add)

            fractions(0, M[3])
            for t in range(TILES):
                norm_tile(0, t)
            dve.wait_ge(norm_tp, 12)
            s5_tile(0, 0, first=True)
            s5_tile(0, 1)
            with dve.Fori(1, KT // 2 - 1) as i:
                st.enter(i - 1, 4)
                s5_tile(i, 0)
                s5_tile(i, 1)
            st.leave(KT // 2 - 2)
            s5_tile(KT // 2 - 1, 0)
            s5_tile(KT // 2 - 1, 1, last=True)
            final_states(KT - 1)
            dve.drain().then_inc(s5_sf, 1)

            dve.wait_ge(s5_y, KT)
            with dve.Fori(0, 4) as g:
                for r in range(GROUP):
                    dve.wait_ge(bank_read, g * GROUP + (r + 3))
                    n = g * GROUP + r
                    V.tensor_tensor(OT0[:, bass.ds(n, 1), :].rearrange("p a n -> p (a n)"), SIG[:, r, :],
                                    YT[:, bass.ds(n, 1), :].rearrange("p a n -> p (a n)"), ALU.mult).then_inc(glu_out, 1)
            add_and_norm(0)

            def top16(lists):
                lists = list(lists)
                for values, best, places, left in lists:
                    ins = V.max(best[:, 0:8], values)
                settle_all(ins)
                for values, best, places, left in lists:
                    V.max_index(places[:, 0:8], best[:, 0:8], values)
                    ins = V.match_replace(left, best[:, 0:8], values, LOWEST)
                settle_all(ins)
                for values, best, places, left in lists:
                    ins = V.max(best[:, 8:16], left)
                settle_all(ins)
                for values, best, places, left in lists:
                    ins = V.max_index(places[:, 8:16], best[:, 8:16], left)
                settle_all(ins)

            tv4 = TV.rearrange("p (t s k) -> p t s k", t=PAIR, s=2)
            ge4 = GE[:, 0:PAIR * PICKS].rearrange("p (t h k) -> p t h k", t=PAIR, h=HEADS)
            gi4 = GI[:, 0:PAIR * PICKS].rearrange("p (t h k) -> p t h k", t=PAIR, h=HEADS)

            def as_cube(ap):
                return ap.rearrange("p (t a b) -> p t a b", t=PAIR, a=TOPK)

            def key_lists(bank):
                for j in range(2 * PAIR):
                    at, out = P * j, slice(TOPK * j, TOPK * (j + 1))
                    yield ps[:, bank, at:at + P], TV[:, out], TI[:, out], LEFT[:, at:at + P]

            def candidate_lists():
                for t in range(PAIR):
                    out, at = slice(TOPK * t, TOPK * (t + 1)), slice(CANDS * t, CANDS * (t + 1))
                    yield C[:, at], BV[:, out], BP[:, out], LEFT_C[:, at]

            def candidates(par):
                V.tensor_copy(TF[par], TI)
                return V.tensor_tensor(as_cube(C), tv4[:, :, 0, :].unsqueeze(3).to_broadcast(cube),
                                       tv4[:, :, 1, :].unsqueeze(2).to_broadcast(cube), ALU.add)

            def positions(ge):
                bv = BV.rearrange("p (t k) -> p t k", t=PAIR)
                V.tensor_scalar(AB[:, 0:PAIR * TOPK], BP, 4, None, ALU.logical_shift_right)
                V.tensor_scalar(AB[:, PAIR * TOPK:], BP, 15, None, ALU.bitwise_and)
                return V.tensor_tensor(ge, bv, bv[:, :, 0:1].to_broadcast([P, PAIR, TOPK]), ALU.subtract)

            def sum_parts():
                return V.tensor_reduce(II, OH.rearrange("p (a b) -> p a b", b=TOPK), AX_X, ALU.add)

            def expert_numbers(to):
                ii = II.rearrange("p (s t k) -> p s t k", s=2, t=PAIR)
                return V.scalar_tensor_tensor(to, ii[:, 0], float(NKEYS), ii[:, 1], ALU.mult, ALU.add)

            def of_head(ap, h):
                return ap[:, :, bass.ds(h, 1), :].rearrange("p t a k -> p t (a k)")

            def choose(layer, h, par, keyed=True, cands=True, experts=True):
                if keyed:
                    dve.wait_ge(key_mm, h + (HEADS * layer + 1))
                if keyed or cands:
                    dve.sem_inc(top_go, 1)
                    top16([*(key_lists(4 + par) if keyed else ()), *(candidate_lists() if cands else ())])
                if experts:
                    dve.wait_ge(picked, h - 2 + (HEADS * layer + 1))
                    ins = sum_parts()
                if cands:
                    ins = positions(of_head(ge4, h - 1))
                if keyed:
                    dve.sem_inc(key_used, 1)
                    ins = candidates(par)
                settle(ins)
                if experts:
                    dve.sem_inc(pick_read, 1)
                    expert_numbers(of_head(gi4, h - 2)).then_inc(experts_set, 1)
                if cands:
                    V.tensor_copy(ABF[1 - par], AB).then_inc(pos_set, 1)

            def choose_sample(layer):
                tile = slice(2 * PICKS, COLS)
                top16(key_lists(6))
                settle_all(candidates(0))
                top16(candidate_lists())
                settle(positions(GE[:, tile].rearrange("p (t k) -> p t k", t=PAIR)))
                dve.sem_inc(soft_in, 1)
                settle(V.tensor_copy(ABF[0], AB))
                cells = [P, 2 * PAIR * TOPK, TOPK]
                settle(V.tensor_tensor(OH.rearrange("p (a b) -> p a b", b=TOPK), ABF[0].unsqueeze(2).to_broadcast(cells),
                                       iota[:, 0:TOPK].unsqueeze(1).to_broadcast(cells), ALU.is_equal))
                for s in range(2):
                    oh = as_cube(OH[:, PAIR * CANDS * s:PAIR * CANDS * (s + 1)])
                    tf = TF[0].rearrange("p (t s k) -> p t s k", t=PAIR, s=2)[:, :, s, :]
                    ins = V.tensor_tensor(oh, oh, tf.unsqueeze(2).to_broadcast(cube), ALU.mult)
                settle(ins)
                settle(sum_parts())
                expert_numbers(GI[:, tile].rearrange("p (t k) -> p t k", t=PAIR)).then_inc(sample_picks, 1)

            def dot_rows(layer, t, i, rows):
                first = 2 * layer * ROUNDS + ROUND_AT[t]
                for r in rows:
                    dve.wait_ge(row_in[r], i * 16 + 16 * (first + 1))
                    V.tensor_tensor_reduce(ring[:, r, :], ring[:, r, :], HN[:, t, :], 1.0, 0.0, ALU.mult, ALU.add,
                                           A8[:, r:r + 1]).then_inc(row_used, 1)

            def keep_dots(layer, t, i):
                dve.wait_ge(row_used, i * RING + (RING * (2 * layer * ROUNDS + ROUND_AT[t] + 1) + RING))
                settle(V.tensor_copy(AV[:, bass.ds(i * RING + ROUND_AT[t] * RING, RING)], A8))

            def dots(layer, t, start, end):
                with dve.Fori(start, end) as i:
                    st.enter(i - start, 1)
                    dot_rows(layer, t, i, range(RING))
                    keep_dots(layer, t, i)
                st.leave(end - start)

            def peer(layer):
                dve.wait_ge(bank_read, (16, 80)[layer] + 3)
                choose(layer, 0, 0, cands=False, experts=False)
                choose(layer, 1, 1, experts=False)
                with dve.Fori(1, HEADS // 2 - 1) as i:
                    st.enter(i - 1, 2 * 5)
                    choose(layer, i * 2, 0)
                    choose(layer, i * 2 + 1, 1)
                st.leave(HEADS // 2 - 2)
                dot_rows(layer, 0, 0, range(EARLY // 2))
                choose(layer, HEADS - 2, 0)
                dot_rows(layer, 0, 0, range(EARLY // 2, EARLY))
                choose(layer, HEADS - 1, 1)
                dot_rows(layer, 0, 0, range(EARLY, RING))
                keep_dots(layer, 0, 0)
                dots(layer, 0, 1, LAST_HEAD_AT)
                choose(layer, HEADS, 0, keyed=False)
                dots(layer, 0, LAST_HEAD_AT, LAST_HEAD_AT + 2)
                choose(layer, HEADS + 1, 1, keyed=False, cands=False)
                dve.wait_ge(experts_set, HEADS * (layer + 1))
                dve.sem_inc(picks_ready, 1)
                dots(layer, 0, LAST_HEAD_AT + 2, LAST_HEAD_AT + 6)
                choose_sample(layer)
                dots(layer, 0, LAST_HEAD_AT + 6, ROUNDS_OF[0])
                dve.wait_ge(soft_exp, layer + 1)
                ge = GE.rearrange("p (g k) -> p g k", k=TOPK)
                groups = COLS // TOPK
                settle(V.tensor_reduce(GS[:, 0:groups], ge, AX_X, ALU.add))
                settle(V.reciprocal(GS[:, groups:], GS[:, 0:groups]))
                settle(V.tensor_tensor(GG[:, 0:COLS].rearrange("p (g k) -> p g k", k=TOPK), ge,
                                       GS[:, groups:].unsqueeze(2).to_broadcast([P, groups, TOPK]), ALU.mult))
                settle(V.memset(ACC, 0.0))
                for t in range(1, TILES):
                    dots(layer, t, 0, ROUNDS_OF[t])
                dve.sem_inc(dots_done, 1)
                dve.wait_ge(act_g, layer + 1)
                settle(V.tensor_tensor(WG[:, 0:COLS], WG[:, 0:COLS], GG[:, 0:COLS], ALU.mult))
                base = (2 * layer + 1) * ROUNDS
                for t in range(TILES):
                    to = X[:, t, :] if t < 2 else ACC
                    with dve.Fori(0, ROUNDS_OF[t]) as i:
                        first = base + ROUND_AT[t]
                        for r in range(RING):
                            dve.wait_ge(row_in[r], i * 16 + 16 * (first + 1))
                            dve.wait_ge(row_used, i * RING + (RING * first + RING + r))
                            V.scalar_tensor_tensor(to, ring[:, r, :], WG[:, bass.ds(i * RING + (ROUND_AT[t] * RING + r), 1)],
                                                   to, ALU.mult, ALU.add).then_inc(row_used, 1)
                    if t == 1:
                        for n in range(2):
                            norm_tile(2 * layer + 2, n)
                dve.wait_ge(row_used, RING * (base + ROUNDS) + RING)
                dve.sem_inc(peer_acc, 1)
                for c in range(4):
                    dve.wait_ge(peer_sum, 4 * layer + c + 1)
                    cols = slice(BANK * c, BANK * (c + 1))
                    ins = V.tensor_tensor(X[:, 2, cols], ps[:, 4 + c, :], X[:, 2, cols], ALU.add)
                ins.then_inc(peer_x, 1)
                dve.wait_ge(peer_x, layer + 1)
                norm_tile(2 * layer + 2, 2)

            peer(0)
            lam = CH[:, V_LAM, :]
            dve.wait_ge(lru_sp, 2)
            V.tensor_scalar(LS[2], LS[1], 1.0, None, ALU.add).then_inc(lru_sp, 1)
            dve.wait_ge(lru_sp, 4)
            settle(V.tensor_scalar(LS[4], LS[2], -1.0, None, ALU.add))
            settle(V.tensor_scalar(LS[7], LS[4], 0.0, None, ALU.is_equal))
            settle(V.tensor_tensor(LS[4], LS[4], LS[7], ALU.add))
            settle(V.reciprocal(LS[4], LS[4]))
            settle(V.tensor_tensor(LS[3], LS[3], LS[7], ALU.add))
            settle(V.tensor_tensor(LS[3], LS[3], LS[4], ALU.mult))
            settle(V.tensor_tensor(LS[3], LS[3], LS[1], ALU.mult))
            settle(V.tensor_scalar(LS[4], lam, -1.0, 0.0, ALU.mult, ALU.max))
            settle(V.tensor_tensor(LS[3], LS[3], LS[4], ALU.add))
            V.tensor_scalar(LS[5], LS[3], 8.0, None, ALU.mult)
            V.tensor_scalar(LS[6], LS[3], -8.0, None, ALU.mult).then_inc(lru_sp, 1)
            cw = [CH[:, V_CW + n, :] for n in range(4)]
            with dve.Fori(0, KT) as k:
                dve.wait_ge(bank_read, k + (32 + 3))
                st.enter(k, 4)
                xp = XBP[:, bass.ds(k, 1), :].rearrange("p a n -> p (a n)")
                xs = XBS[:, bass.ds(k, 1), :, :].rearrange("p a b n -> p (a b) n")
                op = XC[:, bass.ds(k, 1), 0:SEQ].rearrange("p a n -> p (a n)")
                os_ = XC[:, bass.ds(k, 1), SEQ:NT].rearrange("p a (b n) -> p (a b) n", b=SB)
                one = bass.ds(k, 1)
                V.tensor_scalar(op, xp[:, 0:SEQ], cw[0][:, one], CH[:, V_CB, one], ALU.mult, ALU.add)
                settle(V.tensor_scalar(os_, xs[:, :, 0:ST], cw[0][:, one], CH[:, V_CB, one], ALU.mult, ALU.add))
                for n in range(1, 4):
                    V.scalar_tensor_tensor(op, xp[:, n:n + SEQ], cw[n][:, one], op, ALU.mult, ALU.add)
                    settle(V.scalar_tensor_tensor(os_, xs[:, :, n:n + ST], cw[n][:, one], os_, ALU.mult, ALU.add))
            st.leave(KT)
            V.tensor_copy(LOUT[:, 16:64].rearrange("p (k n) -> p k n", k=KT), XBP[:, :, SEQ:SEQ + 3])
            V.tensor_copy(LOUT[:, 192:576].rearrange("p (k b n) -> p k b n", k=KT, b=SB), XBS[:, :, :, 4:7]).then_inc(lru_st, 1)
            dve.sem_inc(lru_xc, 1)
            dve.wait_ge(gate_ev, 32)
            V.tensor_tensor(IG, IG, XC, ALU.mult)
            dve.wait_ge(lru_th, 1)
            for half in range(2):
                th = TH[:, KT // 2 * half:KT // 2 * (half + 1), :]
                settle(V.tensor_scalar(LV, th, 1.0, None, ALU.add))
                settle(V.reciprocal(LV, LV))
                ins = V.scalar_tensor_tensor(th, th, 2.0, LV, ALU.mult, ALU.mult)
                if half == 0:
                    settle(ins)
            ins.then_inc(lru_v, 1)
            dve.wait_ge(lru_rt, 1)
            settle(V.tensor_tensor(IG, IG, TH, ALU.mult))
            dve.wait_ge(lru_a, 1)
            with dve.Fori(0, KT) as k:
                one = bass.ds(k, 1)
                V.tensor_tensor_scan(XC[:, one, 0:SEQ].rearrange("p a n -> p (a n)"),
                                     RA[:, one, 0:SEQ].rearrange("p a n -> p (a n)"),
                                     IG[:, one, 0:SEQ].rearrange("p a n -> p (a n)"), 0.0, ALU.mult, ALU.add)
            ra_s = RA[:, :, SEQ:NT].rearrange("p k (b t) -> p k b t", b=SB)
            bx_s = IG[:, :, SEQ:NT].rearrange("p k (b t) -> p k b t", b=SB)
            hs_s = XC[:, :, SEQ:NT].rearrange("p k (b t) -> p k b t", b=SB)
            prev = LH0
            for n in range(ST):
                settle(V.tensor_tensor(LT, ra_s[:, :, :, n], prev, ALU.mult))
                settle(V.tensor_tensor(hs_s[:, :, :, n], bx_s[:, :, :, n], LT, ALU.add))
                prev = hs_s[:, :, :, n]
            V.tensor_copy(LOUT[:, 0:16], XC[:, :, SEQ - 1])
            V.tensor_copy(LOUT[:, 64:192].rearrange("p (k b) -> p k b", k=KT), prev).then_inc(lru_hs, 1)
            dve.wait_ge(lru_hs, 1)
            for g in range(4):
                dve.wait_ge(bank_read, 48 + 4 * (g + 1) + 2)
                part = slice(4 * g, 4 * (g + 1))
                ins = V.tensor_tensor(GT[:, part, :], GT[:, part, :], XC[:, part, :], ALU.mult)
            ins.then_inc(lru_y, 1)
            dve.wait_ge(bank_read, 82)
            add_and_norm(1)
            peer(1)


def kernel(**inputs):
    import numpy as np
    import concourse.bacc as _bacc
    from concourse import mybir as _mybir
    from concourse.bass_utils import run_bass_kernel_spmd as _run

    a = {k: np.asarray(v) for k, v in inputs.items()}

    def column_slabs(w):
        n = w.shape[1] // P
        return w.reshape(KT, P, n, P).transpose(2, 1, 0, 3).reshape(n, P, D)

    gates = np.stack([a["lru_w_a"][0], a["lru_w_i"][0]]).reshape(2, 4, 2, 2, P, 2, P)
    keys = a["peer_sub_keys"].reshape(2, 2 * HEADS, NKEYS, P).transpose(0, 3, 1, 2).reshape(2, P, D)
    slabs = np.concatenate([
        column_slabs(a["s5_w_glu"][0]), column_slabs(a["peer_w_q"][0]),
        column_slabs(a["lru_w_in"][0][:, D:]), gates.transpose(1, 4, 2, 0, 5, 3, 6).reshape(4, P, D),
        column_slabs(a["lru_w_in"][0][:, :D]), column_slabs(a["lru_w_out"][0]),
        column_slabs(a["peer_w_q"][1])])

    def channels(v):
        return v.reshape(KT, P).T

    chan = np.concatenate([channels(v) for v in (
        a["s5_d"][0], a["s5_b_glu"][0], *a["lru_conv_w"][0], a["lru_conv_b"][0],
        a["lru_b_a"][0].reshape(-1), a["lru_b_i"][0].reshape(-1), a["lru_lam"][0])], axis=1)

    def states(v):
        return v.reshape(S5_Q, 2, 64, *v.shape[2:]).transpose(1, 2, 0, *range(3, v.ndim + 1)).reshape(P, S5_Q, *v.shape[2:])

    log_dt = np.repeat(a["s5_log_dt"][0][:, None], 64, axis=1)
    s5_vec = np.concatenate([states(a["s5_lam_re"][0]), states(a["s5_lam_im"][0]), states(log_dt)], axis=1)

    def by_group(v):
        out = np.zeros((2, 64, S5_Q, 2, 16), v.dtype)
        w = v.reshape(2, 64, S5_Q, 16)
        out[0, :, :, 0], out[1, :, :, 1] = w[0], w[1]
        return out.reshape(P, KT, P)

    bc = [by_group(states(v)) for v in (a["s5_b_re"][0], a["s5_b_im"][0], a["s5_c_re"][0].transpose(0, 2, 1),
                                        a["s5_c_im"][0].transpose(0, 2, 1))]
    s5_bc = np.stack(bc, axis=2).transpose(1, 0, 2, 3).reshape(KT, P, 4 * P)
    s5_h0 = np.concatenate([states(v[0].transpose(1, 2, 0)).reshape(P, -1) for v in (a["state_s5_re"], a["state_s5_im"])], axis=1)
    conv = a["state_lru_conv"][0].reshape(SB, 3, KT, P).transpose(3, 2, 0, 1).reshape(P, -1)
    h0 = a["state_lru_h"][0].reshape(SB, KT, P).transpose(2, 1, 0).reshape(P, -1)
    sample = a["x_sample"].reshape(NS, D)
    arrays = {
        "x": np.concatenate([a["x_prompt"].reshape(2, P, D), np.tile(sample, (COPIES, 1))[None]]),
        "norms": np.stack([a["norm_mix"][0], a["norm_ffn"][0], a["norm_mix"][1], a["norm_ffn"][1], a["norm_final"]]),
        "slabs": slabs, "keys": keys, "chan": chan, "s5_vec": s5_vec, "s5_bc": s5_bc, "s5_h0": s5_h0,
        "lru_in": np.concatenate([conv, h0], axis=1),
        "u0": a["peer_u"][0], "v0": a["peer_v"][0], "u1": a["peer_u"][1], "v1": a["peer_v"][1],
    }
    outs = {"y": (2, P, D), "ys": (NS, D), "s5p": (P, 2 * S5_Q), "s5s": (P, 2 * S5_Q * SB), "lru": (P, 576)}

    nc = _bacc.Bacc("TRN2", target_bir_lowering=False, num_devices=1)
    args, in_map = [], {}
    for name, v in arrays.items():
        v = np.ascontiguousarray(v)
        in_map[f"in_{name}_dram"] = v
        args.append(nc.dram_tensor(f"in_{name}_dram", v.shape, _mybir.dt.from_np(v.dtype), kind="ExternalInput").ap())
    for name, shape in outs.items():
        args.append(nc.dram_tensor(f"out_{name}_dram", shape, F32, kind="ExternalOutput").ap())
    hybrid_step(nc, *args)
    r = _run(nc, [in_map], core_ids=[0]).results[0]
    y, ys, s5p, s5s, lru = (np.asarray(r[f"out_{name}_dram"]) for name in outs)

    def groups(v):
        return v.reshape(2, 64, S5_Q, -1).transpose(3, 2, 0, 1).reshape(-1, 2 * S5_Q, 64)

    s5p = s5p.reshape(P, 2, S5_Q)
    s5s = s5s.reshape(P, 2, S5_Q, SB)
    hp, cp, hs, cs = lru[:, 0:16], lru[:, 16:64], lru[:, 64:192], lru[:, 192:576]
    return (y.reshape(1, SEQ, D), ys.reshape(SB, ST, D),
            groups(s5p[:, 0])[None], groups(s5p[:, 1])[None], groups(s5s[:, 0])[None], groups(s5s[:, 1])[None],
            hp.T.reshape(1, 1, D), cp.reshape(P, KT, 3).transpose(2, 1, 0).reshape(1, 1, 3, D),
            hs.reshape(P, KT, SB).transpose(2, 1, 0).reshape(1, SB, D),
            cs.reshape(P, KT, SB, 3).transpose(2, 3, 1, 0).reshape(1, SB, 3, D))
```
